# Optimizing a Trainium2 kernel written in Bass

```python
import jax, jax.numpy as jnp
from jax import lax
import numpy as np
import math
import jax
import jax.numpy as jnp

D_MODEL = 1024
BATCH = 1
SEQ = 512
DEPTH = 2

HEAD_DIM = 64
N_Q_HEADS = 8
N_KV_HEADS = 2
ATTN_WIDTH = N_Q_HEADS * HEAD_DIM
KV_WIDTH = N_KV_HEADS * HEAD_DIM
LRU_HEADS = 4
LRU_WIDTH = LRU_HEADS * HEAD_DIM
CONV_GROUPS = 4
CONV_WIDTH = CONV_GROUPS * HEAD_DIM
MIX_WIDTH = ATTN_WIDTH + LRU_WIDTH + CONV_WIDTH
IN_SPLITS = (ATTN_WIDTH, KV_WIDTH, KV_WIDTH, LRU_WIDTH, LRU_WIDTH, CONV_WIDTH, CONV_WIDTH, CONV_WIDTH)
IN_PROJ_WIDTH = sum(IN_SPLITS)
WINDOW = 128
BLOCK = 128
LRU_CONV_K = 4
SHORT_CONV_K = 3
LRU_C = 8.0
D_FF = ((8 * D_MODEL // 3 + 127) // 128) * 128
N_SUBLAYERS = 3
N_MOD = 3 * N_SUBLAYERS
EPS = 1e-6
NEG_INF = -1e30


def rmsnorm(x, g):
    xf = x.astype(jnp.float32)
    y = xf * lax.rsqrt(jnp.mean(xf * xf, axis=-1, keepdims=True) + EPS)
    return (y * g.astype(jnp.float32)).astype(x.dtype)

def modulate(x, g, shift, scale):
    return rmsnorm(x, g) * (1.0 + scale[:, None, :]) + shift[:, None, :]

def swiglu(h, w_gu, w_down):
    gu = h @ w_gu
    g, u = jnp.split(gu, 2, axis=-1)
    return (jax.nn.silu(g) * u) @ w_down

def causal_depthwise_conv(x, w, b=None):
    K = w.shape[0]
    S = x.shape[1]
    xp = jnp.pad(x, ((0, 0), (K - 1, 0), (0, 0)))
    y = xp[:, 0:S] * w[0]
    for k in range(1, K):
        y = y + xp[:, k:k + S] * w[k]
    if b is not None:
        y = y + b
    return y

def alibi_slopes(n_heads):
    return jnp.asarray(2.0 ** (-8.0 * np.arange(1, n_heads + 1) / n_heads), dtype=jnp.float32)

def sliding_window_attention(q, k, v, sinks):
    b, s = q.shape[:2]
    nb = s // BLOCK
    G = N_Q_HEADS // N_KV_HEADS
    qb = q.reshape(b, nb, BLOCK, N_KV_HEADS, G, HEAD_DIM)

    def band(t):
        tb = t.reshape(b, nb, BLOCK, N_KV_HEADS, HEAD_DIM)
        prev = jnp.pad(tb[:, :-1], ((0, 0), (1, 0), (0, 0), (0, 0), (0, 0)))
        return jnp.concatenate([prev, tb], axis=2)

    kb, vb = band(k), band(v)
    scores = jnp.einsum('bnqkgd,bnskd->bnkgqs', qb, kb).astype(jnp.float32) * (HEAD_DIM ** -0.5)
    qi = jnp.arange(BLOCK)[:, None]
    kj = jnp.arange(2 * BLOCK)[None, :]
    dist = qi + BLOCK - kj
    in_window = (dist >= 0) & (dist < WINDOW)
    blk = jnp.arange(nb)[:, None, None]
    valid = in_window[None] & ((blk > 0) | (kj[None] >= BLOCK))
    slopes = alibi_slopes(N_Q_HEADS).reshape(N_KV_HEADS, G)
    bias = -slopes[:, :, None, None] * dist.astype(jnp.float32)
    scores = jnp.where(valid[None, :, None, None], scores + bias[None, None], NEG_INF)
    sink = sinks.astype(jnp.float32).reshape(N_KV_HEADS, G)[None, None, :, :, None, None]
    m = jnp.maximum(jnp.max(scores, axis=-1, keepdims=True), sink)
    p = jnp.exp(scores - m)
    denom = jnp.sum(p, axis=-1, keepdims=True) + jnp.exp(sink - m)
    out = jnp.einsum('bnkgqs,bnskd->bnqkgd', (p / denom).astype(v.dtype), vb)
    return out.reshape(b, s, ATTN_WIDTH)

def rg_lru(x, gate_a_w, gate_a_b, gate_x_w, gate_x_b, lam):
    b, s, _ = x.shape
    xh = x.reshape(b, s, LRU_HEADS, HEAD_DIM)
    r = jax.nn.sigmoid(jnp.einsum('bshd,hde->bshe', xh, gate_a_w).reshape(b, s, LRU_WIDTH) + gate_a_b)
    i = jax.nn.sigmoid(jnp.einsum('bshd,hde->bshe', xh, gate_x_w).reshape(b, s, LRU_WIDTH) + gate_x_b)
    log_a = -LRU_C * r.astype(jnp.float32) * jax.nn.softplus(-lam.astype(jnp.float32))
    a = jnp.exp(log_a)
    mult = jnp.sqrt(-jnp.expm1(2.0 * log_a))
    first = (jnp.arange(s) == 0)[None, :, None]
    mult = jnp.where(first, 1.0, mult)
    u = mult * (i * x).astype(jnp.float32)

    def combine(left, right):
        a1, b1 = left
        a2, b2 = right
        return a1 * a2, a2 * b1 + b2

    _, h = lax.associative_scan(combine, (a, u), axis=1)
    return h.astype(x.dtype)

def hybrid_mixer(h, w_in, w_out, sinks, lru_conv_w, lru_conv_b, lru_gate_a_w, lru_gate_a_b,
                 lru_gate_x_w, lru_gate_x_b, lru_lambda, sc_conv_w):
    proj = h @ w_in
    offs = np.cumsum(IN_SPLITS)[:-1].tolist()
    q, k, v, lx, lg, sb, sc, sx = jnp.split(proj, offs, axis=-1)
    y_attn = sliding_window_attention(q, k, v, sinks)
    lx = causal_depthwise_conv(lx, lru_conv_w, lru_conv_b)
    y_lru = jax.nn.gelu(lg) * rg_lru(lx, lru_gate_a_w, lru_gate_a_b, lru_gate_x_w, lru_gate_x_b, lru_lambda)
    y_sc = sb * causal_depthwise_conv(sc * sx, sc_conv_w)
    y = jnp.concatenate([y_attn, y_lru, y_sc], axis=-1)
    return y @ w_out

def first_inputs(seed: int = 0) -> dict:
    key = jax.random.key(seed)
    ks = jax.random.split(key, 24)
    f32 = jnp.float32

    def nrm(k, shape, scale):
        return jax.random.normal(k, shape, f32) * scale

    u = jax.random.uniform(ks[17], (DEPTH, LRU_WIDTH), f32, 0.9, 0.999)
    a0 = u ** (1.0 / LRU_C)
    lru_lambda = jnp.log(a0) - jnp.log1p(-a0)
    return {
        "x": nrm(ks[0], (BATCH, SEQ, D_MODEL), 1.0),
        "c": nrm(ks[1], (BATCH, D_MODEL), 1.0),
        "w_mod": nrm(ks[2], (DEPTH, D_MODEL, N_MOD * D_MODEL), D_MODEL ** -0.5),
        "b_mod": nrm(ks[3], (DEPTH, N_MOD * D_MODEL), 0.02),
        "g_norm": 1.0 + nrm(ks[4], (DEPTH, N_SUBLAYERS, D_MODEL), 0.02),
        "w_ffn1_gu": nrm(ks[5], (DEPTH, D_MODEL, 2 * D_FF), D_MODEL ** -0.5),
        "w_ffn1_down": nrm(ks[6], (DEPTH, D_FF, D_MODEL), D_FF ** -0.5),
        "w_ffn2_gu": nrm(ks[7], (DEPTH, D_MODEL, 2 * D_FF), D_MODEL ** -0.5),
        "w_ffn2_down": nrm(ks[8], (DEPTH, D_FF, D_MODEL), D_FF ** -0.5),
        "w_in": nrm(ks[9], (DEPTH, D_MODEL, IN_PROJ_WIDTH), D_MODEL ** -0.5),
        "w_out": nrm(ks[10], (DEPTH, MIX_WIDTH, D_MODEL), MIX_WIDTH ** -0.5),
        "attn_sinks": nrm(ks[11], (DEPTH, N_Q_HEADS), 0.5),
        "lru_conv_w": nrm(ks[12], (DEPTH, LRU_CONV_K, LRU_WIDTH), LRU_CONV_K ** -0.5),
        "lru_conv_b": nrm(ks[13], (DEPTH, LRU_WIDTH), 0.02),
        "lru_gate_a_w": nrm(ks[14], (DEPTH, LRU_HEADS, HEAD_DIM, HEAD_DIM), HEAD_DIM ** -0.5),
        "lru_gate_a_b": nrm(ks[15], (DEPTH, LRU_WIDTH), 0.02),
        "lru_gate_x_w": nrm(ks[16], (DEPTH, LRU_HEADS, HEAD_DIM, HEAD_DIM), HEAD_DIM ** -0.5),
        "lru_gate_x_b": nrm(ks[18], (DEPTH, LRU_WIDTH), 0.02),
        "lru_lambda": lru_lambda,
        "sc_conv_w": nrm(ks[19], (DEPTH, SHORT_CONV_K, CONV_WIDTH), SHORT_CONV_K ** -0.5),
        "g_final": 1.0 + nrm(ks[20], (D_MODEL,), 0.02),
    }

def first_block(x, c, w_mod, b_mod, g_norm, w_ffn1_gu, w_ffn1_down, w_ffn2_gu, w_ffn2_down,
              w_in, w_out, attn_sinks, lru_conv_w, lru_conv_b, lru_gate_a_w, lru_gate_a_b,
              lru_gate_x_w, lru_gate_x_b, lru_lambda, sc_conv_w, g_final):
    c_act = jax.nn.silu(c)
    for l in range(DEPTH):
        mod = (c_act @ w_mod[l] + b_mod[l]).reshape(c.shape[0], N_MOD, D_MODEL)
        h = modulate(x, g_norm[l, 0], mod[:, 0], mod[:, 1])
        x = x + 0.5 * mod[:, 2][:, None, :] * swiglu(h, w_ffn1_gu[l], w_ffn1_down[l])
        h = modulate(x, g_norm[l, 1], mod[:, 3], mod[:, 4])
        x = x + mod[:, 5][:, None, :] * hybrid_mixer(
            h, w_in[l], w_out[l], attn_sinks[l], lru_conv_w[l], lru_conv_b[l],
            lru_gate_a_w[l], lru_gate_a_b[l], lru_gate_x_w[l], lru_gate_x_b[l],
            lru_lambda[l], sc_conv_w[l])
        h = modulate(x, g_norm[l, 2], mod[:, 6], mod[:, 7])
        x = x + 0.5 * mod[:, 8][:, None, :] * swiglu(h, w_ffn2_gu[l], w_ffn2_down[l])
    return rmsnorm(x, g_final)


GRID_W = 64
CTX_LEN = 256
N_MIXERS = 4
QBLOCK = 128
ROPE_BASE = 10000.0
LN_EPS = 1e-5
RMS_EPS = 1e-6
NEG_INF_2 = -1e30
DEEPNORM_ALPHA = (2.0 * DEPTH) ** 0.25
DEEPNORM_BETA = (8.0 * DEPTH) ** -0.25

MLA_HEADS = 16
MLA_NOPE_DIM = 64
MLA_ROPE_DIM = 32
MLA_V_DIM = 64
MLA_Q_LORA = 384
MLA_KV_LORA = 256

NA_HEADS = 16
NA_HEAD_DIM = 64
NA_ROWS = 8
NA_COLS = 16
NA_QCOLS = 16
NA_KCOLS = 32

DIFF_HEADS = 8
DIFF_HEAD_DIM = 64

SWA_HEADS = 16
SWA_KV_HEADS = 4
SWA_HEAD_DIM = 64
SWA_WINDOW = 128

FFN_HIDDEN = 2816
FFN_CONV = 3


def layer_norm(x, g, b):
    xf = x.astype(jnp.float32)
    mu = jnp.mean(xf, -1, keepdims=True)
    var = jnp.mean(jnp.square(xf - mu), -1, keepdims=True)
    return ((xf - mu) * lax.rsqrt(var + LN_EPS)).astype(x.dtype) * g + b

def rms_norm(x, g):
    xf = x.astype(jnp.float32)
    return (xf * lax.rsqrt(jnp.mean(jnp.square(xf), -1, keepdims=True) + RMS_EPS)).astype(x.dtype) * g

def softmax_f32(s):
    return jax.nn.softmax(s.astype(jnp.float32), axis=-1)

def modulate_2(t, shift, scale):
    return t * (1.0 + scale) + shift

def axial_rope(n_tokens, rot_dim):
    t = jnp.arange(n_tokens)
    row = (t // GRID_W).astype(jnp.float32)
    col = (t % GRID_W).astype(jnp.float32)
    n_freq = rot_dim // 4
    inv_freq = ROPE_BASE ** (-jnp.arange(n_freq, dtype=jnp.float32) / n_freq)
    ang = jnp.concatenate([row[:, None] * inv_freq, col[:, None] * inv_freq], -1)
    return jnp.cos(ang), jnp.sin(ang)

def apply_rope(x, cos, sin):
    half = x.shape[-1] // 2
    shp = (cos.shape[0],) + (1,) * (x.ndim - 3) + (half,)
    c = cos.reshape(shp).astype(x.dtype)
    s = sin.reshape(shp).astype(x.dtype)
    x1, x2 = x[..., :half], x[..., half:]
    return jnp.concatenate([x1 * c - x2 * s, x2 * c + x1 * s], -1)

def ctx_attention(q, k, v):
    s = jnp.einsum('bqhd,bkhd->bhqk', q, k).astype(jnp.float32) * q.shape[-1] ** -0.5
    p = softmax_f32(s).astype(v.dtype)
    return jnp.einsum('bhqk,bkhd->bqhd', p, v)

def dense_attention(q_lat, q_ctx, k_lat, v_lat, k_ctx, v_ctx):
    B, S, H, dk = q_lat.shape
    dv = v_lat.shape[-1]
    n_ctx = k_ctx.shape[1]
    scale = dk ** -0.5
    nb = S // QBLOCK

    def to_blocks(t):
        return t.reshape(B, nb, QBLOCK, H, dk).swapaxes(0, 1)

    def one_block(qs):
        ql, qc = qs
        s = jnp.concatenate([jnp.einsum('bqhd,bkhd->bhqk', qc, k_ctx),
                             jnp.einsum('bqhd,bkhd->bhqk', ql, k_lat)], -1)
        p = softmax_f32(s.astype(jnp.float32) * scale).astype(v_lat.dtype)
        return (jnp.einsum('bhqk,bkhd->bqhd', p[..., :n_ctx], v_ctx)
                + jnp.einsum('bhqk,bkhd->bqhd', p[..., n_ctx:], v_lat))

    out = lax.map(one_block, (to_blocks(q_lat), to_blocks(q_ctx)))
    return out.swapaxes(0, 1).reshape(B, S, H, dv)

def mla_mixer(h, hc, w_in, q_norm, kv_norm, w_qb, w_kvb, w_o, need_ctx):
    H, DN, DR, DV, QL = MLA_HEADS, MLA_NOPE_DIM, MLA_ROPE_DIM, MLA_V_DIM, MLA_Q_LORA

    def project_q(t):
        cq = rms_norm(t @ w_in[:, :QL], q_norm)
        return (cq @ w_qb).reshape(t.shape[0], t.shape[1], H, DN + DR)

    def project_kv(t):
        a = t @ w_in[:, QL:]
        ckv = rms_norm(a[..., :MLA_KV_LORA], kv_norm)
        kv = (ckv @ w_kvb).reshape(t.shape[0], t.shape[1], H, DN + DV)
        return kv[..., :DN], kv[..., DN:], a[..., MLA_KV_LORA:]

    def full_key(k_nope, k_pe):
        return jnp.concatenate([k_nope, jnp.broadcast_to(k_pe[:, :, None, :], k_nope.shape[:3] + (DR,))], -1)

    B, S, _ = h.shape
    cos, sin = axial_rope(S, DR)
    q = project_q(h)
    k_nope, v, k_pe = project_kv(h)
    q_rot = jnp.concatenate([q[..., :DN], apply_rope(q[..., DN:], cos, sin)], -1)
    k = full_key(k_nope, apply_rope(k_pe, cos, sin))
    kc_nope, vc, kc_pe = project_kv(hc)
    kc = full_key(kc_nope, kc_pe)
    o = dense_attention(q_rot, q, k, v, kc, vc)
    y = o.reshape(B, S, H * DV) @ w_o
    yc = None
    if need_ctx:
        oc = ctx_attention(project_q(hc), kc, vc)
        yc = oc.reshape(oc.shape[0], oc.shape[1], H * DV) @ w_o
    return y, yc

def neighbourhood_attention(q, k, v, kc, vc, rpb):
    B, S, H, d = q.shape
    n_rows = S // GRID_W
    kr = min(NA_ROWS, n_rows)
    n_ctx = kc.shape[1]
    scale = d ** -0.5
    n_cb = GRID_W // NA_QCOLS
    q_cols = np.arange(GRID_W).reshape(n_cb, NA_QCOLS)
    win_start = np.clip(q_cols - NA_COLS // 2, 0, GRID_W - NA_COLS)
    band_start = np.clip(np.arange(n_cb) * NA_QCOLS - NA_COLS // 2, 0, GRID_W - NA_KCOLS)
    band_cols = band_start[:, None] + np.arange(NA_KCOLS)
    col_valid = ((band_cols[:, None, :] >= win_start[..., None])
                 & (band_cols[:, None, :] < win_start[..., None] + NA_COLS))
    col_idx = np.clip(band_cols[:, None, :] - q_cols[..., None] + NA_COLS - 1, 0, 2 * NA_COLS - 2)
    qg = q.reshape(B, n_rows, GRID_W, H, d)
    kg = k.reshape(B, n_rows, GRID_W, H, d)
    vg = v.reshape(B, n_rows, GRID_W, H, d)

    def row_block(r):
        r0 = jnp.clip(r - kr // 2, 0, n_rows - kr)
        kb = lax.dynamic_slice_in_dim(kg, r0, kr, axis=1)[:, :, band_cols]
        vb = lax.dynamic_slice_in_dim(vg, r0, kr, axis=1)[:, :, band_cols]
        qr = lax.dynamic_index_in_dim(qg, r, axis=1, keepdims=False).reshape(B, n_cb, NA_QCOLS, H, d)
        s = jnp.einsum('bjqhd,bmjnhd->bhjqmn', qr, kb).astype(jnp.float32) * scale
        row_idx = r0 + jnp.arange(kr) - r + NA_ROWS - 1
        bias = rpb[:, row_idx][:, :, col_idx].transpose(0, 2, 3, 1, 4)
        s = jnp.where(col_valid[:, :, None, :], s + bias.astype(jnp.float32), NEG_INF_2)
        s_ctx = jnp.einsum('bjqhd,bkhd->bhjqk', qr, kc).astype(jnp.float32) * scale
        p = softmax_f32(jnp.concatenate(
            [s_ctx, s.reshape(B, H, n_cb, NA_QCOLS, kr * NA_KCOLS)], -1)).astype(v.dtype)
        p_lat = p[..., n_ctx:].reshape(B, H, n_cb, NA_QCOLS, kr, NA_KCOLS)
        o = (jnp.einsum('bhjqk,bkhd->bjqhd', p[..., :n_ctx], vc)
             + jnp.einsum('bhjqmn,bmjnhd->bjqhd', p_lat, vb))
        return o.reshape(B, GRID_W, H, d)

    out = lax.map(row_block, jnp.arange(n_rows))
    return out.swapaxes(0, 1).reshape(B, S, H, d)

def na_mixer(h, hc, w_qkv, rpb, w_o, need_ctx):
    H, d = NA_HEADS, NA_HEAD_DIM
    nq = H * d

    def project_q(t):
        return (t @ w_qkv[:, :nq]).reshape(t.shape[0], t.shape[1], H, d)

    def project_kv(t):
        a = (t @ w_qkv[:, nq:]).reshape(t.shape[0], t.shape[1], 2, H, d)
        return a[:, :, 0], a[:, :, 1]

    B, S, _ = h.shape
    q = project_q(h)
    k, v = project_kv(h)
    kc, vc = project_kv(hc)
    y = neighbourhood_attention(q, k, v, kc, vc, rpb).reshape(B, S, H * d) @ w_o
    yc = None
    if need_ctx:
        oc = ctx_attention(project_q(hc), kc, vc)
        yc = oc.reshape(oc.shape[0], oc.shape[1], H * d) @ w_o
    return y, yc

def diff_mixer(h, hc, w_qkv, lam, subln, w_o, layer_idx, need_ctx):
    H, d = DIFF_HEADS, DIFF_HEAD_DIM
    nq = 2 * H * d

    def project_q(t):
        return (t @ w_qkv[:, :nq]).reshape(t.shape[0], t.shape[1], H, 2, d)

    def project_kv(t):
        a = t @ w_qkv[:, nq:]
        return (a[..., :nq].reshape(t.shape[0], t.shape[1], H, 2, d),
                a[..., nq:].reshape(t.shape[0], t.shape[1], H, 2 * d))

    lambda_init = 0.8 - 0.6 * math.exp(-0.3 * layer_idx)
    lf = lam.astype(jnp.float32)
    lam_full = jnp.exp(jnp.sum(lf[0] * lf[1])) - jnp.exp(jnp.sum(lf[2] * lf[3])) + lambda_init

    def combine(o1, o2):
        o = o1 - lam_full.astype(o1.dtype) * o2
        o = rms_norm(o, subln) * (1.0 - lambda_init)
        return o.reshape(o.shape[0], o.shape[1], H * 2 * d) @ w_o

    B, S, _ = h.shape
    cos, sin = axial_rope(S, d)
    q = project_q(h)
    k, v = project_kv(h)
    q_rot, k_rot = apply_rope(q, cos, sin), apply_rope(k, cos, sin)
    kc, vc = project_kv(hc)
    o1 = dense_attention(q_rot[:, :, :, 0], q[:, :, :, 0], k_rot[:, :, :, 0], v, kc[:, :, :, 0], vc)
    o2 = dense_attention(q_rot[:, :, :, 1], q[:, :, :, 1], k_rot[:, :, :, 1], v, kc[:, :, :, 1], vc)
    y = combine(o1, o2)
    yc = None
    if need_ctx:
        qc = project_q(hc)
        yc = combine(ctx_attention(qc[:, :, :, 0], kc[:, :, :, 0], vc),
                     ctx_attention(qc[:, :, :, 1], kc[:, :, :, 1], vc))
    return y, yc

def windowed_sink_attention(q_lat, q_ctx, k_lat, v_lat, k_ctx, v_ctx, sinks):
    B, S, G, R, d = q_lat.shape
    n_ctx = k_ctx.shape[1]
    scale = d ** -0.5
    nb = S // QBLOCK
    band = QBLOCK + 2 * SWA_WINDOW
    pad = ((0, 0), (SWA_WINDOW, SWA_WINDOW), (0, 0), (0, 0))
    kp = jnp.pad(k_lat, pad)
    vp = jnp.pad(v_lat, pad)
    sink_logit = sinks.astype(jnp.float32).reshape(G, R)[None, :, :, None, None]

    def one_block(n):
        start = n * QBLOCK
        ql = lax.dynamic_slice_in_dim(q_lat, start, QBLOCK, axis=1)
        qc = lax.dynamic_slice_in_dim(q_ctx, start, QBLOCK, axis=1)
        kb = lax.dynamic_slice_in_dim(kp, start, band, axis=1)
        vb = lax.dynamic_slice_in_dim(vp, start, band, axis=1)
        qpos = start + jnp.arange(QBLOCK)
        kpos = start - SWA_WINDOW + jnp.arange(band)
        valid = ((jnp.abs(qpos[:, None] - kpos[None, :]) <= SWA_WINDOW)
                 & (kpos[None, :] >= 0) & (kpos[None, :] < S))
        s_lat = jnp.where(valid, jnp.einsum('bqgrd,bkgd->bgrqk', ql, kb).astype(jnp.float32) * scale, NEG_INF_2)
        s_ctx = jnp.einsum('bqgrd,bkgd->bgrqk', qc, k_ctx).astype(jnp.float32) * scale
        sink = jnp.broadcast_to(sink_logit, s_ctx.shape[:-1] + (1,))
        p = softmax_f32(jnp.concatenate([sink, s_ctx, s_lat], -1))[..., 1:].astype(v_lat.dtype)
        return (jnp.einsum('bgrqk,bkgd->bqgrd', p[..., :n_ctx], v_ctx)
                + jnp.einsum('bgrqk,bkgd->bqgrd', p[..., n_ctx:], vb))

    out = lax.map(one_block, jnp.arange(nb))
    return out.swapaxes(0, 1).reshape(B, S, G * R * d)

def ctx_sink_attention(q, k, v, sinks):
    B, L, G, R, d = q.shape
    s = jnp.einsum('bqgrd,bkgd->bgrqk', q, k).astype(jnp.float32) * d ** -0.5
    sink = jnp.broadcast_to(sinks.astype(jnp.float32).reshape(G, R)[None, :, :, None, None], s.shape[:-1] + (1,))
    p = softmax_f32(jnp.concatenate([sink, s], -1))[..., 1:].astype(v.dtype)
    return jnp.einsum('bgrqk,bkgd->bqgrd', p, v).reshape(B, L, G * R * d)

def swa_mixer(h, hc, w_qkv, sinks, w_o, need_ctx):
    H, G, d = SWA_HEADS, SWA_KV_HEADS, SWA_HEAD_DIM
    R = H // G
    nq = H * d

    def project_q(t):
        return (t @ w_qkv[:, :nq]).reshape(t.shape[0], t.shape[1], G, R, d)

    def project_kv(t):
        a = t @ w_qkv[:, nq:]
        return (a[..., :G * d].reshape(t.shape[0], t.shape[1], G, d),
                a[..., G * d:].reshape(t.shape[0], t.shape[1], G, d))

    B, S, _ = h.shape
    cos, sin = axial_rope(S, d)
    q = project_q(h)
    k, v = project_kv(h)
    kc, vc = project_kv(hc)
    o = windowed_sink_attention(apply_rope(q, cos, sin), q, apply_rope(k, cos, sin), v, kc, vc, sinks)
    y = o @ w_o
    yc = None
    if need_ctx:
        yc = ctx_sink_attention(project_q(hc), kc, vc, sinks) @ w_o
    return y, yc

def conv_ffn(h, w_in, conv_w, conv_b, w_out):
    u = h @ w_in
    u = lax.conv_general_dilated(
        u, conv_w[:, None, :].astype(u.dtype), window_strides=(1,),
        padding=[(FFN_CONV // 2, FFN_CONV // 2)],
        dimension_numbers=('NWC', 'WIO', 'NWC'),
        feature_group_count=u.shape[-1]) + conv_b
    a, g = jnp.split(u, 2, axis=-1)
    return (jax.nn.silu(g) * a) @ w_out

def second_inputs(seed: int = 0) -> dict:
    key = jax.random.key(seed)
    ks = iter(jax.random.split(key, 40))

    def nrm(shape, scale):
        return jax.random.normal(next(ks), shape, jnp.float32) * scale

    D, F = D_MODEL, FFN_HIDDEN
    beta = DEEPNORM_BETA
    n_a, n_b, n_c, n_d = [len(range(m, DEPTH, N_MIXERS)) for m in range(N_MIXERS)]
    mla_in = MLA_Q_LORA + MLA_KV_LORA + MLA_ROPE_DIM
    return {
        'x': nrm((BATCH, SEQ, D), 1.0),
        'c': nrm((BATCH, D), 1.0),
        'ctx': nrm((BATCH, CTX_LEN, D), 1.0),
        'c_ctx': nrm((D,), 1.0),
        'ada_w': nrm((DEPTH, D, 6 * D), 0.5 * D ** -0.5),
        'ada_b': nrm((DEPTH, 6 * D), 0.01),
        'ln1_g': 1.0 + nrm((DEPTH, D), 0.02),
        'ln1_b': nrm((DEPTH, D), 0.02),
        'ln2_g': 1.0 + nrm((DEPTH, D), 0.02),
        'ln2_b': nrm((DEPTH, D), 0.02),
        'ffn_w_in': nrm((DEPTH, D, 2 * F), D ** -0.5),
        'ffn_conv_w': nrm((DEPTH, FFN_CONV, 2 * F), FFN_CONV ** -0.5),
        'ffn_conv_b': nrm((DEPTH, 2 * F), 0.01),
        'ffn_w_out': nrm((DEPTH, F, D), beta * F ** -0.5),
        'mla_w_in': nrm((n_a, D, mla_in), D ** -0.5),
        'mla_q_norm': 1.0 + nrm((n_a, MLA_Q_LORA), 0.02),
        'mla_kv_norm': 1.0 + nrm((n_a, MLA_KV_LORA), 0.02),
        'mla_w_qb': nrm((n_a, MLA_Q_LORA, MLA_HEADS * (MLA_NOPE_DIM + MLA_ROPE_DIM)), MLA_Q_LORA ** -0.5),
        'mla_w_kvb': nrm((n_a, MLA_KV_LORA, MLA_HEADS * (MLA_NOPE_DIM + MLA_V_DIM)), MLA_KV_LORA ** -0.5),
        'mla_w_o': nrm((n_a, MLA_HEADS * MLA_V_DIM, D), beta * (MLA_HEADS * MLA_V_DIM) ** -0.5),
        'na_w_qkv': nrm((n_b, D, 3 * NA_HEADS * NA_HEAD_DIM), D ** -0.5),
        'na_rpb': nrm((n_b, NA_HEADS, 2 * NA_ROWS - 1, 2 * NA_COLS - 1), 0.1),
        'na_w_o': nrm((n_b, NA_HEADS * NA_HEAD_DIM, D), beta * (NA_HEADS * NA_HEAD_DIM) ** -0.5),
        'diff_w_qkv': nrm((n_c, D, 6 * DIFF_HEADS * DIFF_HEAD_DIM), D ** -0.5),
        'diff_lambda': nrm((n_c, 4, DIFF_HEAD_DIM), 0.1),
        'diff_subln': 1.0 + nrm((n_c, 2 * DIFF_HEAD_DIM), 0.02),
        'diff_w_o': nrm((n_c, DIFF_HEADS * 2 * DIFF_HEAD_DIM, D), beta * (DIFF_HEADS * 2 * DIFF_HEAD_DIM) ** -0.5),
        'swa_w_qkv': nrm((n_d, D, (SWA_HEADS + 2 * SWA_KV_HEADS) * SWA_HEAD_DIM), D ** -0.5),
        'swa_sinks': nrm((n_d, SWA_HEADS), 0.5),
        'swa_w_o': nrm((n_d, SWA_HEADS * SWA_HEAD_DIM, D), beta * (SWA_HEADS * SWA_HEAD_DIM) ** -0.5),
    }

def second_block(x, c, ctx, c_ctx, ada_w, ada_b, ln1_g, ln1_b, ln2_g, ln2_b,
              ffn_w_in, ffn_conv_w, ffn_conv_b, ffn_w_out,
              mla_w_in, mla_q_norm, mla_kv_norm, mla_w_qb, mla_w_kvb, mla_w_o,
              na_w_qkv, na_rpb, na_w_o,
              diff_w_qkv, diff_lambda, diff_subln, diff_w_o,
              swa_w_qkv, swa_sinks, swa_w_o):
    silu_c = jax.nn.silu(c)
    silu_cc = jax.nn.silu(c_ctx)
    h_lat, h_ctx = x, ctx
    for i in range(DEPTH):
        last = i == DEPTH - 1
        need_ctx = not last
        m = (silu_c @ ada_w[i] + ada_b[i])[:, None, :]
        sh1, sc1, g1, sh2, sc2, g2 = jnp.split(m, 6, axis=-1)
        mc = silu_cc @ ada_w[i] + ada_b[i]
        csh1, csc1, cg1, csh2, csc2, cg2 = jnp.split(mc, 6, axis=-1)
        a_lat = modulate_2(h_lat, sh1, sc1)
        a_ctx = modulate_2(h_ctx, csh1, csc1)
        kind, slot = i % N_MIXERS, i // N_MIXERS
        if kind == 0:
            y, yc = mla_mixer(a_lat, a_ctx, mla_w_in[slot], mla_q_norm[slot], mla_kv_norm[slot],
                              mla_w_qb[slot], mla_w_kvb[slot], mla_w_o[slot], need_ctx)
        elif kind == 1:
            y, yc = na_mixer(a_lat, a_ctx, na_w_qkv[slot], na_rpb[slot], na_w_o[slot], need_ctx)
        elif kind == 2:
            y, yc = diff_mixer(a_lat, a_ctx, diff_w_qkv[slot], diff_lambda[slot], diff_subln[slot],
                               diff_w_o[slot], i, need_ctx)
        else:
            y, yc = swa_mixer(a_lat, a_ctx, swa_w_qkv[slot], swa_sinks[slot], swa_w_o[slot], need_ctx)
        h_lat = layer_norm(DEEPNORM_ALPHA * h_lat + g1 * y, ln1_g[i], ln1_b[i])
        f = conv_ffn(modulate_2(h_lat, sh2, sc2), ffn_w_in[i], ffn_conv_w[i], ffn_conv_b[i], ffn_w_out[i])
        h_lat = layer_norm(DEEPNORM_ALPHA * h_lat + g2 * f, ln2_g[i], ln2_b[i])
        if need_ctx:
            h_ctx = layer_norm(DEEPNORM_ALPHA * h_ctx + cg1 * yc, ln1_g[i], ln1_b[i])
            fc = conv_ffn(modulate_2(h_ctx, csh2, csc2), ffn_w_in[i], ffn_conv_w[i], ffn_conv_b[i], ffn_w_out[i])
            h_ctx = layer_norm(DEEPNORM_ALPHA * h_ctx + cg2 * fc, ln2_g[i], ln2_b[i])
    return h_lat


def setup_inputs(seed=0):
    out = dict(first_inputs(seed))
    for name, value in second_inputs(seed + 1).items():
        if name != "x":
            out[name + "_2"] = value
    return out


def reference(
    x, c, w_mod, b_mod, g_norm, w_ffn1_gu, w_ffn1_down, w_ffn2_gu, w_ffn2_down, w_in, w_out,
    attn_sinks, lru_conv_w, lru_conv_b, lru_gate_a_w, lru_gate_a_b, lru_gate_x_w, lru_gate_x_b,
    lru_lambda, sc_conv_w, g_final, c_2, ctx_2, c_ctx_2, ada_w_2, ada_b_2, ln1_g_2, ln1_b_2,
    ln2_g_2, ln2_b_2, ffn_w_in_2, ffn_conv_w_2, ffn_conv_b_2, ffn_w_out_2, mla_w_in_2,
    mla_q_norm_2, mla_kv_norm_2, mla_w_qb_2, mla_w_kvb_2, mla_w_o_2, na_w_qkv_2, na_rpb_2,
    na_w_o_2, diff_w_qkv_2, diff_lambda_2, diff_subln_2, diff_w_o_2, swa_w_qkv_2, swa_sinks_2,
    swa_w_o_2,
):
    x = first_block(
        x, c, w_mod, b_mod, g_norm, w_ffn1_gu, w_ffn1_down, w_ffn2_gu, w_ffn2_down, w_in, w_out,
        attn_sinks, lru_conv_w, lru_conv_b, lru_gate_a_w, lru_gate_a_b, lru_gate_x_w,
        lru_gate_x_b, lru_lambda, sc_conv_w, g_final,
    )
    return second_block(
        x, c_2, ctx_2, c_ctx_2, ada_w_2, ada_b_2, ln1_g_2, ln1_b_2, ln2_g_2, ln2_b_2,
        ffn_w_in_2, ffn_conv_w_2, ffn_conv_b_2, ffn_w_out_2, mla_w_in_2, mla_q_norm_2,
        mla_kv_norm_2, mla_w_qb_2, mla_w_kvb_2, mla_w_o_2, na_w_qkv_2, na_rpb_2, na_w_o_2,
        diff_w_qkv_2, diff_lambda_2, diff_subln_2, diff_w_o_2, swa_w_qkv_2, swa_sinks_2,
        swa_w_o_2,
    )


_drawn_inputs = setup_inputs


def setup_inputs(seed=0):
    import zlib

    import numpy as np

    out = dict(_drawn_inputs(seed))
    spreads = {}
    factors = {'attn_sinks': 2.971,
     'lru_gate_a_b': 8.0,
     'lru_gate_x_b': 8.0,
     'g_final': 2.831,
     'ctx_2': 5.454,
     'ada_b_2': 8.0,
     'ffn_conv_b_2': 37.583,
     'mla_q_norm_2': 8.0,
     'mla_kv_norm_2': 8.0,
     'mla_w_qb_2': 4.497,
     'na_rpb_2': 64.0}
    for name, (base, spread) in spreads.items():
        noise = np.random.default_rng([zlib.crc32(name.encode()), seed]).standard_normal(out[name].shape)
        drawn = base * np.exp(spread * noise) if base else spread * noise
        out[name] = jnp.asarray(drawn.astype(out[name].dtype))
    for name, factor in factors.items():
        out[name] = (out[name] * factor).astype(out[name].dtype)
    return out
```

```python
import numpy as np

import concourse.bass as bass
from concourse import mybir

F32 = mybir.dt.float32
F32R = mybir.dt.float32r
ACT = mybir.ActivationFunctionType
ALU = mybir.AluOpType
AX_X = mybir.AxisListType.X
ds = bass.ds

P = 128
D = 1024
S = 512
C = 256
KD = D // P
DEPTH = 2
FF = 2816
FC = FF // P
HALVES = ((0, 12), (12, FC - 12))
GP = 256
MOD_PANELS = 9 * D // GP
ADA_PANELS = 6 * D // GP
G_ADA = DEPTH * MOD_PANELS
G_ALL = G_ADA + DEPTH * ADA_PANELS
CTX_COL = 2 * G_ALL
MOD_COLS = CTX_COL + 2 * DEPTH * ADA_PANELS
NQ, HD = 8, 64
EPS_RMS, EPS_LN = 1e-6, 1e-5
ALPHA = (2.0 * DEPTH) ** 0.25
NEG = -1e30
PROLOGUE = 8
T = C + S
NH = 16
PER = 4
LQ, LKV, NOPE, ROPE = 384, 256, 64, 32
DQ = NOPE + ROPE
GRID, NA_ROWS, NA_COLS, QC, KC_ = 64, 8, 16, 16, 32
ROWS = S // GRID
WIDE = QC + KC_
BAND = [min(max(j * QC - NA_COLS // 2, 0), GRID - KC_) for j in range(GRID // QC)]


class Counts:

    def __init__(self):
        self.at = {}

    def __getitem__(self, name):
        return self.at.get(name, 0)

    def add(self, more):
        for name, n in more.items():
            self.at[name] = self.at.get(name, 0) + n


class Chain:

    def __init__(self, eng, sem):
        self.eng, self.sem, self.n = eng, sem, 0

    def step(self, ins):
        ins.then_inc(self.sem, 1)
        self.n = self.n + 1
        return self.n

    def wait(self, value):
        self.eng.wait_ge(self.sem, value)

    def link(self, ins):
        self.wait(self.step(ins))

    def loop(self, count, per, body, peel=True):
        start = self.n
        if count > 1:
            with self.eng.Fori(0, count - 1) as i:
                self.n = start + i * per
                body(i, False)
        self.n = start + (count - 1) * per
        body(count - 1, True)
        assert self.n == start + count * per, (self.n - start - (count - 1) * per, per)


def vector_rows(a):
    def rows(ap, pattern, **kw):
        return ap.rearrange(pattern, q=P, **kw)

    return [
        ("c", rows(a["c"], "a (k q) -> (a k) q")),
        ("c_2", rows(a["c_2"], "a (k q) -> (a k) q")),
        ("c_ctx", rows(a["c_ctx_2"], "(k q) -> k q")),
        ("b_mod", rows(a["b_mod"], "l (k q) -> (l k) q")),
        ("ada_b", rows(a["ada_b_2"], "l (k q) -> (l k) q")),
        ("g_norm", rows(a["g_norm"], "l s (k q) -> (l s k) q")),
        ("g_final", rows(a["g_final"], "(k q) -> k q")),
        ("ln1_g", rows(a["ln1_g_2"], "l (k q) -> (l k) q")),
        ("ln1_b", rows(a["ln1_b_2"], "l (k q) -> (l k) q")),
        ("ln2_g", rows(a["ln2_g_2"], "l (k q) -> (l k) q")),
        ("ln2_b", rows(a["ln2_b_2"], "l (k q) -> (l k) q")),
        ("fconv_w", rows(a["ffn_conv_w_2"], "l t (k q) -> (l t k) q")),
        ("fconv_b", rows(a["ffn_conv_b_2"], "l (k q) -> (l k) q")),
        ("lconv_w", rows(a["lru_conv_w"], "l t (k q) -> (l t k) q")),
        ("lconv_b", rows(a["lru_conv_b"], "l (k q) -> (l k) q")),
        ("gate_a_b", rows(a["lru_gate_a_b"], "l (k q) -> (l k) q")),
        ("gate_x_b", rows(a["lru_gate_x_b"], "l (k q) -> (l k) q")),
        ("lam", rows(a["lru_lambda"], "l (k q) -> (l k) q")),
        ("sconv_w", rows(a["sc_conv_w"], "l t (k q) -> (l t k) q")),
        ("q_norm", rows(a["mla_q_norm_2"], "l (k q) -> (l k) q")),
        ("kv_norm", rows(a["mla_kv_norm_2"], "l (k q) -> (l k) q")),
    ]


def weight_panels(w):
    return w.rearrange("(k p) n -> p k n", p=P)


def gu_step(w, half, norm_first, gemv, conv=None, N=S, ctx=False):
    k0, n = HALVES[half]
    wp = weight_panels(w)
    return dict(kind="gu", iters=n // 2, shapes=[(KD, 2 * P)] * 2, n=n, wait_h=norm_first, gemv=gemv, conv=conv, k0=k0, N=N, ctx=ctx,
                dma=lambda i, j: [(None, wp[:, :, ds((j if conv is None else 1 - j) * FF + k0 * P + (i * 2 if j else i) * (P if j else 2 * P), 2 * P)])],
                totals=dict(g_read=n // 2, product=n // 2, hid_hi=n // 2, hid_lo=n // 2,
                            g_affine=n // 2 if conv is not None else 0, g_conv=n // 2 if conv is not None else 0,
                            u_affine=n // 2 if conv is not None else 0))


def dn_step(w, half, gate, gemv, N=S, ctx=False):
    k0, nk = HALVES[half]
    wp = weight_panels(w)
    return dict(kind="dn", iters=KD // 2, shapes=[(nk, P)] * 2, nk=nk, gate=gate, gemv=gemv, N=N, ctx=ctx,
                dma=lambda i, j: [(None, wp[:, k0:k0 + nk, ds(j * P + i * (2 * P), P)])],
                totals=dict(down0=KD // 2, down1=KD // 2))


def proj_step(dma, gate, gemv, ctx_gate=None):
    return dict(kind="proj", iters=2, shapes=[(KD, 2 * P)] * 2, gate=gate, gemv=gemv, ctx_gate=ctx_gate,
                dma=dma, totals=dict(proj0=2, proj1=2))


def plan_block2(a, col):
    steps = []
    for l in range(DEPTH):
        m = lambda k: 2 * G_ADA + l * 2 * ADA_PANELS + k * KD
        cm = lambda k: CTX_COL + l * 2 * ADA_PANELS + k * KD
        wo = weight_panels((a["mla_w_o_2"] if l == 0 else a["na_w_o_2"])[0])
        w_gu, w_dn = a["ffn_w_in_2"][l], a["ffn_w_out_2"][l]
        conv = (col["fconv_w"] + l * 3 * 2 * FC, col["fconv_b"] + l * 2 * FC)
        ln = lambda n, p: col[f"ln{n}_{p}"] + l * KD
        if l == 0:
            steps += [dict(kind="prologue", gemvs=[G_ADA + ADA_PANELS - 1], totals={})]
        steps += [mods_step(G_ADA + (l + 1) * ADA_PANELS, [(m(0), m(6), m(0)), (cm(0), cm(6), m(0))], None,
                            plus=[(m(1), None), (m(4), None), (cm(1), None), (cm(4), None)]),
                  norm_step("mod_h", m(1), m(0)),
                  norm_step("mod_h", cm(1), cm(0), N=C, ctx=True, dst="ch")]
        if l == 0:
            steps += [mla_in_step(a), mla_step(a),
                      dict(kind="gather", ctx=True, totals=dict(h_hi=16, h_ready=16))]
        else:
            steps += [na_step(a), dict(kind="gather", ctx=False, totals=dict(h_hi=8, h_ready=8))]
        steps += [dict(kind="alpha", ctx=False, totals={})]
        if l == 0:
            steps += [dict(kind="alpha", ctx=True, totals={})]
        steps += [proj_step(lambda i, j, wo=wo: [(None, wo[:, :, ds(j * 2 * P + i * (4 * P), 2 * P)])], m(2), None,
                            ctx_gate=cm(2) if l == 0 else None),
                  norm_step("ln_x", ln(1, "g"), ln(1, "b"))]
        if l == 0:
            steps += [norm_step("ln_x", ln(1, "g"), ln(1, "b"), N=C, ctx=True)]
        for ctx in ((False, True) if l == 0 else (False,)):
            f, N = (cm, C) if ctx else (m, S)
            g = [(96, 102, 106, 111), (None, None, 115, None)][ctx] if l == 0 else (None,) * 4
            steps += [norm_step("mod_h", f(4), f(3), N=N, ctx=ctx), dict(kind="alpha", ctx=ctx, totals={}),
                      gu_step(w_gu, 0, True, g[0], conv, N, ctx), dn_step(w_dn, 0, f(5), g[1], N, ctx),
                      gu_step(w_gu, 1, False, g[2], conv, N, ctx), dn_step(w_dn, 1, f(5), g[3], N, ctx),
                      norm_step("ln_x", ln(2, "g"), ln(2, "b"), N=N, ctx=ctx)]
    return steps


def mla_in_step(a):
    wp = weight_panels(a["mla_w_in_2"][0])
    spans = [(0, 256), (256, 512), (512, 640), (LQ + LKV + ROPE - DQ, LQ + LKV + ROPE)]
    return dict(kind="mla_in", iters=1, shapes=[(KD, hi - lo) for lo, hi in spans],
                dma=lambda i, j: [(None, wp[:, :, spans[j][0]:spans[j][1]])],
                totals=dict(low_out=4, low_sq=5, low_sum=2, low_dev=2, low_full=5, low_hi=5, low_lo=5,
                            pe_rot=1, pe_key=1, rope_in=48))


def mla_step(a):
    wq, wkv = weight_panels(a["mla_w_qb_2"][0]), weight_panels(a["mla_w_kvb_2"][0])
    units = PER * 6
    n = NH // PER
    return dict(kind="mla", iters=n, shapes=[(3, PER * DQ), (2, PER * P)],
                dma=lambda i, j: [(None, (wq, wkv)[j][:, :, ds(i * (PER * (DQ, P)[j]), PER * (DQ, P)[j])])],
                totals=dict(head_mm=3 * n, head_out=3 * n, q_rot=n, s_made=units * n, s_max=units * n, s_exp=units * n,
                            turned0=units * n, turned1=4 * PER * n, copied0=units * n, copied1=4 * PER * n,
                            s_weighted=units * n, s_shared=units * n, s_kept=PER * n))


def na_step(a):
    w = weight_panels(a["na_w_qkv_2"][0])
    units = PER * 4
    n = NH // PER
    halves = [(0, KD), (0, KD), (0, KD // 2), (KD // 2, KD)]
    return dict(kind="na", iters=n, shapes=[(k1 - k0, 2 * P) for k0, k1 in halves],
                dma=lambda i, j: [(None, w[:, halves[j][0]:halves[j][1], ds(min(j, 2) * D + i * (2 * P), 2 * P)])],
                totals=dict(n_out=n, n_out_q=n, bias_in0=PER // 2 * n * 16 * ROWS, bias_in1=PER // 2 * n * 16 * ROWS,
                            bias_made=units * n, na_mask=16, band_in=n * 16 * 4 * ROWS, s_biased=units * n,
                            s_made=units * n, s_max=units * n, s_exp=units * n, turned0=units * n, turned1=units * n,
                            copied0=units * n, copied1=units * n, s_weighted=units * n, s_shared=units * n, s_kept=PER // 2 * n))


def norm_step(mode, A, B=None, N=S, ctx=False, dst="h"):
    tot = {}
    if mode in ("rms_h", "rms_x", "ln_x"):
        tot.update(squared=KD, square_summed=KD, deviation=1)
    if mode == "ln_x":
        tot.update(mean_summed=1, centred=KD)
    if mode in ("rms_h", "mod_h"):
        tot.update(h_full=KD, h_hi=KD, h_ready=KD)
    if mode in ("rms_x", "ln_x"):
        tot.update(x_new=KD)
    return dict(kind="norm", mode=mode, A=A, B=B, N=N, ctx=ctx, dst=dst, totals=tot)


def mods_step(need, lo, hi, plus=(), half=()):
    return dict(kind="mods", need=need, spans=[(lo, hi, lo)] if isinstance(lo, int) else lo, plus=plus, half=half, totals={})


def plan_block1(a, col):
    steps = [dict(kind="load", totals=dict(row_tile=7, row_col=7, x_tr=KD, x_in=KD, hc_tr=KD, hc_in=KD, c_act=1)),
             dict(kind="prologue", gemvs=range(PROLOGUE), totals={})]
    M = 2 * MOD_PANELS
    g = [None] * DEPTH
    for l in range(DEPTH):
        m = lambda k: l * M + k * KD
        gn = lambda s: col["g_norm"] + (l * 3 + s) * KD
        w_gu, w_dn = (a["w_ffn1_gu"][l], a["w_ffn2_gu"][l]), (a["w_ffn1_down"][l], a["w_ffn2_down"][l])
        free = [(8, 14, 18, 23), (55, 61, 65, None)][l]
        steps += [mods_step(l * MOD_PANELS + 8, m(0), m(2), plus=[(m(1), gn(0))]),
                  norm_step("rms_h", m(1), m(0)),
                  gu_step(w_gu[0], 0, True, free[0]),
                  mods_step(l * MOD_PANELS + 12, m(2), m(3), half=[m(2)]),
                  dn_step(w_dn[0], 0, m(2), free[1]),
                  gu_step(w_gu[0], 1, False, free[2]),
                  dn_step(w_dn[0], 1, m(2), free[3]),
                  mods_step(l * MOD_PANELS + 24, m(3), m(6), plus=[(m(4), gn(1))]),
                  norm_step("rms_h", m(4), m(3)),
                  mixer_step(a, l, [range(27, 32), range(70, 76)][l]),
                  proj_step(mixer_out_dma(a["w_out"][l]), m(5), None),
                  ]
        gm = [range(32, 36), range(76, 80)][l]
        steps += [dict(kind="prologue", gemvs=gm, totals={}),
                  mods_step(l * MOD_PANELS + 36, m(6), m(9), plus=[(m(7), gn(2))], half=[m(8)]),
                  norm_step("rms_h", m(7), m(6))]
        free = [(36, 42, 46, 51), (80, 86, 90, None)][l]
        steps += [gu_step(w_gu[1], 0, True, free[0]),
                  dn_step(w_dn[1], 0, m(8), free[1]),
                  gu_step(w_gu[1], 1, False, free[2]),
                  dn_step(w_dn[1], 1, m(8), free[3])]
    steps += [norm_step("rms_x", col["g_final"])]
    return steps


def mixer_step(a, l, gemvs):
    wp = weight_panels(a["w_in"][l])
    starts = [768, 1024, 1536, 1792, 1280, 512]

    def dma(i, j):
        if j < 6:
            return [(None, wp[:, :, starts[j]:starts[j] + 2 * P])]
        out = []
        for c in range(2):
            for g in range(2):
                head = g * 4 + 2 * (j - 6) + c
                out.append((("cols", (2 * c + g) * HD, HD), wp[:, :, head * HD:head * HD + HD]))
        return out

    return dict(kind="mixer", iters=1, shapes=[(KD, 2 * P)] * 8, dma=dma, l=l, gemvs=list(gemvs), w=a["w_in"][l],
                totals=dict(in_evac=8, lconv=2, gates_mm=2, gates_r=2, gates_i=2, lru_t=1, lru_m=1, lru_q=1, lru_h=1,
                            gelu=1, y_lru=1, y_sc=1, lam_in=1, lam_exp=1, at_s_read=8, at_s=8, at_sub=8, at_exp=8, at_p=8, at_t=8, at_pt=8,
                            at_o=8, y_at=4, h_hi=8, h_ready=8, misc_in=160))


def mixer_out_dma(w):
    wp = weight_panels(w)
    heads = w[0:512, :].rearrange("(g i d) n -> d g i n", g=2, d=HD)

    def dma(i, j):
        c = ds(j * 2 * P + i * (4 * P), 2 * P)
        return [(("k", 4, 8, 0, P), wp[:, 4:8, c]),
                (("k", 0, 4, 0, HD), heads[:, 0, :, c]),
                (("k", 0, 4, HD, P), heads[:, 1, :, c])]
    return dma


def build(nc, a, out, upto=99, probe=False):
    rows = vector_rows(a)
    col, at = {}, 0
    for name, ap in rows:
        col[name] = at
        at += ap.shape[0]
    n_rows = at
    row_tiles = -(-n_rows // P)
    assert row_tiles == 7 and col["ada_b"] == col["b_mod"] + 2 * G_ADA
    PLAN = (plan_block1(a, col) + plan_block2(a, col))[:upto]
    PLAN.append(dict(kind="store", probe=probe, totals=dict(o_tr=4, o_out=4)))

    n_panels, n_gemvs, raw_count = 0, 0, [0, 0]
    for st in PLAN:
        st["shapes"] = st.get("shapes", [])
        st["iters"] = st.get("iters", 0)
        st["p0"] = n_panels
        st["raw0"] = tuple(raw_count)
        st["n_dma"] = [len(st["dma"](0, j)) for j in range(len(st["shapes"]))]
        for j, n in enumerate(st["n_dma"]):
            raw_count[j % 2] += 16 * n * st["iters"]
        n_panels += len(st["shapes"]) * st["iters"]
        if st["kind"] == "mods":
            assert n_gemvs >= st["need"], (n_gemvs, st["need"])
            st["need"] = n_gemvs
        n_gemvs += len(st.get("gemvs", ())) + (st["iters"] if st.get("gemv") is not None else 0)
    streams = [st for st in PLAN if st["shapes"]]
    for st, following in zip(streams, streams[1:] + [None]):
        st["following"] = following
    totals = Counts()
    for st in PLAN:
        st["base"] = Counts()
        st["base"].add(totals.at)
        totals.add(st["totals"])

    base = (nc.sbuf_base + 63) // 64 * 64
    place = [0]

    def sb(name, shape, dt=F32, at=None):
        size = 4 * int(np.prod(shape[1:]))
        off = place[0] if at is None else at
        if at is None:
            place[0] += -(-size // 32) * 32
        assert base + off + size <= nc.sbuf_usable_end, (name, base + off + size, nc.sbuf_usable_end)
        return nc.alloc_sbuf_tensor_at(name, shape, dt, offset=base + off)

    x = sb("x", [P, KD * S])
    hc = sb("hc", [P, KD * C])
    h_hi = sb("h_hi", [P, KD * S], F32R)
    h_lo = sb("h_lo", [P, KD * S], F32R)
    raw = sb("raw", [P, 2, 2048])
    w_hi = sb("w_hi", [P, 2, 2048], F32R)
    w_lo = sb("w_lo", [P, 2, 2048], F32R)
    g_raw = sb("g_raw", [P, 2, KD, GP])
    acc = sb("acc", [P, 2, GP])
    hid = place[0]
    hid_hi = sb("hid_hi", [P, 12 * S], F32R)
    hid_lo = sb("hid_lo", [P, 12 * S], F32R)
    tmp = place[0]
    gate_t = sb("gate_t", [P, 2, S])
    prod_t = sb("prod_t", [P, 2, S])
    squares = sb("squares", [P, 4, S], at=tmp)
    unit_t = sb("unit_t", [P, 2, S])
    full_t = sb("full_t", [P, 2, S])
    rstd = sb("rstd", [P, S])
    modc = sb("modc", [P, MOD_COLS])
    colv = sb("colv", [P, row_tiles * P])
    c_col = sb("c_col", [P, 3 * KD])
    ident = sb("ident", [P, P])
    mean_m = sb("mean_m", [P, P])
    ones = sb("ones", [P, 1])
    eps = sb("eps", [P, 2])
    spare = place[0]
    row_in = sb("row_in", [P, row_tiles, P], at=hid)
    x_rows = sb("x_rows", [P, 4, D], at=hid + 4096)
    c_rows = sb("c_rows", [P, 2, D], at=hid + 4096 + 16384)
    x_out = sb("x_out", [P, 4, D], at=hid)
    mq = sb("mq", [P, 4, S], at=hid)
    mk = sb("mk", [P, S], at=hid + 8192)
    mv = sb("mv", [P, 4, P], at=hid + 10240)
    lx = sb("lx", [P, 2, S], at=hid + 12288)
    lg = sb("lg", [P, 2, S], at=hid + 16384)
    sbt = sb("sbt", [P, 2, S], at=hid + 20480)
    sct = sb("sct", [P, 2, S], at=hid + 24576)
    sxt = sb("sxt", [P, 2, S], at=hid + 28672)
    alibi = sb("alibi", [P, NQ, 2 * P], at=hid + 32768)
    att = sb("att", [P, 2, 4, 2 * P], at=hid + 40960)
    att_t = sb("att_t", [P, 2, 8, P], at=spare)
    cx = sb("cx", [P, 2, S], at=tmp)
    ga = sb("ga", [P, 2, S], at=tmp + 4096)
    gx = sb("gx", [P, 2, S], at=tmp + 8192)
    lt = sb("lt", [P, 2, S], at=tmp + 12288)
    gate_w = sb("gate_w", [P, 2, 2, P], at=spare + 8192)
    small = sb("small", [P, 256], at=spare + 10240)
    sinks = small[:, 0:NQ]
    lsp = small[:, 16:16 + 4 * 2]
    sm = lambda k, n=4: small[:, 32 + 4 * k:32 + 4 * k + n]

    low_hi = sb("low_hi", [P, 5, T], F32R, at=hid + 16384)
    low_lo = sb("low_lo", [P, 5, T], F32R, at=hid + 16384 + 15360)
    g_raw_at, h_at = 16384 + 8192 + 32768 + 16384 + 32768, 16384 + 8192
    ch_hi = sb("ch_hi", [P, KD * C], F32R, at=hid)
    ch_lo = sb("ch_lo", [P, KD * C], F32R, at=hid + 8192)
    low = sb("low", [P, 5, T], at=g_raw_at)
    low_pe = sb("low_pe", [P, T], at=tmp)
    low_squares = sb("low_squares", [P, 3, T], at=spare)
    low_rstd = sb("low_rstd", [P, T], at=spare + 9216)
    q_flat = sb("q_flat", [P, PER, S], at=h_at)
    q_turn = sb("q_turn", [P, PER, S], at=h_at + 8192)
    q_ctx = sb("q_ctx", [P, PER, C], at=h_at + 16384)
    keys = sb("keys", [P, PER, T], at=h_at + 20480)
    vals = sb("vals", [P, 6, PER * HD], at=g_raw_at)
    diag = sb("diag", [P, 2, P], at=g_raw_at + 9216)
    prob_t = sb("prob_t", [P, 2, T], at=spare)
    prob = sb("prob", [P, 2, T], at=spare + 6144)
    o_lat = sb("o_lat", [P, KD, S], at=hid)
    o_ctx = sb("o_ctx", [P, KD, C], at=tmp)
    oc_hi = sb("oc_hi", [P, KD * C], F32R, at=hid + 16384)
    oc_lo = sb("oc_lo", [P, KD * C], F32R, at=hid + 16384 + 8192)
    turns = sb("turns", [P, 2, S], at=tmp + 8192)
    turned = sb("turned", [P, S], at=tmp + 12288)
    turn_m = sb("turn_m", [P, DQ], at=spare + 12288)
    stat = sb("stat", [P, 96], at=spare + 12288 + 384)
    nq = sb("nq", [P, 2, S], at=g_raw_at)
    nk = sb("nk", [P, 2, T], at=g_raw_at + 4096)
    nv = sb("nv", [P, 6, PER * HD], at=spare)
    nvb = sb("nvb", [P, 4, 2, PER * HD], at=tmp + 4096)
    on_lat = sb("on_lat", [P, KD, S], at=hid + 16384)
    prob_n = sb("prob_n", [P, 2, S], at=hid + 32768)
    bias_m = sb("bias_m", [P, 4, ROWS, KC_], at=hid + 36864)
    prob_nt = sb("prob_nt", [P, 2, S], at=hid + 40960)
    diag_n = sb("diag_n", [P, 2, P], at=hid + 45056)
    bias_w = sb("bias_w", [P, 2, ROWS, WIDE], at=tmp)
    na_mask = sb("na_mask", [P, 3, KC_], at=tmp + 3072)
    table = sb("table", [8 * 15, 2, 64], at=spare)
    wide = nc.dram_tensor("bias_rows", [QC, NH * 15 * WIDE], F32, kind="Internal").ap()

    ps_all = nc.alloc_psum_tensor("ps_all", [P, 8, S], F32)
    ps_g, ps_u, ps_d = ps_all[:, 0:2, :], ps_all[:, 2:4, :], ps_all[:, 4:6, :]
    ps_mod, ps_s = ps_all[:, 6, :], ps_all[:, 7, :]

    names = sorted(set(totals.at) | {"raw_in0", "raw_in1", "w_split_hi", "w_split_lo", "panel_used",
                                     "gemv_in0", "gemv_in1", "gemv_done", "gemv_reduced", "rows_in", "const_in", "x_rows_in",
                                     "consts", "act_chain", "dve_chain", "pool_chain", "stored", "table_in", "table_zero", "table_scaled", "wide_in"})
    sem = {n: nc.alloc_semaphore(n) for n in names}

    def src(st):
        return (hc, C) if st["ctx"] else (x, S)

    def dst_of(st):
        return (ch_hi, ch_lo) if st["dst"] == "ch" else (h_hi, h_lo)

    def view(buf, nk, n):
        return buf.rearrange("p (k n) -> p k n", n=n)

    def w_view(t, slot, shape):
        nk, n = shape
        return t[:, slot, 0:nk * n].rearrange("p (k n) -> p k n", n=n)

    def ahead(st, i, j, last):
        per = len(st["shapes"])
        if j + 2 < per:
            return st, i, j + 2
        if not last:
            return st, i + 1, j + 2 - per
        f = st["following"]
        return (f, 0, j + 2 - per) if f is not None else None

    def number(st, i, j):
        return st["p0"] + i * len(st["shapes"]) + j

    def raw_need(st, i, j):
        per = 16 * sum(st["n_dma"][j % 2::2])
        upto = 16 * sum(st["n_dma"][j % 2:j + 1:2])
        return st["raw0"][j % 2] + i * per + upto

    block_cm = nc.Block()
    block = block_cm.__enter__()

    @block.sync
    def _(sp):
        def load_panel(st, i, j):
            parts = st["dma"](i, j)
            if not (st["p0"] == 0 and isinstance(i, int) and i == 0 and j < 2):
                sp.wait_ge(sem["w_split_lo"], number(st, i, j) - 1)
            for where, ap in parts:
                dst = w_view(raw, j % 2, st["shapes"][j])
                if where and where[0] == "cols":
                    dst = dst[:, :, where[1]:where[1] + where[2]]
                elif where and where[0] == "k":
                    dst = dst[where[3]:where[4], where[1]:where[2], :]
                sp.dma_start(dst, ap).then_inc(sem[f"raw_in{j % 2}"], 16)

        def gemv_ap(g, i=0):
            if g < G_ADA:
                l, w = g // MOD_PANELS, a["w_mod"]
                off = (g % MOD_PANELS) * GP
            else:
                l, w = (g - G_ADA) // ADA_PANELS, a["ada_w_2"]
                off = ((g - G_ADA) % ADA_PANELS) * GP
            return weight_panels(w[l])[:, :, ds(off + i * GP, GP)]

        for t in range(row_tiles):
            for name, ap in rows:
                lo, hi = max(col[name], t * P), min(col[name] + ap.shape[0], (t + 1) * P)
                if lo < hi:
                    sp.dma_start(row_in[lo - t * P:hi - t * P, t, :], ap[lo - col[name]:hi - col[name], :]).then_inc(sem["rows_in"], 16)
        sp.dma_start(ident[:, :], a["k_ident"]).then_inc(sem["const_in"], 16)
        sp.dma_start(x_rows[:, :, :], a["x"][0].rearrange("(t p) n -> p t n", p=P)).then_inc(sem["x_rows_in"], 16)
        sp.dma_start(c_rows[:, :, :], a["ctx_2"][0].rearrange("(t p) n -> p t n", p=P)).then_inc(sem["x_rows_in"], 16)
        sp.wait_ge(sem["table_zero"], 1)
        for t in range(2):
            sp.dma_start(table[:, t, 16:47], a["na_rpb_2"][0].rearrange("h m n -> (h m) n")[t * 120:(t + 1) * 120, :]).then_inc(sem["table_in"], 16)
        sp.wait_ge(sem["table_scaled"], 1)
        for t in range(2):
            for q in range(QC):
                sp.dma_start(wide[q, t * 120 * WIDE:(t + 1) * 120 * WIDE].rearrange("(m n) -> m n", n=WIDE), table[:, t, 15 - q:15 - q + WIDE]).then_inc(sem["wide_in"], 16)
        early = None
        for st in PLAN:
            b = st["base"]
            if st["kind"] == "prologue":
                for n, g in enumerate(st["gemvs"]):
                    if g >= 1:
                        sp.wait_ge(sem["gemv_done"], max(g - 1, 0) if n else g)
                    sp.dma_start(g_raw[:, n % 2, :, :], gemv_ap(g)).then_inc(sem[f"gemv_in{n % 2}"], 16)
            elif st["kind"] == "mixer":
                l = st["l"]
                sp.wait_ge(sem["down1"], b["down1"])
                sp.dma_start(alibi[:, :, :], a["k_alibi"]).then_inc(sem["misc_in"], 16)
                sp.dma_start(sinks, a["attn_sinks"][l:l + 1, :].broadcast_to([P, NQ])).then_inc(sem["misc_in"], 16)
                for m, name in enumerate(("lru_gate_a_w", "lru_gate_x_w")):
                    for h in range(4):
                        q = HD * (h % 2)
                        sp.wait_ge(sem["consts"], 5)
                        if l:
                            sp.wait_ge(sem["gates_i"], b["gates_i"])
                        sp.dma_start(gate_w[q:q + HD, m, h // 2, q:q + HD], a[name][l, h]).then_inc(sem["misc_in"], 16)
                for n in range(max(8, len(st["gemvs"]) + 2)):
                    if n < 8:
                        load_panel(st, 0, n)
                    if 2 <= n < len(st["gemvs"]) + 2:
                        g = st["gemvs"][n - 2]
                        sp.wait_ge(sem["gemv_done"], g)
                        sp.dma_start(g_raw[:, 0, :, :], gemv_ap(g)).then_inc(sem["gemv_in0"], 16)
            elif st["kind"] == "mla_in":
                load_panel(st, 0, 0)
                load_panel(st, 0, 1)
                sp.wait_ge(sem["h_ready"], b["h_ready"])
                sp.dma_start(turns[64:96, 0, :], a["k_rope"][0]).then_inc(sem["rope_in"], 16)
                sp.dma_start(turns[64:96, 1, :], a["k_rope"][1]).then_inc(sem["rope_in"], 16)
                sp.dma_start(turn_m[0:DQ, :], a["k_turn"]).then_inc(sem["rope_in"], 16)
                for j in (2, 3):
                    load_panel(st, 0, j)
            elif st["kind"] == "na":
                load_panel(st, 0, 0)
                load_panel(st, 0, 1)
                sp.wait_ge(sem["h_ready"], b["h_ready"])
                sp.wait_ge(sem["wide_in"], 16 * 2 * QC)
                sp.dma_start(na_mask[:, :, :], a["k_na_mask"]).then_inc(sem["na_mask"], 16)

                def biases(i, h, first):
                    of_row = lambda row: wide[:, ds((h * 15 + 7 - row) * WIDE + i * (PER * 15 * WIDE), ROWS * WIDE)]
                    source = of_row(0)
                    if h >= 2 or not first:
                        sp.wait_ge(sem["bias_made"], b["bias_made"] + (i * PER + h - 1) * 4)
                    for row in range(ROWS):
                        dst = bias_w[row * QC:(row + 1) * QC, h % 2, :, :].rearrange("q m n -> q (m n)")
                        sp.dma_start(dst, source if row == 0 else of_row(row)).then_inc(sem[f"bias_in{h % 2}"], 16)

                def one(i, first, last):
                    load_panel(st, i, 2)
                    load_panel(st, i, 3)
                    for h in (0, 1):
                        biases(i, h, first)
                    for j in range(2):
                        load_panel(st["following"] if last else st, 0 if last else i + 1, j)
                    sp.wait_ge(sem["n_out"], b["n_out"] + i + 1)
                    for j in range(4):
                        for row in range(ROWS):
                            p0, q0 = (row % 4) * KC_, (row % 2) * GRID + BAND[j]
                            sp.dma_start(nvb[p0:p0 + KC_, j, row // 4, :], nv[q0:q0 + KC_, 2 + row // 2, :]).then_inc(sem["band_in"], 16)
                    for h in (2, 3):
                        biases(i, h, first)
                one(0, True, False)
                with sp.Fori(1, st["iters"] - 1) as i:
                    one(i, False, False)
                one(st["iters"] - 1, False, True)
                early = st["following"]
            elif st["shapes"] and st["kind"] in ("gu", "dn", "proj", "mla"):
                def one(i, g, loaded=False):
                    for j in range(0 if loaded else len(st["shapes"])):
                        load_panel(st, i, j)
                    if g is not None:
                        sp.wait_ge(sem["gemv_done"], g + i)
                        sp.dma_start(g_raw[:, 0, :, :], gemv_ap(g, i)).then_inc(sem["gemv_in0"], 16)
                start = 0
                if st["p0"] == 0 or st is early:
                    one(0, st.get("gemv"), st is early)
                    start = 1
                with sp.Fori(start, st["iters"]) as i:
                    one(i, st.get("gemv"))
        b = PLAN[-1]["base"]
        for t in range(4):
            sp.wait_ge(sem["o_out"], b["o_out"] + t + 1)
            sp.dma_start(out[0].rearrange("(t p) n -> p t n", p=P)[:, t, :], x_out[:, t, :]).then_inc(sem["stored"], 16)
        sp.wait_ge(sem["stored"], 64)
        sp.wait_ge(sem["wide_in"], 16 * 2 * QC)

    @block.gpsimd
    def _(pool):
        pool.memset(mean_m[:, :], 1.0 / D).then_inc(sem["consts"], 1)
        pool.memset(ones[:, :], 1.0).then_inc(sem["consts"], 1)
        pool.memset(eps[:, 0:1], EPS_RMS).then_inc(sem["consts"], 1)
        pool.memset(eps[:, 1:2], EPS_LN).then_inc(sem["consts"], 1)
        pool.memset(gate_w[:, :, :, :], 0.0).then_inc(sem["consts"], 1)
        pool.memset(table[:, :, :], 0.0).then_inc(sem["table_zero"], 1)

        def split_lo(target):
            if target is None:
                return
            st, i, j = target
            pool.wait_ge(sem["w_split_hi"], number(st, i, j) + 1)
            v = lambda t: w_view(t, j % 2, st["shapes"][j])
            nc.gpsimd.tensor_tensor(v(w_lo), v(raw), v(w_hi).bitcast(F32), ALU.subtract).then_inc(sem["w_split_lo"], 1)

        def h_low(b, n, k, N, full, to):
            hi, lo = to
            pool.wait_ge(sem["h_hi"], b["h_hi"] + n + 1)
            nc.gpsimd.tensor_tensor(lo[:, k * N:(k + 1) * N], full, hi[:, k * N:(k + 1) * N].bitcast(F32),
                                    ALU.subtract).then_inc(sem["h_ready"], 1)

        pool.wait_ge(sem["table_in"], 32)
        nc.gpsimd.tensor_scalar(table[:, :, :], table[:, :, :], HD ** 0.5, None, ALU.mult).then_inc(sem["table_scaled"], 1)
        split_lo((streams[0], 0, 0))
        split_lo((streams[0], 0, 1))
        for st in PLAN:
            b = st["base"]
            if st["kind"] == "norm" and "h_ready" in st["totals"]:
                for k in range(KD):
                    h_low(b, k, k, st["N"], full_t[:, k % 2, 0:st["N"]], dst_of(st))
            elif st["kind"] == "mixer":
                for j in range(6):
                    split_lo(ahead(st, 0, j, True))
                order = [(4, lt[:, 0, :]), (5, lt[:, 1, :]), (6, sxt[:, 0, :]), (7, sxt[:, 1, :])] + [(i, mq[:, i, :]) for i in range(4)]
                for j in (6, 7):
                    split_lo(ahead(st, 0, j, True))
                for n, (k, full) in enumerate(order):
                    h_low(b, n, k, S, full, (h_hi, h_lo))
            elif st["kind"] == "gather":
                for k in range(KD):
                    h_low(b, k, k, S, (o_lat if st["ctx"] else on_lat)[:, k, :], (h_hi, h_lo))
                if st["ctx"]:
                    for k in range(KD):
                        h_low(b, KD + k, k, C, o_ctx[:, k, :], (oc_hi, oc_lo))
            elif st["kind"] == "mla_in":
                for j in range(4):
                    split_lo(ahead(st, 0, j, True))
                for k in range(5):
                    pool.wait_ge(sem["low_hi"], b["low_hi"] + k + 1)
                    nc.gpsimd.tensor_tensor(low_lo[:, k, :], low[:, k, :], low_hi[:, k, :].bitcast(F32), ALU.subtract).then_inc(sem["low_lo"], 1)
            elif st["kind"] == "na":
                pool.wait_ge(sem["na_mask"], 16)

                def one(i, last):
                    for j in range(4):
                        split_lo(ahead(st, i, j, last))
                        h = j
                        pool.wait_ge(sem[f"bias_in{h % 2}"], b[f"bias_in{h % 2}"] + (i * (PER // 2) + h // 2 + 1) * (16 * ROWS))
                        for u in range(4):
                            kind_j = (0, 1, 1, 2)[u]
                            x0 = BAND[u] - u * QC + QC
                            if not (isinstance(i, int) and i * PER + h < 1):
                                pool.wait_ge(sem["s_biased"], b["s_biased"] + i * (4 * PER) + h * 4 + u - 3)
                            nc.gpsimd.tensor_tensor(bias_m[:, u, :, :], bias_w[:, h % 2, :, x0:x0 + KC_],
                                                    na_mask[:, kind_j, :].rearrange("p (o n) -> p o n", o=1).broadcast_to([P, ROWS, KC_]),
                                                    ALU.add).then_inc(sem["bias_made"], 1)
                one(0, False)
                with pool.Fori(1, st["iters"] - 1) as i:
                    one(i, False)
                one(st["iters"] - 1, True)
            elif st["kind"] in ("gu", "dn", "proj", "mla"):
                def one(i, last):
                    for j in range(len(st["shapes"])):
                        split_lo(ahead(st, i, j, last))
                Chain(pool, sem["pool_chain"]).loop(st["iters"], 0, one)

    def mixer_act(st, b, act, split_hi):
        l = st["l"]
        dest = [lx[:, :, :], lg[:, :, :], sct[:, :, :], sxt[:, :, :], sbt[:, :, :], None, mq[:, 0:2, :], mq[:, 2:4, :]]

        def evac(j):
            act.wait_ge(sem["panel_used"], st["p0"] + j + 1)
            pair = (ps_g, ps_u)[j % 2]
            if j == 5:
                nc.scalar.activation(mk[:, :], pair[:, 0, :], ACT.Copy)
                nc.scalar.activation(mv[:, :, :].rearrange("p a b -> p (a b)"), pair[:, 1, :], ACT.Copy).then_inc(sem["in_evac"], 1)
            else:
                nc.scalar.activation(dest[j], pair[:, :, :], ACT.Copy).then_inc(sem["in_evac"], 1)
            split_hi(ahead(st, 0, j, True))

        act.wait_ge(sem["lam_in"], b["lam_in"] + 1)
        nc.scalar.activation(sm(14, 2), sm(17, 2), ACT.Exp).then_inc(sem["lam_exp"], 1)
        evac(0)
        evac(1)
        evac(2)
        bc = lambda name, c: colv[:, col[name] + l * 2 + c:col[name] + l * 2 + c + 1]
        for c in range(2):
            act.wait_ge(sem["gates_mm"], b["gates_mm"] + 1)
            nc.scalar.activation(ga[:, c, :], ps_d[:, c, :], ACT.Sigmoid, bias=bc("gate_a_b", c)).then_inc(sem["gates_r"], 1)
        evac(3)
        evac(4)
        for c in range(2):
            act.wait_ge(sem["gates_mm"], b["gates_mm"] + 2)
            nc.scalar.activation(gx[:, c, :], ps_d[:, c, :], ACT.Sigmoid, bias=bc("gate_x_b", c)).then_inc(sem["gates_i"], 1)
        act.wait_ge(sem["lru_q"], b["lru_q"] + 1)
        act.wait_ge(sem["gates_r"], b["gates_r"] + 2)
        for c in range(2):
            ins = nc.scalar.activation(lt[:, c, :], ga[:, c, :], ACT.Tanh, scale=lsp[:, c:c + 1])
        ins.then_inc(sem["lru_t"], 1)
        act.wait_ge(sem["lru_t"], b["lru_t"] + 1)
        evac(5)
        for c in range(2):
            ins = nc.scalar.activation(ga[:, c, :], ga[:, c, :], ACT.Exp, scale=lsp[:, 4 + c:5 + c])
        ins.then_inc(sem["act_chain"], 1)
        evac(6)
        evac(7)
        act.wait_ge(sem["lru_m"], b["lru_m"] + 1)
        nc.scalar.activation(lt[:, :, :], lt[:, :, :], ACT.Sqrt, scale=2.0)
        nc.scalar.activation(lg[:, :, :], lg[:, :, :], ACT.Gelu_apprx_tanh).then_inc(sem["gelu"], 1)

        def high(n, k, full):
            nc.scalar.activation(h_hi[:, k * S:(k + 1) * S], full, ACT.Copy).then_inc(sem["h_hi"], 1)

        act.wait_ge(sem["y_lru"], b["y_lru"] + 1)
        high(0, 4, lt[:, 0, :])
        high(1, 5, lt[:, 1, :])
        act.wait_ge(sem["y_sc"], b["y_sc"] + 1)
        high(2, 6, sxt[:, 0, :])
        high(3, 7, sxt[:, 1, :])
        for h in range(NQ):
            q = h % 2
            act.wait_ge(sem["at_sub"], b["at_sub"] + h + 1)
            nc.scalar.activation(sm(h % 2 * 6 + 2), sm(h % 2 * 6 + 1), ACT.Exp, bias=sinks_col(h))
            nc.scalar.activation(att[:, q, :, :], att[:, q, :, :], ACT.Exp).then_inc(sem["at_exp"], 1)
            if h >= 1:
                pt_copy(act, b, h - 1)
        pt_copy(act, b, NQ - 1)

    def sinks_col(h):
        head = h // 2 + 4 * (h % 2)
        return sinks[:, head:head + 1]

    def pt_copy(act, b, h):
        act.wait_ge(sem["at_t"], b["at_t"] + h + 1)
        if h >= 2:
            act.wait_ge(sem["at_o"], b["at_o"] + h - 1)
        nc.scalar.activation(att_t[:, h % 2, :, :], ps_d[:, :, :].rearrange("p c (j q) -> p (c j) q", q=P), ACT.Copy).then_inc(sem["at_pt"], 1)
        if h % 2 == 1:
            i = h // 2
            act.wait_ge(sem["at_o"], b["at_o"] + 2 * i + 2)
            nc.scalar.activation(mq[:, i, :], ps_s[:, :], ACT.Copy).then_inc(sem["y_at"], 1)
            act.wait_ge(sem["y_at"], b["y_at"] + i + 1)
            nc.scalar.activation(h_hi[:, i * S:(i + 1) * S], mq[:, i, :], ACT.Copy).then_inc(sem["h_hi"], 1)

    def mla_in_act(st, b, act, split_hi):
        def evac(k, bank, cbank, c):
            nc.scalar.activation(low[:, k, C:T], bank, ACT.Copy)
            return nc.scalar.activation(low[:, k, 0:C], cbank[:, c * C:(c + 1) * C], ACT.Copy)

        places = [[(0, ps_g[:, 0, :], 0), (1, ps_g[:, 1, :], 1)], [(2, ps_u[:, 0, :], 0), (3, ps_u[:, 1, :], 1)], [(4, ps_g[:, 0, :], 0)]]
        for j in range(3):
            act.wait_ge(sem["panel_used"], st["p0"] + j + 1)
            for k, bank, c in places[j]:
                ins = evac(k, bank, ps_d[:, j % 2, :], c)
            ins.then_inc(sem["low_out"], 1)
            split_hi(ahead(st, 0, j, True))
        act.wait_ge(sem["panel_used"], st["p0"] + 4)
        act.wait_ge(sem["rope_in"], 48)
        nc.scalar.activation(low_pe[64:96, C:T], ps_u[64:96, 0, :], ACT.Copy)
        nc.scalar.activation(low_pe[64:96, 0:C], ps_d[64:96, 1, 0:C], ACT.Copy).then_inc(sem["low_out"], 1)
        split_hi(ahead(st, 0, 3, True))
        act.wait_ge(sem["low_out"], b["low_out"] + 4)
        for n, (k0, k1, width) in enumerate(((0, 3, LQ), (3, 5, LKV))):
            if n:
                act.wait_ge(sem["low_sum"], b["low_sum"] + n)
            for k in range(k0, k1):
                nc.scalar.activation(low_squares[:, k - k0, :], low[:, k, :], ACT.Square).then_inc(sem["low_sq"], 1)
            act.wait_ge(sem["low_sum"], b["low_sum"] + n + 1)
            if n:
                act.wait_ge(sem["low_full"], b["low_full"] + 3)
            for o, i_ in ((low_rstd[:, C:T], ps_g[:, 1, :]), (low_rstd[:, 0:C], ps_s[:, 0:C])):
                ins = nc.scalar.activation(o, i_, ACT.Sqrt, scale=float(D) / width, bias=eps[:, 0:1])
            ins.then_inc(sem["low_dev"], 1)
            for k in range(k0, k1):
                act.wait_ge(sem["low_full"], b["low_full"] + k + 1)
                nc.scalar.activation(low_hi[:, k, :], low[:, k, :], ACT.Copy).then_inc(sem["low_hi"], 1)
        for h in range(PER):
            ins = nc.scalar.activation(keys[64:96, h, 0:C], low_pe[64:96, 0:C], ACT.Copy)
        ins.then_inc(sem["act_chain"], 1)

    MLA_UNITS = [(h, ctx, q) for h in range(PER) for ctx, n in ((0, 4), (1, 2)) for q in range(n)]
    MLA_LAT = [sum(1 for u in MLA_UNITS[:n] if not u[1]) for n in range(len(MLA_UNITS))]

    def mla_act(st, b, act, split_hi, i, last):
        base_of = lambda name, per: b[name] + i * per
        U = len(MLA_UNITS)
        act.wait_ge(sem["panel_used"], st["p0"] + i * 2 + 1)
        for h in range(PER):
            nc.scalar.activation(q_flat[0:DQ, h, :], ps_all[0:DQ, h, :], ACT.Copy)
            nc.scalar.activation(q_turn[0:NOPE, h, :], ps_all[0:NOPE, h, :], ACT.Copy)
        for h in range(PER):
            ins = nc.scalar.activation(q_ctx[0:DQ, h, :], ps_d[0:DQ, h // 2, (h % 2) * C:(h % 2 + 1) * C], ACT.Copy)
        ins.then_inc(sem["head_out"], 1)
        split_hi(ahead(st, i, 0, last))
        act.wait_ge(sem["head_mm"], base_of("head_mm", 3) + 2)
        for h in range(PER):
            ins = nc.scalar.activation(keys[0:NOPE, h, C:T], ps_all[0:NOPE, 4 + h, :], ACT.Copy)
        ins.then_inc(sem["head_out"], 1)
        act.wait_ge(sem["head_mm"], base_of("head_mm", 3) + 3)
        for h in range(PER):
            nc.scalar.activation(keys[0:NOPE, h, 0:C], ps_g[0:NOPE, h // 2, (h % 2) * C:(h % 2 + 1) * C], ACT.Copy)
        for t in (0, 2, 4):
            if t == 4:
                act.wait_ge(sem["panel_used"], st["p0"] + i * 2 + 2)
            ins = nc.scalar.activation(vals[:, t:t + 2, :], ps_all[:, (2, 3, 4)[t // 2], :].rearrange("p (t n) -> p t n", t=2), ACT.Copy)
        ins.then_inc(sem["head_out"], 1)
        split_hi(ahead(st, i, 1, last))

        def exps(n):
            h, ctx, q = MLA_UNITS[n]
            act.wait_ge(sem["s_max"], base_of("s_max", U) + n + 1)
            if n >= 2:
                act.wait_ge(sem["turned0"], base_of("turned0", U) + n - 1)
                if not MLA_UNITS[n - 2][1]:
                    act.wait_ge(sem["turned1"], base_of("turned1", 4 * PER) + MLA_LAT[n - 2] + 1)
            pair = ps_all[:, 2 * (n % 2):2 * (n % 2) + 2, :].rearrange("p b n -> p (b n)")
            W = C if ctx else T
            nc.scalar.activation(prob[:, n % 2, 0:W], pair[:, C:C + W], ACT.Exp, scale=DQ ** -0.5,
                                 bias=stat[:, 4 * (n % 2) + 1:4 * (n % 2) + 2], accum_out=stat[:, 4 * (n % 2) + 2:4 * (n % 2) + 3]).then_inc(sem["s_exp"], 1)

        def copy(n):
            h, ctx, q = MLA_UNITS[n]
            act.wait_ge(sem["turned0"], base_of("turned0", U) + n + 1)
            if n >= 2:
                act.wait_ge(sem["s_weighted"], base_of("s_weighted", U) + n - 1)
            W = (2 if ctx else 3) * P
            nc.scalar.activation(prob_t[:, n % 2, 0:W], ps_all[:, 4, 0:W], ACT.Copy).then_inc(sem["copied0"], 1)

        def keep(n):
            h, ctx, q = MLA_UNITS[n]
            act.wait_ge(sem["s_weighted"], base_of("s_weighted", U) + n + 1)
            N, to = (C, o_ctx) if ctx else (S, o_lat)
            nc.scalar.activation(to.rearrange("p k n -> p (k n)")[:, ds(i * (2 * N) + (h // 2) * N, N)], ps_all[:, 6 + ctx, 0:N], ACT.Copy).then_inc(sem["s_kept"], 1)

        exps(0)
        for n in range(U):
            if n + 1 < U:
                exps(n + 1)
            copy(n)
            if n >= 2 and MLA_UNITS[n - 2][0] % 2 and MLA_UNITS[n - 2][1:] in ((0, 3), (1, 1)):
                keep(n - 2)
        keep(U - 1)

    NA_UNITS = [(h, j) for h in range(PER) for j in range(4)]

    def na_act(st, b, act, split_hi, i, last):
        base_of = lambda name, per: b[name] + i * per
        U = len(NA_UNITS)
        act.wait_ge(sem["panel_used"], st["p0"] + i * 4 + 2)
        for c in range(2):
            nc.scalar.activation(nq[:, c, :].rearrange("p (j r q) -> p r j q", j=GRID // QC, q=QC),
                                 ps_g[:, c, :].rearrange("p (r j q) -> p r j q", j=GRID // QC, q=QC), ACT.Copy)
        split_hi(ahead(st, i, 0, last))
        nc.scalar.activation(nk[:, :, C:T], ps_u, ACT.Copy)
        nc.scalar.activation(nk[:, :, 0:C], ps_all[:, 4, :].rearrange("p (c n) -> p c n", c=2), ACT.Copy).then_inc(sem["n_out_q"], 1)
        split_hi(ahead(st, i, 1, last))
        act.wait_ge(sem["panel_used"], st["p0"] + i * 4 + 4)
        for t in (0, 2, 4):
            ins = nc.scalar.activation(nv[:, t:t + 2, :], ps_all[:, 5 + t // 2, :].rearrange("p (t n) -> p t n", t=2), ACT.Copy)
        ins.then_inc(sem["n_out"], 1)
        split_hi(ahead(st, i, 2, last))
        split_hi(ahead(st, i, 3, last))

        def exps(n):
            act.wait_ge(sem["s_max"], base_of("s_max", U) + n + 1)
            if n >= 2:
                act.wait_ge(sem["turned1"], base_of("turned1", U) + n - 1)
            nc.scalar.activation(prob_n[:, n % 2, :], ps_all[:, n % 4, :], ACT.Exp, scale=HD ** -0.5,
                                 bias=stat[:, 4 * (n % 4) + 1:4 * (n % 4) + 2], accum_out=stat[:, 4 * (n % 4) + 2:4 * (n % 4) + 3]).then_inc(sem["s_exp"], 1)

        def copy(n):
            act.wait_ge(sem["turned0"], base_of("turned0", U) + n + 1)
            if n >= 2:
                act.wait_ge(sem["s_weighted"], base_of("s_weighted", U) + n - 1)
            nc.scalar.activation(prob_nt[:, n % 2, 0:C], ps_all[:, 4, 0:C], ACT.Copy).then_inc(sem["copied0"], 1)

        def keep(n):
            h, j = NA_UNITS[n]
            act.wait_ge(sem["s_weighted"], base_of("s_weighted", U) + n + 1)
            to = on_lat.rearrange("p k n -> p (k n)")[:, ds(i * (2 * S) + (h // 2) * S, S)]
            nc.scalar.activation(to.rearrange("p (r j q) -> p r j q", j=GRID // QC, q=QC),
                                 ps_all[:, 6 + h // 2, :].rearrange("p (j r q) -> p r j q", j=GRID // QC, q=QC), ACT.Copy).then_inc(sem["s_kept"], 1)

        exps(0)
        for n in range(U):
            if n + 1 < U:
                exps(n + 1)
            copy(n)
            if n >= 2 and NA_UNITS[n - 2] == (1, 3):
                keep(n - 2)
        keep(U - 1)

    @block.scalar
    def _(act):
        ch = Chain(act, sem["act_chain"])

        def split_hi(target):
            if target is None:
                return
            st, i, j = target
            act.wait_ge(sem[f"raw_in{j % 2}"], raw_need(st, i, j))
            if not (st["p0"] == 0 and isinstance(i, int) and i == 0 and j < 2):
                act.wait_ge(sem["panel_used"], number(st, i, j) - 1)
            nc.scalar.activation(w_view(w_hi, j % 2, st["shapes"][j]), w_view(raw, j % 2, st["shapes"][j]),
                                 ACT.Copy).then_inc(sem["w_split_hi"], 1)

        for st in PLAN:
            b = st["base"]
            if st["kind"] == "load":
                for t in range(row_tiles):
                    act.wait_ge(sem["row_tile"], t + 1)
                    n = min(P, n_rows - t * P)
                    nc.scalar.activation(colv[:, t * P:t * P + n], ps_d[:, t % 2, 0:n], ACT.Copy).then_inc(sem["row_col"], 1)
                act.wait_ge(sem["row_col"], row_tiles)
                nc.scalar.activation(c_col[:, :], colv[:, 0:3 * KD], ACT.Silu).then_inc(sem["c_act"], 1)
                for k in range(KD):
                    act.wait_ge(sem["x_tr"], k + 1)
                    nc.scalar.activation(x[:, k * S:(k + 1) * S], ps_g[:, k % 2, :], ACT.Copy).then_inc(sem["x_in"], 1)
                for k in range(KD):
                    act.wait_ge(sem["hc_tr"], k + 1)
                    nc.scalar.activation(hc[:, k * C:(k + 1) * C], ps_u[:, k % 2, 0:C], ACT.Copy).then_inc(sem["hc_in"], 1)
                split_hi((streams[0], 0, 0))
                split_hi((streams[0], 0, 1))
            elif st["kind"] == "norm":
                buf, N = src(st)
                if st["mode"] != "mod_h":
                    for n in ("x_in", "down0", "down1", "proj0", "proj1", "x_new"):
                        if b[n] and st["mode"] != "ln_x":
                            act.wait_ge(sem[n], b[n])
                    for k in range(KD):
                        if st["mode"] == "ln_x":
                            act.wait_ge(sem["centred"], b["centred"] + k + 1)
                        if k >= 4:
                            act.wait_ge(sem["square_summed"], b["square_summed"] + k - 3)
                        nc.scalar.activation(squares[:, k % 4, 0:N], buf[:, k * N:(k + 1) * N], ACT.Square).then_inc(sem["squared"], 1)
                    act.wait_ge(sem["square_summed"], b["square_summed"] + KD)
                    e = eps[:, 1:2] if st["mode"] == "ln_x" else eps[:, 0:1]
                    act.wait_ge(sem["consts"], 5)
                    nc.scalar.activation(rstd[:, 0:N], ps_s[:, 0:N], ACT.Sqrt, bias=e).then_inc(sem["deviation"], 1)
                if "h_hi" in st["totals"]:
                    for k in range(KD):
                        act.wait_ge(sem["h_full"], b["h_full"] + k + 1)
                        nc.scalar.activation(dst_of(st)[0][:, k * N:(k + 1) * N], full_t[:, k % 2, 0:N], ACT.Copy).then_inc(sem["h_hi"], 1)
            elif st["kind"] == "gu":
                N = st["N"]
                p0, g0, pr, hh, hl = st["p0"], b["g_read"], b["product"], b["hid_hi"], b["hid_lo"]

                def one(i, last):
                    split_hi(ahead(st, i, 0, last))
                    act.wait_ge(sem["panel_used"], p0 + i * 2 + 1)
                    act.wait_ge(sem["product"], pr + i)
                    if st["conv"] is None:
                        nc.scalar.activation(gate_t[:, :, 0:N], ps_g[:, :, 0:N], ACT.Silu).then_inc(sem["g_read"], 1)
                        split_hi(ahead(st, i, 1, last))
                    else:
                        wc, bc = st["conv"]
                        for c in range(2):
                            cc = st["k0"] + i * 2 + c
                            ins = nc.scalar.activation(gate_t[:, c, 0:N], ps_g[:, c, 0:N], ACT.Identity,
                                                       scale=colv[:, ds(wc + 2 * FC + st["k0"] + FC + c + i * 2, 1)], bias=colv[:, ds(bc + FC + st["k0"] + c + i * 2, 1)])
                        ins.then_inc(sem["g_affine"], 1)
                        act.wait_ge(sem["g_conv"], b["g_conv"] + i + 1)
                        nc.scalar.activation(gate_t[:, :, 0:N], gate_t[:, :, 0:N], ACT.Silu).then_inc(sem["g_read"], 1)
                        split_hi(ahead(st, i, 1, last))
                        act.wait_ge(sem["panel_used"], p0 + i * 2 + 2)
                        act.wait_ge(sem["hid_lo"], hl + i)
                        for c in range(2):
                            ins = nc.scalar.activation(prod_t[:, c, 0:N], ps_u[:, c, 0:N], ACT.Identity,
                                                       scale=colv[:, ds(wc + 2 * FC + st["k0"] + c + i * 2, 1)], bias=colv[:, ds(bc + st["k0"] + c + i * 2, 1)])
                        ins.then_inc(sem["u_affine"], 1)
                    act.wait_ge(sem["product"], pr + i + 1)
                    nc.scalar.activation(hid_hi[:, ds(i * (2 * N), 2 * N)].rearrange("p (c n) -> p c n", c=2), prod_t[:, :, 0:N],
                                         ACT.Copy).then_inc(sem["hid_hi"], 1)
                ch.loop(st["iters"], 0, one)
            elif st["kind"] in ("dn", "proj"):
                def one(i, last):
                    for j in range(len(st["shapes"])):
                        split_hi(ahead(st, i, j, last))
                ch.loop(st["iters"], 0, one)
            elif st["kind"] == "mixer":
                mixer_act(st, b, act, split_hi)
            elif st["kind"] == "mla_in":
                mla_in_act(st, b, act, split_hi)
            elif st["kind"] == "mla":
                ch.loop(st["iters"], 0, lambda i, last: mla_act(st, b, act, split_hi, i, last))
            elif st["kind"] == "na":
                ch.loop(st["iters"], 0, lambda i, last: na_act(st, b, act, split_hi, i, last))
            elif st["kind"] == "gather":
                act.wait_ge(sem["s_kept"], b["s_kept"])
                for k in range(KD):
                    nc.scalar.activation(h_hi[:, k * S:(k + 1) * S], (o_lat if st["ctx"] else on_lat)[:, k, :], ACT.Copy).then_inc(sem["h_hi"], 1)
                if st["ctx"]:
                    for k in range(KD):
                        nc.scalar.activation(oc_hi[:, k * C:(k + 1) * C], o_ctx[:, k, :], ACT.Copy).then_inc(sem["h_hi"], 1)
            elif st["kind"] == "store":
                for t in range(4):
                    pair = (ps_g, ps_u)[t % 2]
                    act.wait_ge(sem["o_tr"], b["o_tr"] + t + 1)
                    nc.scalar.activation(x_out[:, t, :].rearrange("p (c n) -> p c n", c=2), pair[:, :, :], ACT.Copy).then_inc(sem["o_out"], 1)

    def mixer_pe(st, b, pe, reduce_gemv, triple):
        for j in range(8):
            pair = (ps_g, ps_u)[j % 2]
            pe.wait_ge(sem["w_split_lo"], st["p0"] + j + 1)
            if j >= 2:
                pe.wait_ge(sem["in_evac"], b["in_evac"] + j - 1)
            whi, wlo = (w_view(t, j % 2, st["shapes"][j]) for t in (w_hi, w_lo))
            for k in range(KD):
                if j == 0:
                    pe.wait_ge(sem["h_ready"], b["h_ready"] - KD + k + 1)
                hh, hl = (t[:, k * S:(k + 1) * S] for t in (h_hi, h_lo))
                for c in range(2):
                    cc = slice(c * P, (c + 1) * P)
                    if j == 5 and c == 1:
                        continue
                    ins = triple(pair[:, c, :], whi[:, k, cc], wlo[:, k, cc], hh, hl, k == 0, k == KD - 1)
            if j == 5:
                for t in range(4):
                    tt = slice(t * P, (t + 1) * P)
                    for k in range(KD):
                        hh, hl = (u[:, k * S:(k + 1) * S][:, tt] for u in (h_hi, h_lo))
                        ins = triple(pair[:, 1, tt], hh, hl, whi[:, k, P:2 * P], wlo[:, k, P:2 * P], k == 0, k == KD - 1)
            ins.then_inc(sem["panel_used"], 1)
            if 1 <= j <= 5 and j - 1 < len(st["gemvs"]):
                reduce_gemv(st["gemvs"][j - 1])
            if j in (1, 3):
                m = j // 2
                pe.wait_ge(sem["lconv"], b["lconv"] + 2)
                if m == 0:
                    pe.wait_ge(sem["misc_in"], 16 * 10 * (st["l"] + 1))
                else:
                    pe.wait_ge(sem["gates_r"], b["gates_r"] + 2)
                for c in range(2):
                    ins = nc.tensor.matmul(ps_d[:, c, :], gate_w[:, m, c, :], cx[:, c, :], start=True, stop=True)
                ins.then_inc(sem["gates_mm"], 1)
        for n in range(5, len(st["gemvs"])):
            reduce_gemv(st["gemvs"][n])
        pe.wait_ge(sem["in_evac"], b["in_evac"] + 8)
        pe.wait_ge(sem["gates_i"], b["gates_i"] + 2)

        def scores(h):
            i, g = h // 2, h % 2
            pr = slice(g * HD, (g + 1) * HD)
            pair = (ps_g, ps_u)[g]
            if h >= 2:
                pe.wait_ge(sem["at_s_read"], b["at_s_read"] + h - 1)
            for n in range(4):
                q = mq[pr, i, n * P:(n + 1) * P]
                o = pair[:, n // 2, (n % 2) * 2 * P:(n % 2 + 1) * 2 * P]
                if n == 0:
                    ins = nc.tensor.matmul(o[:, P:2 * P], q, mk[pr, 0:P], start=True, stop=True)
                else:
                    ins = nc.tensor.matmul(o, q, mk[pr, (n - 1) * P:(n + 1) * P], start=True, stop=True)
            ins.then_inc(sem["at_s"], 1)

        def weigh(h):
            i, g = h // 2, h % 2
            pe.wait_ge(sem["at_p"], b["at_p"] + h + 1)
            if h >= 1:
                pe.wait_ge(sem["at_pt"], b["at_pt"] + h)
            for n in range(4):
                for j in range(2):
                    if n == 0 and j == 0:
                        continue
                    t = 2 * n + j
                    ins = nc.tensor.transpose(ps_d[:, t // 4, (t % 4) * P:(t % 4 + 1) * P], att[:, g, n, j * P:(j + 1) * P], ident[:, :])
            ins.then_inc(sem["at_t"], 1)

        def values(h):
            i, g = h // 2, h % 2
            pe.wait_ge(sem["at_pt"], b["at_pt"] + h + 1)
            if h >= 2 and g == 0:
                pe.wait_ge(sem["y_at"], b["y_at"] + i)
            for n in range(4):
                o = ps_s[g * HD:(g + 1) * HD, n * P:(n + 1) * P]
                for j in range(1 if n == 0 else 0, 2):
                    ins = nc.tensor.matmul(o, mv[:, n - 1 + j, g * HD:(g + 1) * HD], att_t[:, g, 2 * n + j, :],
                                           start=(j == 0 or n == 0), stop=(j == 1))
            ins.then_inc(sem["at_o"], 1)

        scores(0)
        for h in range(NQ):
            if h + 1 < NQ:
                scores(h + 1)
            if h >= 1:
                values(h - 1)
            weigh(h)
        values(NQ - 1)

    def mla_in_pe(st, b, pe, triple):
        pe.wait_ge(sem["h_ready"], b["h_ready"])
        plans = [[(ps_g[:, 0, :], 0, P, 0), (ps_g[:, 1, :], P, 2 * P, 1)], [(ps_u[:, 0, :], 0, P, 0), (ps_u[:, 1, :], P, 2 * P, 1)],
                 [(ps_g[:, 0, :], 0, P, 0)], [(ps_u[:, 0, :], 0, DQ, 0)]]
        for j in range(4):
            pe.wait_ge(sem["w_split_lo"], st["p0"] + j + 1)
            if j >= 2:
                pe.wait_ge(sem["low_out"], b["low_out"] + j - 1)
            whi, wlo = (w_view(t, j % 2, st["shapes"][j]) for t in (w_hi, w_lo))
            for bank, c0, c1, c in plans[j]:
                for k in range(KD):
                    m = [t[:, k * S:(k + 1) * S] for t in (h_hi, h_lo)]
                    triple(bank[0:c1 - c0, :], whi[:, k, c0:c1], wlo[:, k, c0:c1], *m, k == 0, k == KD - 1)
                for k in range(KD):
                    m = [t[:, k * C:(k + 1) * C] for t in (ch_hi, ch_lo)]
                    ins = triple(ps_d[0:c1 - c0, j % 2, c * C:(c + 1) * C], whi[:, k, c0:c1], wlo[:, k, c0:c1], *m, k == 0, k == KD - 1)
            ins.then_inc(sem["panel_used"], 1)
        pe.wait_ge(sem["low_out"], b["low_out"] + 4)
        nc.tensor.matmul(ps_d[64:96, 0, :], turn_m[NOPE:DQ, NOPE:DQ], low_pe[64:96, C:T], start=True, stop=True).then_inc(sem["pe_rot"], 1)
        for n, (k0, k1) in enumerate(((0, 3), (3, 5))):
            if n:
                pe.wait_ge(sem["low_dev"], b["low_dev"] + n)
            for k in range(k0, k1):
                pe.wait_ge(sem["low_sq"], b["low_sq"] + k + 1)
                nc.tensor.matmul(ps_g[:, 1, :], mean_m[:, :], low_squares[:, k - k0, C:T], start=(k == k0), stop=(k == k1 - 1))
                ins = nc.tensor.matmul(ps_s[:, 0:C], mean_m[:, :], low_squares[:, k - k0, 0:C], start=(k == k0), stop=(k == k1 - 1))
            ins.then_inc(sem["low_sum"], 1)

    def mla_pe(st, b, pe, triple, i):
        base_of = lambda name, per: b[name] + i * per
        U = len(MLA_UNITS)
        p0 = st["p0"]
        lows = lambda k, s: [t[:, k, s] for t in (low_hi, low_lo)]
        lat, ctx_s = slice(C, T), slice(0, C)
        pe.wait_ge(sem["w_split_lo"], p0 + i * 2 + 1)
        pe.wait_ge(sem["s_kept"], base_of("s_kept", PER))
        whi, wlo = (w_view(t, 0, st["shapes"][0]) for t in (w_hi, w_lo))
        for h in range(PER):
            cc = slice(h * DQ, (h + 1) * DQ)
            for k in range(3):
                triple(ps_all[0:DQ, h, :], whi[:, k, cc], wlo[:, k, cc], *lows(k, lat), k == 0, k == 2)
            for k in range(3):
                ins = triple(ps_d[0:DQ, h // 2, (h % 2) * C:(h % 2 + 1) * C], whi[:, k, cc], wlo[:, k, cc], *lows(k, ctx_s), k == 0, k == 2)
        ins.then_inc(sem["panel_used"], 1)
        pe.wait_ge(sem["head_out"], base_of("head_out", 3) + 1)
        for h in range(PER):
            ins = nc.tensor.matmul(ps_all[0:DQ, h, :], turn_m[0:DQ, :], q_flat[0:DQ, h, :], start=True, stop=True)
        ins.then_inc(sem["head_mm"], 1)
        pe.wait_ge(sem["w_split_lo"], p0 + i * 2 + 2)
        whi, wlo = (w_view(t, 1, st["shapes"][1]) for t in (w_hi, w_lo))
        for h in range(PER):
            cc = slice(h * P, (h + 1) * P)
            for k in range(2):
                ins = triple(ps_all[:, 4 + h, :], whi[:, k, cc], wlo[:, k, cc], *lows(3 + k, lat), k == 0, k == 1)
        ins.then_inc(sem["head_mm"], 1)
        pe.wait_ge(sem["q_rot"], base_of("q_rot", 1) + 1)
        for h in range(PER):
            cc = slice(h * P, (h + 1) * P)
            for k in range(2):
                triple(ps_g[:, h // 2, (h % 2) * C:(h % 2 + 1) * C], whi[:, k, cc], wlo[:, k, cc], *lows(3 + k, ctx_s), k == 0, k == 1)

        def tile_of_values(t):
            tt = slice(t * P, (t + 1) * P)
            o = ps_all[:, 2 + t // 2, (t % 2) * C:(t % 2 + 1) * C].rearrange("p (h n) -> p h n", n=HD)
            for k in range(2):
                vh, vl = (w[:, k, :].rearrange("p (h n) -> p h n", n=P)[:, :, NOPE:P] for w in (whi, wlo))
                ins = triple(o, *lows(3 + k, tt), vh, vl, k == 0, k == 1)
            return ins

        for t in range(4):
            ins = tile_of_values(t)
        ins.then_inc(sem["head_mm"], 1)
        pe.wait_ge(sem["head_out"], base_of("head_out", 3) + 2)
        for t in (4, 5):
            ins = tile_of_values(t)
        ins.then_inc(sem["panel_used"], 1)
        pe.wait_ge(sem["head_out"], base_of("head_out", 3) + 3)

        def scores(n):
            h, ctx, q = MLA_UNITS[n]
            if n >= 2:
                pe.wait_ge(sem["s_exp"], base_of("s_exp", U) + n - 1)
            qq = slice(q * P, (q + 1) * P)
            o = ps_all[:, 2 * (n % 2), C:2 * C]
            if ctx:
                ins = nc.tensor.matmul(o, q_ctx[0:DQ, h, qq], keys[0:DQ, h, 0:C], start=True, stop=True)
            else:
                nc.tensor.matmul(o, q_flat[0:DQ, h, qq], keys[0:DQ, h, 0:C], start=True, stop=True)
                ins = nc.tensor.matmul(ps_all[:, 2 * (n % 2) + 1, :], q_turn[0:DQ, h, qq], keys[0:DQ, h, C:T], start=True, stop=True)
            ins.then_inc(sem["s_made"], 1)

        def turn(n):
            h, ctx, q = MLA_UNITS[n]
            pe.wait_ge(sem["s_shared"], base_of("s_shared", U) + n + 1)
            pe.wait_ge(sem["copied0"], base_of("copied0", U) + n)
            for t in range(2 if ctx else 3):
                ins = nc.tensor.matmul(ps_all[:, 4, t * P:(t + 1) * P], prob[:, n % 2, t * P:(t + 1) * P], diag[:, n % 2, :], start=True, stop=True)
            ins.then_inc(sem["turned0"], 1)
            if not ctx:
                pe.wait_ge(sem["copied1"], base_of("copied1", 4 * PER) + MLA_LAT[n])
                for t in range(3, 6):
                    ins = nc.tensor.matmul(ps_all[:, 5, (t - 3) * P:(t - 2) * P], prob[:, n % 2, t * P:(t + 1) * P], diag[:, n % 2, :], start=True, stop=True)
                ins.then_inc(sem["turned1"], 1)

        def weigh(n):
            h, ctx, q = MLA_UNITS[n]
            pe.wait_ge(sem["copied0"], base_of("copied0", U) + n + 1)
            if not ctx:
                pe.wait_ge(sem["copied1"], base_of("copied1", 4 * PER) + MLA_LAT[n] + 1)
            if q == 0 and h == 2:
                pe.wait_ge(sem["s_kept"], base_of("s_kept", PER) + ctx + 1)
            for t in range(2 if ctx else 6):
                v = vals[:, t, h * HD:(h + 1) * HD]
                ins = nc.tensor.matmul(ps_all[(h % 2) * HD:(h % 2 + 1) * HD, 6 + ctx, q * P:(q + 1) * P], v, prob_t[:, n % 2, t * P:(t + 1) * P], start=(t == 0), stop=(t == (1 if ctx else 5)))
            ins.then_inc(sem["s_weighted"], 1)

        scores(0)
        for n in range(U):
            if n + 1 < U:
                scores(n + 1)
            if n:
                weigh(n - 1)
            turn(n)
        weigh(U - 1)

    def na_pe(st, b, pe, triple, i):
        base_of = lambda name, per: b[name] + i * per
        U = len(NA_UNITS)
        p0 = st["p0"]
        pe.wait_ge(sem["s_kept"], base_of("s_kept", PER // 2))
        pe.wait_ge(sem["h_ready"], b["h_ready"])
        for j in range(4):
            pe.wait_ge(sem["w_split_lo"], p0 + i * 4 + j + 1)
            whi, wlo = (w_view(t, j % 2, st["shapes"][j]) for t in (w_hi, w_lo))
            if j < 2:
                for c in range(2):
                    cc = slice(c * P, (c + 1) * P)
                    for k in range(KD):
                        m = [t[:, k * S:(k + 1) * S] for t in (h_hi, h_lo)]
                        ins = triple(ps_all[:, 2 * j + c, :], whi[:, k, cc], wlo[:, k, cc], *m, k == 0, k == KD - 1)
                    if j == 1:
                        for k in range(KD):
                            m = [t[:, k * C:(k + 1) * C] for t in (ch_hi, ch_lo)]
                            ins = triple(ps_all[:, 4, c * C:(c + 1) * C], whi[:, k, cc], wlo[:, k, cc], *m, k == 0, k == KD - 1)
            else:
                for t in range(6):
                    bank = ps_all[:, 5 + t // 2, (t % 2) * 2 * P:(t % 2 + 1) * 2 * P]
                    for kk in range(KD // 2):
                        k = (j - 2) * (KD // 2) + kk
                        if t < 2:
                            m = [u[:, k * C + t * P:k * C + (t + 1) * P] for u in (ch_hi, ch_lo)]
                        else:
                            m = [u[:, k * S + (t - 2) * P:k * S + (t - 1) * P] for u in (h_hi, h_lo)]
                        ins = triple(bank, *m, whi[:, kk, :], wlo[:, kk, :], k == 0 and t % 2 == 0, k == KD - 1 and t % 2 == 1)
            ins.then_inc(sem["panel_used"], 1)
        pe.wait_ge(sem["n_out_q"], base_of("n_out_q", 1) + 1)

        def scores(n):
            h, j = NA_UNITS[n]
            r, c = slice((h % 2) * HD, (h % 2 + 1) * HD), h // 2
            if n >= 4:
                pe.wait_ge(sem["s_exp"], base_of("s_exp", U) + n - 3)
            q = nq[r, c, j * P:(j + 1) * P]
            kk = nk[r, c, C:T].rearrange("p (r n) -> p r n", n=GRID)[:, :, BAND[j]:BAND[j] + KC_]
            nc.tensor.matmul(ps_all[:, n % 4, 0:C], q, nk[r, c, 0:C], start=True, stop=True)
            nc.tensor.matmul(ps_all[:, n % 4, C:2 * C].rearrange("p (r n) -> p r n", n=KC_), q, kk, start=True, stop=True).then_inc(sem["s_made"], 1)

        def turn(n):
            pe.wait_ge(sem["s_shared"], base_of("s_shared", U) + n + 1)
            for half in range(2):
                pe.wait_ge(sem[f"copied{half}"], base_of(f"copied{half}", U) + n)
                for t in range(2):
                    w = slice((2 * half + t) * P, (2 * half + t + 1) * P)
                    ins = nc.tensor.matmul(ps_all[:, 4 + half, t * P:(t + 1) * P], prob_n[:, n % 2, w], diag_n[:, n % 2, :], start=True, stop=True)
                ins.then_inc(sem[f"turned{half}"], 1)

        def weigh(n):
            h, j = NA_UNITS[n]
            for half in range(2):
                pe.wait_ge(sem[f"copied{half}"], base_of(f"copied{half}", U) + n + 1)
            if n == 0:
                pe.wait_ge(sem["band_in"], base_of("band_in", 16 * 4 * ROWS) + 16 * 4 * ROWS)
            cc = slice(h * HD, (h + 1) * HD)
            for t in range(4):
                v = nv[:, t, cc] if t < 2 else nvb[:, j, t - 2, cc]
                ins = nc.tensor.matmul(ps_all[(h % 2) * HD:(h % 2 + 1) * HD, 6 + h // 2, j * P:(j + 1) * P], v, prob_nt[:, n % 2, t * P:(t + 1) * P], start=(t == 0), stop=(t == 3))
            ins.then_inc(sem["s_weighted"], 1)

        scores(0)
        scores(1)
        pe.wait_ge(sem["n_out"], base_of("n_out", 1) + 1)
        for n in range(U):
            if n + 2 < U:
                scores(n + 2)
            if n:
                weigh(n - 1)
            turn(n)
        weigh(U - 1)

    @block.tensor
    def _(pe):
        def reduce_gemv(g, i=0):
            pe.wait_ge(sem["gemv_done"], g + i + 1)
            for h in range(2):
                part = lambda t: acc[:, t, h * P:(h + 1) * P]
                if g < G_ADA:
                    o = ps_mod[:, ds(2 * g + h + i * 2, 1)]
                    nc.tensor.matmul(o, part(0), ones[:, :], start=True, stop=False)
                    ins = nc.tensor.matmul(o, part(1), ones[:, :], start=False, stop=True)
                else:
                    nc.tensor.matmul(ps_mod[:, ds(2 * g + h + i * 2, 1)], part(0), ones[:, :], start=True, stop=True)
                    ins = nc.tensor.matmul(ps_mod[:, ds(CTX_COL + 2 * (g - G_ADA) + h + i * 2, 1)], part(1), ones[:, :], start=True, stop=True)
            ins.then_inc(sem["gemv_reduced"], 1)

        def triple(o, whi, wlo, mhi, mlo, first, last):
            nc.tensor.matmul(o, whi, mhi, start=first, stop=False)
            nc.tensor.matmul(o, whi, mlo, start=False, stop=False)
            return nc.tensor.matmul(o, wlo, mhi, start=False, stop=last)

        pe.wait_ge(sem["consts"], 5)
        for st in PLAN:
            b = st["base"]
            kind = st["kind"]
            if kind == "load":
                pe.wait_ge(sem["const_in"], 16)
                n_in = sum(1 for t in range(row_tiles) for name, ap in rows
                           if max(col[name], t * P) < min(col[name] + ap.shape[0], (t + 1) * P))
                pe.wait_ge(sem["rows_in"], 16 * n_in)
                for t in range(row_tiles):
                    n = min(P, n_rows - t * P)
                    if t >= 2:
                        pe.wait_ge(sem["row_col"], t - 1)
                    nc.tensor.transpose(ps_d[:, t % 2, 0:n], row_in[0:n, t, :], ident[0:n, 0:n]).then_inc(sem["row_tile"], 1)
                pe.wait_ge(sem["x_rows_in"], 32)
                for k in range(KD):
                    if k >= 2:
                        pe.wait_ge(sem["x_in"], k - 1)
                    for t in range(4):
                        ins = nc.tensor.transpose(ps_g[:, k % 2, t * P:(t + 1) * P], x_rows[:, t, k * P:(k + 1) * P], ident[:, :])
                    ins.then_inc(sem["x_tr"], 1)
                for k in range(KD):
                    if k >= 2:
                        pe.wait_ge(sem["hc_in"], k - 1)
                    for t in range(2):
                        ins = nc.tensor.transpose(ps_u[:, k % 2, t * P:(t + 1) * P], c_rows[:, t, k * P:(k + 1) * P], ident[:, :])
                    ins.then_inc(sem["hc_tr"], 1)
            elif kind == "prologue":
                for g in st["gemvs"]:
                    reduce_gemv(g)
            elif kind == "norm" and st["mode"] != "mod_h":
                buf, N = src(st)
                if st["mode"] == "ln_x":
                    for n in ("down0", "down1", "proj0", "proj1", "deviation"):
                        if b[n]:
                            pe.wait_ge(sem[n], b[n])
                    for k in range(KD):
                        ins = nc.tensor.matmul(ps_s[:, 0:N], mean_m[:, :], buf[:, k * N:(k + 1) * N], start=(k == 0), stop=(k == KD - 1))
                    ins.then_inc(sem["mean_summed"], 1)
                    pe.wait_ge(sem["centred"], b["centred"] + KD)
                for k in range(KD):
                    pe.wait_ge(sem["squared"], b["squared"] + k + 1)
                    nc.tensor.matmul(ps_s[:, 0:N], mean_m[:, :], squares[:, k % 4, 0:N], start=(k == 0), stop=(k == KD - 1)).then_inc(sem["square_summed"], 1)
            elif kind == "gu":
                N, p0 = st["N"], st["p0"]

                def one(i, last):
                    for j, bank in enumerate((ps_g, ps_u)):
                        pe.wait_ge(sem["w_split_lo"], p0 + i * 2 + j + 1)
                        read = ("g_read", "product")[j]
                        pe.wait_ge(sem[read], b[read] + i)
                        whi, wlo = (w_view(t, j, st["shapes"][j]) for t in (w_hi, w_lo))
                        for k in range(KD):
                            if st["wait_h"] and j == 0:
                                pe.wait_ge(sem["h_ready"], b["h_ready"] - KD + k + 1)
                            m = [t[:, k * N:(k + 1) * N] for t in (h_hi, h_lo)]
                            for c in range(2):
                                cc = slice(c * P, (c + 1) * P)
                                ins = triple(bank[:, c, 0:N], whi[:, k, cc], wlo[:, k, cc], *m, k == 0, k == KD - 1)
                        ins.then_inc(sem["panel_used"], 1)
                    if st["gemv"] is not None:
                        reduce_gemv(st["gemv"], i)
                Chain(pe, None).loop(st["iters"], 0, one)
            elif kind == "dn":
                N, p0, nk = st["N"], st["p0"], st["nk"]
                pe.wait_ge(sem["hid_lo"], b["hid_lo"])

                def one(i, last):
                    for j in range(2):
                        pe.wait_ge(sem["w_split_lo"], p0 + i * 2 + j + 1)
                        pe.wait_ge(sem[f"down{j}"], b[f"down{j}"] + i)
                        whi, wlo = (w_view(t, j, st["shapes"][j]) for t in (w_hi, w_lo))
                        for k in range(nk):
                            m = [t[:, k * N:(k + 1) * N] for t in (hid_hi, hid_lo)]
                            ins = triple(ps_d[:, j, 0:N], whi[:, k, :], wlo[:, k, :], *m, k == 0, k == nk - 1)
                        ins.then_inc(sem["panel_used"], 1)
                    if st["gemv"] is not None:
                        reduce_gemv(st["gemv"], i)
                Chain(pe, None).loop(st["iters"], 0, one)
            elif kind == "proj":
                p0 = st["p0"]

                def one(i, last):
                    for j, bank in enumerate((ps_g, ps_u)):
                        pe.wait_ge(sem["w_split_lo"], p0 + i * 2 + j + 1)
                        pe.wait_ge(sem[f"proj{j}"], b[f"proj{j}"] + i)
                        whi, wlo = (w_view(t, j, st["shapes"][j]) for t in (w_hi, w_lo))
                        for k in range(KD):
                            m = [t[:, k * S:(k + 1) * S] for t in (h_hi, h_lo)]
                            for c in range(2):
                                cc = slice(c * P, (c + 1) * P)
                                ins = triple(bank[:, c, :], whi[:, k, cc], wlo[:, k, cc], *m, k == 0, k == KD - 1)
                        if st["ctx_gate"] is not None:
                            for c in range(2):
                                cc = slice(c * P, (c + 1) * P)
                                for k in range(KD):
                                    m = [t[:, k * C:(k + 1) * C] for t in (oc_hi, oc_lo)]
                                    ins = triple(ps_d[:, j, c * C:(c + 1) * C], whi[:, k, cc], wlo[:, k, cc], *m, k == 0, k == KD - 1)
                        ins.then_inc(sem["panel_used"], 1)
                pe.wait_ge(sem["h_ready"], b["h_ready"])
                Chain(pe, None).loop(st["iters"], 0, one)
            elif kind == "mixer":
                mixer_pe(st, b, pe, reduce_gemv, triple)
            elif kind == "mla_in":
                mla_in_pe(st, b, pe, triple)
            elif kind == "mla":
                pe.wait_ge(sem["low_lo"], b["low_lo"])
                Chain(pe, None).loop(st["iters"], 0, lambda i, last: mla_pe(st, b, pe, triple, i))
            elif kind == "na":
                Chain(pe, None).loop(st["iters"], 0, lambda i, last: na_pe(st, b, pe, triple, i))
            elif kind == "store":
                for n in ("down0", "down1", "x_new", "x_in", "proj0", "proj1", "h_ready", "s_kept", "low_lo"):
                    if b[n]:
                        pe.wait_ge(sem[n], b[n])
                for t in range(4):
                    if t >= 2:
                        pe.wait_ge(sem["o_out"], b["o_out"] + t - 1)
                    for k in range(KD):
                        o = (ps_g, ps_u)[t % 2][:, k // 4, (k % 4) * P:(k % 4 + 1) * P]
                        tok = hc[:, k * C + (t % 2) * P:k * C + (t % 2 + 1) * P] if st["probe"] else x[:, k * S + t * P:k * S + (t + 1) * P]
                        ins = nc.tensor.transpose(o, tok, ident[:, :])
                    ins.then_inc(sem["o_tr"], 1)

    def mixer_dve(st, b, dve, ch, mix_gemv):
        l = st["l"]
        V = nc.vector
        cw = lambda name, t, c, taps: colv[:, col[name] + (l * taps + t) * 2 + c:col[name] + (l * taps + t) * 2 + c + 1]
        cb = lambda name, c: colv[:, col[name] + l * 2 + c:col[name] + l * 2 + c + 1]
        lam = colv[:, col["lam"] + 2 * l:col["lam"] + 2 * l + 2]
        y, z, z2, s = sm(14, 2), sm(15, 2), sm(16, 2), sm(17, 2)
        mix_gemv(0)
        ch.link(V.tensor_scalar(z, lam, -1.0, None, ALU.mult))
        ch.link(V.tensor_tensor(z2, z, lam, ALU.min))
        V.tensor_scalar(s, z2, 1.0, None, ALU.mult).then_inc(sem["lam_in"], 1)
        dve.wait_ge(sem["lam_exp"], b["lam_exp"] + 1)
        ch.link(V.tensor_scalar(z, y, 2.0, None, ALU.add))
        ch.link(V.reciprocal(z, z))
        ch.link(V.tensor_tensor(z, z, y, ALU.mult))
        ch.link(V.tensor_tensor(z2, z, z, ALU.mult))
        ch.link(V.tensor_scalar(s, z2, 1.0 / 17, 1.0 / 15, ALU.mult, ALU.add))
        for d in (13, 11, 9, 7, 5, 3, 1):
            ch.link(V.tensor_tensor(s, s, z2, ALU.mult))
            ch.link(V.tensor_scalar(s, s, 1.0 / d, None, ALU.add))
        ch.link(V.tensor_tensor(s, s, z, ALU.mult))
        ch.link(V.tensor_scalar(z, lam, -1.0, 0.0, ALU.mult, ALU.max))
        ch.link(V.scalar_tensor_tensor(s, s, 2.0, z, ALU.mult, ALU.add))
        ch.link(V.tensor_scalar(lsp[:, 0:2], s, 8.0, None, ALU.mult))
        V.tensor_scalar(lsp[:, 4:6], s, -8.0, None, ALU.mult).then_inc(sem["lru_q"], 1)
        dve.wait_ge(sem["in_evac"], b["in_evac"] + 1)
        for c in range(2):
            ch.link(V.tensor_scalar(cx[:, c, :], lx[:, c, :], cw("lconv_w", 3, c, 4), cb("lconv_b", c), ALU.mult, ALU.add))
            for t in (1, 2, 3):
                o = cx[:, c, t:]
                ins = V.scalar_tensor_tensor(o, lx[:, c, 0:S - t], cw("lconv_w", 3 - t, c, 4), o, ALU.mult, ALU.add)
                if t < 3:
                    ch.link(ins)
            ins.then_inc(sem["lconv"], 1)
        mix_gemv(1)
        mix_gemv(2)
        dve.wait_ge(sem["in_evac"], b["in_evac"] + 4)
        ch.link(V.tensor_tensor(sct[:, :, :], sct[:, :, :], sxt[:, :, :], ALU.mult))
        for c in range(2):
            ch.link(V.tensor_scalar(sxt[:, c, :], sct[:, c, :], cw("sconv_w", 2, c, 3), None, ALU.mult))
            for t in (1, 2):
                o = sxt[:, c, t:]
                ch.link(V.scalar_tensor_tensor(o, sct[:, c, 0:S - t], cw("sconv_w", 2 - t, c, 3), o, ALU.mult, ALU.add))
        dve.wait_ge(sem["in_evac"], b["in_evac"] + 5)
        V.tensor_tensor(sxt[:, :, :], sxt[:, :, :], sbt[:, :, :], ALU.mult).then_inc(sem["y_sc"], 1)
        mix_gemv(3)
        dve.wait_ge(sem["lru_t"], b["lru_t"] + 1)
        ch.link(V.tensor_scalar(lx[:, :, :], lt[:, :, :], 1.0, None, ALU.add))
        ch.link(V.reciprocal(lx[:, :, :], lx[:, :, :]))
        V.tensor_tensor(lt[:, :, :], lt[:, :, :], lx[:, :, :], ALU.mult).then_inc(sem["lru_m"], 1)
        mix_gemv(4)
        dve.wait_ge(sem["gates_i"], b["gates_i"] + 2)
        ch.link(V.tensor_tensor(gx[:, :, :], gx[:, :, :], cx[:, :, :], ALU.mult))
        dve.wait_ge(sem["gelu"], b["gelu"] + 1)
        ch.link(V.memset(lt[:, :, 0:1], 1.0))
        ch.link(V.tensor_tensor(gx[:, :, :], gx[:, :, :], lt[:, :, :], ALU.mult))
        for c in range(2):
            ch.link(V.tensor_tensor_scan(lx[:, c, :], ga[:, c, :], gx[:, c, :], 0.0, ALU.mult, ALU.add))
        V.tensor_tensor(lt[:, :, :], lx[:, :, :], lg[:, :, :], ALU.mult).then_inc(sem["y_lru"], 1)
        for n in range(5, len(st["gemvs"])):
            mix_gemv(n)
        for q in range(2):
            ch.link(V.memset(att[:, q, 0, 0:P], NEG))
        dve.wait_ge(sem["misc_in"], 160 * (l + 1))

        def soften(h):
            q, head = h % 2, h // 2 + 4 * (h % 2)
            pair = (ps_g, ps_u)[q]
            mx, nm, es, su = (sm(q * 6 + t) for t in range(4))
            dve.wait_ge(sem["at_s"], b["at_s"] + h + 1)
            if h >= 2:
                dve.wait_ge(sem["at_t"], b["at_t"] + h - 1)
                V.memset(att[:, q, 0, 0:P], NEG)
            ch.step(V.scalar_tensor_tensor(att[:, q, 0, P:2 * P], pair[:, 0, P:2 * P], HD ** -0.5, alibi[:, head, P:2 * P], ALU.mult, ALU.add))
            ch.step(V.scalar_tensor_tensor(att[:, q, 1, :], pair[:, 0, 2 * P:4 * P], HD ** -0.5, alibi[:, head, :], ALU.mult, ALU.add))
            for n in (2, 3):
                last = V.scalar_tensor_tensor(att[:, q, n, :], pair[:, 1, (n - 2) * 2 * P:(n - 1) * 2 * P], HD ** -0.5, alibi[:, head, :], ALU.mult, ALU.add)
                if n == 2:
                    ch.step(last)
            last.then_inc(sem["at_s_read"], 1)
            dve.wait_ge(sem["at_s_read"], b["at_s_read"] + h + 1)
            ch.link(V.tensor_reduce(mx, att[:, q, :, :], AX_X, ALU.max))
            ch.link(V.tensor_scalar(mx, mx, sinks_col(h), None, ALU.max))
            ch.link(V.tensor_scalar(nm, mx, -1.0, None, ALU.mult))
            V.tensor_tensor(att[:, q, :, :], att[:, q, :, :], mx.rearrange("p (n o) -> p n o", o=1).broadcast_to([P, 4, 2 * P]), ALU.subtract).then_inc(sem["at_sub"], 1)

        def share(h):
            q = h % 2
            mx, nm, es, su = (sm(q * 6 + t) for t in range(4))
            dve.wait_ge(sem["at_exp"], b["at_exp"] + h + 1)
            ch.link(V.tensor_reduce(su, att[:, q, :, :], AX_X, ALU.add))
            ch.link(V.tensor_tensor(su, su, es, ALU.add))
            ch.link(V.reciprocal(su, su))
            V.tensor_tensor(att[:, q, :, :], att[:, q, :, :], su.rearrange("p (n o) -> p n o", o=1).broadcast_to([P, 4, 2 * P]), ALU.mult).then_inc(sem["at_p"], 1)

        soften(0)
        for h in range(NQ):
            if h + 1 < NQ:
                soften(h + 1)
            share(h)

    def conv_taps(st, b, i, dve, ch):
        N, p0 = st["N"], st["p0"]
        wc, bc = st["conv"]
        V = nc.vector
        for half, (ready, t_, ps, off) in enumerate((("g_affine", gate_t, ps_g, FC), ("u_affine", prod_t, ps_u, 0))):
            dve.wait_ge(sem[ready], b[ready] + i + 1)
            w = lambda tap, c: colv[:, ds(wc + tap * 2 * FC + off + st["k0"] + c + i * 2, 1)]
            tok = []
            for c in range(2):
                o = t_[:, c, 1:N]
                tok.append(ch.step(V.scalar_tensor_tensor(o, ps[:, c, 0:N - 1], w(0, c), o, ALU.mult, ALU.add)))
            for c in range(2):
                o = t_[:, c, 0:N - 1]
                ch.wait(tok[c])
                ins = V.scalar_tensor_tensor(o, ps[:, c, 1:N], w(2, c), o, ALU.mult, ALU.add)
                if half == 0 and c == 1:
                    ins.then_inc(sem["g_conv"], 1)
                else:
                    last = ch.step(ins)
                    if half == 0:
                        ch.wait(last)
        ch.wait(last)

    def rope(dve, ch, o, x_, swapped):
        V = nc.vector
        ch.step(V.tensor_tensor(o, x_, turns[64:96, 0, :], ALU.mult))
        ch.link(V.tensor_tensor(turned[64:96, :], swapped, turns[64:96, 1, :], ALU.mult))
        return V.tensor_tensor(o, o, turned[64:96, :], ALU.add)

    def mla_in_dve(st, b, dve, ch):
        V = nc.vector
        dve.wait_ge(sem["rope_in"], 48)
        dve.wait_ge(sem["pe_rot"], b["pe_rot"] + 1)
        ch.link(rope(dve, ch, keys[64:96, 0, C:T], low_pe[64:96, C:T], ps_d[64:96, 0, :]))
        for h in range(1, PER):
            ins = V.tensor_copy(keys[64:96, h, C:T], keys[64:96, 0, C:T])
        ins.then_inc(sem["pe_key"], 1)
        for n, (k0, k1, g) in enumerate(((0, 3, col["q_norm"]), (3, 5, col["kv_norm"]))):
            dve.wait_ge(sem["low_dev"], b["low_dev"] + n + 1)
            ch.link(V.reciprocal(low_rstd[:, :], low_rstd[:, :]))
            for k in range(k0, k1):
                ch.link(V.tensor_tensor(low[:, k, :], low[:, k, :], low_rstd[:, :], ALU.mult))
                V.tensor_scalar(low[:, k, :], low[:, k, :], colv[:, g + k - k0:g + k - k0 + 1], None, ALU.mult).then_inc(sem["low_full"], 1)

    def share(dve, ch, s_, ready, o):
        dve.wait_ge(sem["s_exp"], ready)
        ch.link(nc.vector.reciprocal(s_(3), s_(2)))
        nc.vector.tensor_scalar(o, ident[:, :], s_(3), None, ALU.mult).then_inc(sem["s_shared"], 1)

    MLA_LINKS = 2 * PER + (PER - 1) + 2 * PER * 6

    def mla_dve(st, b, dve, ch, i):
        V = nc.vector
        base_of = lambda name, per: b[name] + i * per
        U = len(MLA_UNITS)
        dve.wait_ge(sem["head_out"], base_of("head_out", 3) + 1)
        dve.wait_ge(sem["head_mm"], base_of("head_mm", 3) + 1)
        for h in range(PER):
            ins = rope(dve, ch, q_turn[64:96, h, :], q_flat[64:96, h, :], ps_all[64:96, h, :])
            if h < PER - 1:
                ch.link(ins)
            else:
                ins.then_inc(sem["q_rot"], 1)

        def most(n):
            h, ctx, q = MLA_UNITS[n]
            dve.wait_ge(sem["s_made"], base_of("s_made", U) + n + 1)
            pair = ps_all[:, 2 * (n % 2):2 * (n % 2) + 2, :].rearrange("p b n -> p (b n)")
            s_ = lambda t: stat[:, 4 * (n % 2) + t:4 * (n % 2) + t + 1]
            if n >= 2:
                dve.wait_ge(sem["s_shared"], base_of("s_shared", U) + n - 1)
            ch.link(V.tensor_reduce(s_(0), pair[:, C:C + (C if ctx else T)], AX_X, ALU.max))
            V.tensor_scalar(s_(1), s_(0), -(DQ ** -0.5), None, ALU.mult).then_inc(sem["s_max"], 1)

        def copy(n):
            h, ctx, q = MLA_UNITS[n]
            if ctx:
                return
            dve.wait_ge(sem["turned1"], base_of("turned1", 4 * PER) + MLA_LAT[n] + 1)
            if n >= 2:
                dve.wait_ge(sem["s_weighted"], base_of("s_weighted", U) + n - 1)
            V.tensor_copy(prob_t[:, n % 2, 3 * P:T], ps_all[:, 5, 0:3 * P]).then_inc(sem["copied1"], 1)

        most(0)
        for n in range(U):
            if n:
                copy(n - 1)
            share(dve, ch, lambda t: stat[:, 4 * (n % 2) + t:4 * (n % 2) + t + 1], base_of("s_exp", U) + n + 1, diag[:, n % 2, :])
            if n + 1 < U:
                most(n + 1)
        copy(U - 1)

    NA_LINKS = 2 * 16

    def na_dve(st, b, dve, ch, i):
        V = nc.vector
        base_of = lambda name, per: b[name] + i * per
        U = len(NA_UNITS)

        def most(n):
            h, j = NA_UNITS[n]
            dve.wait_ge(sem["s_made"], base_of("s_made", U) + n + 1)
            dve.wait_ge(sem["bias_made"], base_of("bias_made", U) + n + 1)
            s_ = lambda t: stat[:, 4 * (n % 4) + t:4 * (n % 4) + t + 1]
            band = ps_all[:, n % 4, C:2 * C].rearrange("p (r n) -> p r n", n=KC_)
            V.tensor_tensor(band, band, bias_m[:, j, :, :], ALU.add).then_inc(sem["s_biased"], 1)
            dve.wait_ge(sem["s_biased"], base_of("s_biased", U) + n + 1)
            ch.link(V.tensor_reduce(s_(0), ps_all[:, n % 4, :], AX_X, ALU.max))
            V.tensor_scalar(s_(1), s_(0), -(HD ** -0.5), None, ALU.mult).then_inc(sem["s_max"], 1)

        def copy(n):
            dve.wait_ge(sem["turned1"], base_of("turned1", U) + n + 1)
            if n >= 2:
                dve.wait_ge(sem["s_weighted"], base_of("s_weighted", U) + n - 1)
            V.tensor_copy(prob_nt[:, n % 2, C:2 * C], ps_all[:, 5, 0:C]).then_inc(sem["copied1"], 1)

        most(0)
        for n in range(U):
            if n:
                copy(n - 1)
            share(dve, ch, lambda t: stat[:, 4 * (n % 4) + t:4 * (n % 4) + t + 1], base_of("s_exp", U) + n + 1, diag_n[:, n % 2, :])
            if n + 1 < U:
                most(n + 1)
        copy(U - 1)

    @block.vector
    def _(dve):
        ch = Chain(dve, sem["dve_chain"])
        def gemv(g, slot=0, i=0, count=None):
            dve.wait_ge(sem[f"gemv_in{slot}"], count)
            if not (isinstance(g, int) and g == 0 and isinstance(i, int)):
                dve.wait_ge(sem["gemv_reduced"], g + i)
            two = g >= G_ADA
            seen = []
            total = 16 if two else 8
            for t in range(total):
                k = t // 2 if two else t
                cc = (KD * (1 + t % 2) if two else 0) + k
                s, o, w = c_col[:, cc:cc + 1], acc[:, t % 2, :], g_raw[:, slot, k, :]
                if t >= 2:
                    ch.wait(seen[t - 1] if t == total - 1 else seen[t - 2])
                    ins = nc.vector.scalar_tensor_tensor(o, w, s, o, ALU.mult, ALU.add)
                else:
                    ins = nc.vector.tensor_scalar(o, w, s, None, ALU.mult)
                if t < total - 1:
                    seen.append(ch.step(ins))
            ins.then_inc(sem["gemv_done"], 1)

        n_gemv = [0, 0]
        for st in PLAN:
            b = st["base"]
            kind = st["kind"]
            if kind == "load":
                dve.wait_ge(sem["c_act"], 1)
                dve.wait_ge(sem["consts"], 5)
            elif kind == "prologue":
                for n, g in enumerate(st["gemvs"]):
                    n_gemv[n % 2] += 16
                    gemv(g, n % 2, 0, n_gemv[n % 2])
            elif kind == "mods":
                dve.wait_ge(sem["gemv_reduced"], st["need"])
                for lo, hi, bias in st["spans"]:
                    ch.link(nc.vector.tensor_tensor(modc[:, lo:hi], ps_mod[:, lo:hi], colv[:, col["b_mod"] + bias:col["b_mod"] + bias + hi - lo], ALU.add))
                for c0, g0 in st["plus"]:
                    v = modc[:, c0:c0 + KD]
                    if g0 is None:
                        ch.link(nc.vector.tensor_scalar(v, v, 1.0, None, ALU.add))
                    else:
                        ch.link(nc.vector.scalar_tensor_tensor(v, v, 1.0, colv[:, g0:g0 + KD], ALU.add, ALU.mult))
                for c0 in st["half"]:
                    v = modc[:, c0:c0 + KD]
                    ch.link(nc.vector.tensor_scalar(v, v, 0.5, None, ALU.mult))
            elif kind == "norm":
                buf, N = src(st)
                mode = st["mode"]
                cols_of = modc if mode in ("rms_h", "mod_h") else colv
                A = lambda k: cols_of[:, st["A"] + k:st["A"] + k + 1]
                B = lambda k: cols_of[:, st["B"] + k:st["B"] + k + 1]
                if mode == "ln_x":
                    dve.wait_ge(sem["mean_summed"], b["mean_summed"] + 1)
                    for k in range(KD):
                        v = buf[:, k * N:(k + 1) * N]
                        nc.vector.tensor_tensor(v, v, ps_s[:, 0:N], ALU.subtract).then_inc(sem["centred"], 1)
                if mode != "mod_h":
                    dve.wait_ge(sem["deviation"], b["deviation"] + 1)
                    ch.link(nc.vector.reciprocal(rstd[:, 0:N], rstd[:, 0:N]))
                for k in range(KD):
                    v = buf[:, k * N:(k + 1) * N]
                    unit = v
                    if mode != "mod_h":
                        unit = unit_t[:, k % 2, 0:N]
                        ch.link(nc.vector.tensor_tensor(unit, v, rstd[:, 0:N], ALU.mult))
                    if "h_full" in st["totals"]:
                        if b["h_ready"] + k >= 2:
                            dve.wait_ge(sem["h_ready"], b["h_ready"] + k - 1)
                        nc.vector.tensor_scalar(full_t[:, k % 2, 0:N], unit, A(k), B(k), ALU.mult, ALU.add).then_inc(sem["h_full"], 1)
                    elif mode == "rms_x":
                        nc.vector.tensor_scalar(v, unit, A(k), None, ALU.mult).then_inc(sem["x_new"], 1)
                    else:
                        nc.vector.tensor_scalar(v, unit, A(k), B(k), ALU.mult, ALU.add).then_inc(sem["x_new"], 1)
                if "x_new" in st["totals"]:
                    dve.wait_ge(sem["x_new"], b["x_new"] + KD)
            elif kind == "gu":
                N, p0, pr, hh = st["N"], st["p0"], b["product"], b["hid_hi"]
                per_g = 0 if st["gemv"] is None else (15 if st["gemv"] >= G_ADA else 7)
                start0 = n_gemv[0]

                def one(i, last):
                    if per_g:
                        gemv(st["gemv"], 0, i, start0 + 16 + i * 16)
                    if st["conv"] is not None:
                        conv_taps(st, b, i, dve, ch)
                    dve.wait_ge(sem["g_read"], b["g_read"] + i + 1)
                    dve.wait_ge(sem["panel_used"], p0 + i * 2 + 2)
                    dve.wait_ge(sem["hid_hi"], hh + i)
                    other = ps_u[:, :, 0:N] if st["conv"] is None else prod_t[:, :, 0:N]
                    nc.vector.tensor_tensor(prod_t[:, :, 0:N], gate_t[:, :, 0:N], other, ALU.mult).then_inc(sem["product"], 1)
                    dve.wait_ge(sem["hid_hi"], hh + i + 1)
                    w = ds(i * (2 * N), 2 * N)
                    nc.vector.tensor_tensor(hid_lo[:, w].rearrange("p (c n) -> p c n", c=2), prod_t[:, :, 0:N],
                                            hid_hi[:, w].rearrange("p (c n) -> p c n", c=2).bitcast(F32), ALU.subtract).then_inc(sem["hid_lo"], 1)
                ch.loop(st["iters"], per_g + (7 if st["conv"] is not None else 0), one)
                if per_g:
                    n_gemv[0] += 16 * st["iters"]
            elif kind == "dn":
                N, p0 = st["N"], st["p0"]
                buf, _ = src(st)
                per_g = 0 if st["gemv"] is None else (15 if st["gemv"] >= G_ADA else 7)
                start0 = n_gemv[0]

                def one(i, last):
                    if per_g:
                        gemv(st["gemv"], 0, i, start0 + 16 + i * 16)
                    for j in range(2):
                        dve.wait_ge(sem["panel_used"], p0 + i * 2 + j + 1)
                        v = buf[:, ds(i * (2 * N) + j * N, N)]
                        nc.vector.scalar_tensor_tensor(v, ps_d[:, j, 0:N], modc[:, ds(st["gate"] + j + i * 2, 1)], v, ALU.mult, ALU.add).then_inc(sem[f"down{j}"], 1)
                ch.loop(st["iters"], per_g, one)
                if per_g:
                    n_gemv[0] += 16 * st["iters"]
                for j in range(2):
                    dve.wait_ge(sem[f"down{j}"], b[f"down{j}"] + st["iters"])
            elif kind == "proj":
                p0 = st["p0"]

                def one(i, last):
                    for j, bank in enumerate((ps_g, ps_u)):
                        dve.wait_ge(sem["panel_used"], p0 + i * 2 + j + 1)
                        for c in range(2):
                            v = x[:, ds(i * (4 * S) + (2 * j + c) * S, S)]
                            ins = nc.vector.scalar_tensor_tensor(v, bank[:, c, :], modc[:, ds(st["gate"] + 2 * j + c + i * 4, 1)], v, ALU.mult, ALU.add)
                        for c in range(2 if st["ctx_gate"] is not None else 0):
                            v = hc[:, ds(i * (4 * C) + (2 * j + c) * C, C)]
                            ins = nc.vector.scalar_tensor_tensor(v, ps_d[:, j, c * C:(c + 1) * C], modc[:, ds(st["ctx_gate"] + 2 * j + c + i * 4, 1)], v, ALU.mult, ALU.add)
                        ins.then_inc(sem[f"proj{j}"], 1)
                ch.loop(st["iters"], 0, one)
                for j in range(2):
                    dve.wait_ge(sem[f"proj{j}"], b[f"proj{j}"] + st["iters"])
            elif kind == "alpha":
                dve.wait_ge(sem["h_full"], b["h_full"])
                v = hc if st["ctx"] else x
                n = KD * (C if st["ctx"] else S)
                ch.link(nc.vector.tensor_scalar(v[:, 0:n], v[:, 0:n], ALPHA, None, ALU.mult))
            elif kind == "mla_in":
                mla_in_dve(st, b, dve, ch)
            elif kind == "mla":
                ch.loop(st["iters"], MLA_LINKS, lambda i, last: mla_dve(st, b, dve, ch, i))
            elif kind == "na":
                ch.loop(st["iters"], NA_LINKS, lambda i, last: na_dve(st, b, dve, ch, i))
            elif kind == "mixer":
                def mix_gemv(n):
                    if n < len(st["gemvs"]):
                        n_gemv[0] += 16
                        gemv(st["gemvs"][n], 0, 0, n_gemv[0])
                mixer_dve(st, b, dve, ch, mix_gemv)

    block_cm.__exit__(None, None, None)


def constants():
    q, k = np.arange(P)[:, None], np.arange(2 * P)[None, :]
    dist = (q + P - k).astype(np.float32)
    slopes = (2.0 ** (-8.0 * np.arange(1, NQ + 1) / NQ)).astype(np.float32)
    valid = (dist >= 0) & (dist < P)
    alibi = np.where(valid[:, None, :], -slopes[None, :, None] * dist[:, None, :], np.float32(NEG)).astype(np.float32)
    t = np.arange(S)
    inv = (10000.0 ** (-np.arange(ROPE // 4, dtype=np.float32) / (ROPE // 4))).astype(np.float32)
    ang = np.concatenate([(t // GRID).astype(np.float32)[:, None] * inv, (t % GRID).astype(np.float32)[:, None] * inv], -1)
    rope = np.stack([np.cos(ang).T, np.sin(ang).T]).astype(np.float32)
    rope = np.ascontiguousarray(np.concatenate([rope, rope], 1))
    half = ROPE // 2
    turn = np.zeros((DQ, DQ), np.float32)
    for i in range(NOPE, NOPE + half):
        turn[i + half, i], turn[i, i + half] = -1.0, 1.0
    mask = np.zeros((P, 3, KC_), np.float32)
    for n, j in enumerate((0, 1, 3)):
        qc = j * QC + np.arange(QC)
        start = np.clip(qc - NA_COLS // 2, 0, GRID - NA_COLS)
        kc = BAND[j] + np.arange(KC_)
        ok = (kc[None, :] >= start[:, None]) & (kc[None, :] < start[:, None] + NA_COLS)
        mask[:, n, :] = np.tile(np.where(ok, 0.0, NEG), (ROWS, 1))
    return {"k_ident": np.eye(P, dtype=np.float32), "k_alibi": alibi, "k_rope": rope, "k_turn": turn, "k_na_mask": mask}


INS = ["x", "c", "w_mod", "b_mod", "g_norm", "w_ffn1_gu", "w_ffn1_down", "w_ffn2_gu", "w_ffn2_down", "w_in", "w_out",
       "attn_sinks", "lru_conv_w", "lru_conv_b", "lru_gate_a_w", "lru_gate_a_b", "lru_gate_x_w", "lru_gate_x_b",
       "lru_lambda", "sc_conv_w", "g_final", "c_2", "ctx_2", "c_ctx_2", "ada_w_2", "ada_b_2", "ln1_g_2", "ln1_b_2",
       "ln2_g_2", "ln2_b_2", "ffn_w_in_2", "ffn_conv_w_2", "ffn_conv_b_2", "ffn_w_out_2", "mla_w_in_2",
       "mla_q_norm_2", "mla_kv_norm_2", "mla_w_qb_2", "mla_w_kvb_2", "mla_w_o_2", "na_w_qkv_2", "na_rpb_2", "na_w_o_2"]
UNUSED = ["diff_w_qkv_2", "diff_lambda_2", "diff_subln_2", "diff_w_o_2", "swa_w_qkv_2", "swa_sinks_2", "swa_w_o_2"]


def kernel(**inputs):
    import numpy as _np
    import concourse.bacc as _bacc
    from concourse import mybir as _mybir
    from concourse.bass_utils import run_bass_kernel_spmd as _run

    nc = _bacc.Bacc("TRN2", target_bir_lowering=False, num_devices=1)
    arrays, aps = {}, {}
    given = {name: _np.ascontiguousarray(inputs[name]) for name in INS}
    for name, a in {**given, **constants()}.items():
        arrays[f"in_{name}_dram"] = a
        aps[name] = nc.dram_tensor(f"in_{name}_dram", a.shape, _mybir.dt.from_np(a.dtype), kind="ExternalInput").ap()
    out = nc.dram_tensor("out_0_dram", (1, S, D), _mybir.dt.float32, kind="ExternalOutput").ap()
    build(nc, aps, out)
    r = _run(nc, [arrays], core_ids=[0])
    return r.results[0]["out_0_dram"]
```

```python
import numpy as np

import concourse.bass as bass
from concourse import mybir

F32 = mybir.dt.float32
F32R = mybir.dt.float32r
ACT = mybir.ActivationFunctionType
ALU = mybir.AluOpType
AX_X = mybir.AxisListType.X
ds = bass.ds

P = 128
D = 1024
S = 512
C = 256
KD = D // P
DEPTH = 2
FF = 2816
FC = FF // P
HALVES = ((0, 12), (12, FC - 12))
GP = 256
MOD_PANELS = 9 * D // GP
ADA_PANELS = 6 * D // GP
G_ADA = DEPTH * MOD_PANELS
G_ALL = G_ADA + DEPTH * ADA_PANELS
CTX_COL = 2 * G_ALL
MOD_COLS = CTX_COL + 2 * DEPTH * ADA_PANELS
NQ, HD = 8, 64
EPS_RMS, EPS_LN = 1e-6, 1e-5
ALPHA = (2.0 * DEPTH) ** 0.25
NEG = -1e30
PROLOGUE = 8
T = C + S
NH = 16
PER = 4
LQ, LKV, NOPE, ROPE = 384, 256, 64, 32
DQ = NOPE + ROPE
GRID, NA_ROWS, NA_COLS, QC, KC_ = 64, 8, 16, 16, 32
ROWS = S // GRID
WIDE = QC + KC_
BAND = [min(max(j * QC - NA_COLS // 2, 0), GRID - KC_) for j in range(GRID // QC)]


class Counts:

    def __init__(self):
        self.at = {}

    def __getitem__(self, name):
        return self.at.get(name, 0)

    def add(self, more):
        for name, n in more.items():
            self.at[name] = self.at.get(name, 0) + n


class Chain:

    def __init__(self, eng, sem):
        self.eng, self.sem, self.n = eng, sem, 0

    def step(self, ins):
        ins.then_inc(self.sem, 1)
        self.n = self.n + 1
        return self.n

    def wait(self, value):
        self.eng.wait_ge(self.sem, value)

    def link(self, ins):
        self.wait(self.step(ins))

    def loop(self, count, per, body):
        start = self.n
        if count > 1:
            with self.eng.Fori(0, count - 1) as i:
                self.n = start + i * per
                body(i, False)
        self.n = start + (count - 1) * per
        body(count - 1, True)
        assert self.n == start + count * per, (self.n - start - (count - 1) * per, per)


def vector_rows(a):
    def rows(ap, pattern, **kw):
        return ap.rearrange(pattern, q=P, **kw)

    return [
        ("c", rows(a["c"], "a (k q) -> (a k) q")),
        ("c_2", rows(a["c_2"], "a (k q) -> (a k) q")),
        ("c_ctx", rows(a["c_ctx_2"], "(k q) -> k q")),
        ("b_mod", rows(a["b_mod"], "l (k q) -> (l k) q")),
        ("ada_b", rows(a["ada_b_2"], "l (k q) -> (l k) q")),
        ("g_norm", rows(a["g_norm"], "l s (k q) -> (l s k) q")),
        ("g_final", rows(a["g_final"], "(k q) -> k q")),
        ("ln1_g", rows(a["ln1_g_2"], "l (k q) -> (l k) q")),
        ("ln1_b", rows(a["ln1_b_2"], "l (k q) -> (l k) q")),
        ("ln2_g", rows(a["ln2_g_2"], "l (k q) -> (l k) q")),
        ("ln2_b", rows(a["ln2_b_2"], "l (k q) -> (l k) q")),
        ("fconv_w", rows(a["ffn_conv_w_2"], "l t (k q) -> (l t k) q")),
        ("fconv_b", rows(a["ffn_conv_b_2"], "l (k q) -> (l k) q")),
        ("lconv_w", rows(a["lru_conv_w"], "l t (k q) -> (l t k) q")),
        ("lconv_b", rows(a["lru_conv_b"], "l (k q) -> (l k) q")),
        ("gate_a_b", rows(a["lru_gate_a_b"], "l (k q) -> (l k) q")),
        ("gate_x_b", rows(a["lru_gate_x_b"], "l (k q) -> (l k) q")),
        ("lam", rows(a["lru_lambda"], "l (k q) -> (l k) q")),
        ("sconv_w", rows(a["sc_conv_w"], "l t (k q) -> (l t k) q")),
        ("q_norm", rows(a["mla_q_norm_2"], "l (k q) -> (l k) q")),
        ("kv_norm", rows(a["mla_kv_norm_2"], "l (k q) -> (l k) q")),
    ]


def weight_panels(w):
    return w.rearrange("(k p) n -> p k n", p=P)


def gu_step(w, half, norm_first, gemv, conv=None, N=S, ctx=False):
    k0, n = HALVES[half]
    wp = weight_panels(w)
    return dict(kind="gu", iters=n // 2, shapes=[(KD, 2 * P)] * 2, n=n, wait_h=norm_first, gemv=gemv, conv=conv, k0=k0, N=N, ctx=ctx,
                dma=lambda i, j: [(None, wp[:, :, ds((j if conv is None else 1 - j) * FF + k0 * P + (i * 2 if j else i) * (P if j else 2 * P), 2 * P)])],
                totals=dict(g_read=n // 2, product=n // 2, hid_hi=n // 2, hid_lo=n // 2,
                            g_affine=n // 2 if conv is not None else 0, g_conv=n // 2 if conv is not None else 0,
                            u_affine=n // 2 if conv is not None else 0))


SUMS = {None: {}, "square": dict(squared=KD, square_summed=1), "mean": dict(mean_summed=1)}


def dn_step(w, half, gate, gemv, N=S, ctx=False, sums=None):
    k0, nk = HALVES[half]
    wp = weight_panels(w)
    return dict(kind="dn", iters=KD // 2, shapes=[(nk, P)] * 2, nk=nk, gate=gate, gemv=gemv, N=N, ctx=ctx, sums=sums,
                dma=lambda i, j: [(None, wp[:, k0:k0 + nk, ds(j * P + i * (2 * P), P)])],
                totals=dict(down0=KD // 2, down1=KD // 2, **SUMS[sums]))


def proj_step(dma, gate, gemvs=(), ctx_gate=None, sums=None, order=tuple(range(KD))):
    return dict(kind="proj", iters=2, shapes=[(KD, 2 * P)] * 2, gate=gate, gemvs=list(gemvs), ctx_gate=ctx_gate, sums=sums, order=order, N=S, ctx=False,
                dma=dma, totals=dict(proj0=2, proj1=2, **SUMS[sums]))


def mods_of(l):
    m, cm = (lambda k: 2 * G_ADA + l * 2 * ADA_PANELS + k * KD), (lambda k: CTX_COL + l * 2 * ADA_PANELS + k * KD)
    return mods_step(G_ADA + (l + 1) * ADA_PANELS, [(m(0), m(6), m(0)), (cm(0), cm(6), m(0))], None,
                     plus=[(m(1), None), (m(4), None), (cm(1), None), (cm(4), None)])


def plan_block2(a, col):
    steps = []
    for l in range(DEPTH):
        m = lambda k: 2 * G_ADA + l * 2 * ADA_PANELS + k * KD
        cm = lambda k: CTX_COL + l * 2 * ADA_PANELS + k * KD
        wo = weight_panels((a["mla_w_o_2"] if l == 0 else a["na_w_o_2"])[0])
        w_gu, w_dn = a["ffn_w_in_2"][l], a["ffn_w_out_2"][l]
        conv = (col["fconv_w"] + l * 3 * 2 * FC, col["fconv_b"] + l * 2 * FC)
        ln = lambda n, p: col[f"ln{n}_{p}"] + l * KD
        if l == 0:
            steps += [norm_step("rms_x", col["g_final"], then=(m(1), m(0)), fused=True),
                      mla_in_step(a), mla_step(a),
                      dict(kind="gather", ctx=True, totals=dict(h_hi=16, h_ready=16)),
                      dict(kind="alpha", ctx=False, totals={}), dict(kind="alpha", ctx=True, totals={})]
        else:
            steps += [na_step(a), dict(kind="gather", ctx=False, totals=dict(h_hi=8, h_ready=8)),
                      dict(kind="alpha", ctx=False, totals={})]
        steps += [proj_step(lambda i, j, wo=wo: [(None, wo[:, :, ds(j * 2 * P + i * (4 * P), 2 * P)])], m(2),
                            range(96, 101) if l == 0 else (), cm(2) if l == 0 else None, sums="mean"),
                  norm_step("ln_x", ln(1, "g"), ln(1, "b"), then=(m(4), m(3)), fused=True),
                  dict(kind="alpha", ctx=False, totals={})]
        g = (101, 107, 111, 116) if l == 0 else (None,) * 4
        steps += [gu_step(w_gu, 0, True, g[0], conv), dn_step(w_dn, 0, m(5), g[1]),
                  gu_step(w_gu, 1, False, g[2], conv), dn_step(w_dn, 1, m(5), g[3], sums="mean")]
        if l == 1:
            steps += [norm_step("ln_x", ln(2, "g"), ln(2, "b"), fused=True)]
        else:
            m1, cm1 = (lambda k: m(k) + 2 * ADA_PANELS), (lambda k: cm(k) + 2 * ADA_PANELS)
            steps += [mods_of(1), norm_step("ln_x", ln(2, "g"), ln(2, "b"), fused=True, then=(m1(1), m1(0)))]
            steps += [norm_step("ln_x", ln(1, "g"), ln(1, "b"), N=C, ctx=True, then=(cm(4), cm(3)), dst="c0"), dict(kind="alpha", ctx=True, totals={}),
                      gu_step(w_gu, 0, True, None, conv, C, True), dn_step(w_dn, 0, cm(5), None, C, True),
                      gu_step(w_gu, 1, False, None, conv, C, True),
                      dn_step(w_dn, 1, cm(5), None, C, True, sums="mean"),
                      norm_step("ln_x", ln(2, "g"), ln(2, "b"), N=C, ctx=True, then=(cm1(1), cm1(0)), fused=True, dst="ch")]
    return steps


def mla_in_step(a):
    wp = weight_panels(a["mla_w_in_2"][0])
    spans = [(0, 256), (256, 512), (512, 640), (LQ + LKV + ROPE - DQ, LQ + LKV + ROPE)]
    return dict(kind="mla_in", iters=1, shapes=[(KD, hi - lo) for lo, hi in spans],
                dma=lambda i, j: [(None, wp[:, :, spans[j][0]:spans[j][1]])],
                totals=dict(low_out=4, low_sq=5, low_sum=2, low_dev=2, low_full=5, low_hi=5, low_lo=5,
                            pe_rot=1, pe_key=1, rope_in=48))


def mla_step(a):
    wq, wkv = weight_panels(a["mla_w_qb_2"][0]), weight_panels(a["mla_w_kvb_2"][0])
    units = PER * 6
    n = NH // PER
    return dict(kind="mla", iters=n, shapes=[(3, PER * DQ), (2, PER * P)],
                dma=lambda i, j: [(None, (wq, wkv)[j][:, :, ds(i * (PER * (DQ, P)[j]), PER * (DQ, P)[j])])],
                totals=dict(head_mm=4 * n, head_out=4 * n, q_rot=n, s_made=units * n, s_max=units * n, s_exp=units * n,
                            turned0=units * n, turned1=4 * PER * n, copied0=units * n, copied1=4 * PER * n,
                            s_weighted=units * n, s_shared=units * n, s_kept=PER * n))


def na_step(a):
    w = weight_panels(a["na_w_qkv_2"][0])
    units = PER * 4
    n = NH // PER
    halves = [(0, KD), (0, KD // 2), (KD // 2, KD), (0, KD)]
    part = (0, 2, 2, 1)
    return dict(kind="na", iters=n, shapes=[(k1 - k0, 2 * P) for k0, k1 in halves],
                dma=lambda i, j: [(None, w[:, halves[j][0]:halves[j][1], ds(part[j] * D + i * (2 * P), 2 * P)])],
                totals=dict(n_out=n, key_mm=n, keys_out=2 * n, bias_in0=PER // 2 * n * 16 * ROWS, bias_in1=PER // 2 * n * 16 * ROWS,
                            bias_made=units * n, na_mask=16, band_in=n * 16 * 4 * ROWS, s_biased=units * n,
                            s_made=units * n, s_max=units * n, s_exp=units * n, turned0=units * n, turned1=units * n,
                            copied0=units * n, copied1=units * n, s_weighted=units * n, s_shared=units * n, s_kept=PER // 2 * n))


def norm_step(mode, A, B=None, N=S, ctx=False, dst="h", then=None, fused=False):
    tot = {}
    if mode != "mod_h":
        tot.update(deviation=1)
    if mode == "ln_x":
        tot.update(centred=KD)
    if mode != "mod_h" and not (fused and mode != "ln_x"):
        tot.update(SUMS["square"])
    if mode == "ln_x" and not fused:
        tot.update(SUMS["mean"])
    if mode in ("rms_x", "ln_x"):
        tot.update(x_new=KD)
    if mode in ("rms_h", "mod_h") or then:
        tot.update(h_full=KD, h_hi=KD, h_ready=KD)
    return dict(kind="norm", mode=mode, A=A, B=B, N=N, ctx=ctx, dst=dst, then=then, fused=fused, totals=tot)


def mods_step(need, lo, hi, plus=(), half=()):
    return dict(kind="mods", need=need, spans=[(lo, hi, lo)] if isinstance(lo, int) else lo, plus=plus, half=half, totals={})


def plan_block1(a, col):
    steps = [dict(kind="load", totals=dict(row_tile=7, row_col=7, x_tr=KD, x_in=KD, c_act=1, **SUMS["square"])),
             dict(kind="prologue", gemvs=range(PROLOGUE), totals={})]
    M = 2 * MOD_PANELS
    for l in range(DEPTH):
        m = lambda k: l * M + k * KD
        gn = lambda s: col["g_norm"] + (l * 3 + s) * KD
        w_gu, w_dn = (a["w_ffn1_gu"][l], a["w_ffn2_gu"][l]), (a["w_ffn1_down"][l], a["w_ffn2_down"][l])
        free = [(8, 14, 18, 23), (55, 61, 65, None)][l]
        steps += [mods_step(l * MOD_PANELS + 8, m(0), m(2), plus=[(m(1), gn(0))]),
                  norm_step("rms_h", m(1), m(0), fused=True)] + [
                  gu_step(w_gu[0], 0, True, free[0]),
                  mods_step(l * MOD_PANELS + 12, m(2), m(3), half=[m(2)]),
                  dn_step(w_dn[0], 0, m(2), free[1])]
        if l == 0:
            steps += [dict(kind="context", totals=dict(hc_tr=KD, hc_in=KD))]
        steps += [
                  gu_step(w_gu[0], 1, False, free[2]),
                  dn_step(w_dn[0], 1, m(2), free[3], sums="square"),
                  mods_step(l * MOD_PANELS + 24, m(3), m(6), plus=[(m(4), gn(1))]),
                  norm_step("rms_h", m(4), m(3), fused=True),
                  mixer_step(a, l, [range(27, 32), range(70, 76)][l]),
                  proj_step(mixer_out_dma(a["w_out"][l]), m(5), [range(32, 36), range(76, 81)][l], sums="square", order=(4, 5, 6, 7, 0, 1, 2, 3)),
                  mods_step(l * MOD_PANELS + 36, m(6), m(9), plus=[(m(7), gn(2))], half=[m(8)]),
                  norm_step("rms_h", m(7), m(6), fused=True)]
        free = [(36, 42, 46, 51), (81, 87, 91, None)][l]
        steps += [gu_step(w_gu[1], 0, True, free[0]),
                  dn_step(w_dn[1], 0, m(8), free[1]),
                  gu_step(w_gu[1], 1, False, free[2]),
                  ]
        if l == DEPTH - 1:
            steps += [mods_of(0), norm_step("mod_h", CTX_COL + KD, CTX_COL, N=C, ctx=True, dst="c0")]
        steps += [dn_step(w_dn[1], 1, m(8), free[3], sums="square")]
    return steps


def mixer_step(a, l, gemvs):
    wp = weight_panels(a["w_in"][l])
    starts = [768, 1024, 1536, 1792, 1280, 512]

    def dma(i, j):
        if j < 6:
            return [(None, wp[:, :, starts[j]:starts[j] + 2 * P])]
        out = []
        for c in range(2):
            for g in range(2):
                head = g * 4 + 2 * (j - 6) + c
                out.append((("cols", (2 * c + g) * HD, HD), wp[:, :, head * HD:head * HD + HD]))
        return out

    return dict(kind="mixer", iters=1, shapes=[(KD, 2 * P)] * 8, dma=dma, l=l, gemvs=list(gemvs), w=a["w_in"][l],
                totals=dict(in_evac=8, lconv=2, gates_mm=2, gates_r=2, gates_i=2, lru_t=1, lru_m=1, lru_q=1, lru_h=1,
                            gelu=1, y_lru=1, y_sc=1, lam_in=1, lam_exp=1, at_s_read=8, at_s=8, at_max=8, at_exp=8, at_p=8, at_t0=8, at_t1=8, at_pt0=8, at_pt1=8,
                            at_o=8, y_at=4, h_hi=8, h_ready=8, misc_in=160))


def mixer_out_dma(w):
    wp = weight_panels(w)
    heads = w[0:512, :].rearrange("(g i d) n -> d g i n", g=2, d=HD)

    def dma(i, j):
        c = ds(j * 2 * P + i * (4 * P), 2 * P)
        return [(("k", 4, 8, 0, P), wp[:, 4:8, c]),
                (("k", 0, 4, 0, HD), heads[:, 0, :, c]),
                (("k", 0, 4, HD, P), heads[:, 1, :, c])]
    return dma


def build(nc, a, out, upto=99, probe=False):
    rows = vector_rows(a)
    col, at = {}, 0
    for name, ap in rows:
        col[name] = at
        at += ap.shape[0]
    n_rows = at
    row_tiles = -(-n_rows // P)
    assert row_tiles == 7 and col["ada_b"] == col["b_mod"] + 2 * G_ADA
    PLAN = (plan_block1(a, col) + plan_block2(a, col))[:upto]
    PLAN.append(dict(kind="store", probe=probe, totals=dict(o_tr=4, o_out=4)))

    n_panels, n_gemvs, raw_count = 0, 0, [0, 0]
    for st in PLAN:
        st["shapes"] = st.get("shapes", [])
        st["iters"] = st.get("iters", 0)
        st["p0"] = n_panels
        st["raw0"] = tuple(raw_count)
        st["n_dma"] = [len(st["dma"](0, j)) for j in range(len(st["shapes"]))]
        for j, n in enumerate(st["n_dma"]):
            raw_count[j % 2] += 16 * n * st["iters"]
        n_panels += len(st["shapes"]) * st["iters"]
        if st["kind"] == "mods":
            assert n_gemvs >= st["need"], (n_gemvs, st["need"])
            st["need"] = n_gemvs
        n_gemvs += len(st.get("gemvs", ())) + (st["iters"] if st.get("gemv") is not None else 0)
    streams = [st for st in PLAN if st["shapes"]]
    for st, following in zip(streams, streams[1:] + [None]):
        st["following"] = following
    totals = Counts()
    for st in PLAN:
        st["base"] = Counts()
        st["base"].add(totals.at)
        totals.add(st["totals"])

    base = (nc.sbuf_base + 63) // 64 * 64
    place = [0]

    def sb(name, shape, dt=F32, at=None):
        size = 4 * int(np.prod(shape[1:]))
        off = place[0] if at is None else at
        if at is None:
            place[0] += -(-size // 32) * 32
        assert base + off + size <= nc.sbuf_usable_end, (name, base + off + size, nc.sbuf_usable_end)
        return nc.alloc_sbuf_tensor_at(name, shape, dt, offset=base + off)

    x = sb("x", [P, KD * S])
    hc = sb("hc", [P, KD * C])
    h_at = place[0]
    h_hi = sb("h_hi", [P, KD * S], F32R)
    h_lo = sb("h_lo", [P, KD * S], F32R)
    raw = sb("raw", [P, 2, 2048])
    w_hi = sb("w_hi", [P, 2, 2048], F32R)
    w_lo = sb("w_lo", [P, 2, 2048], F32R)
    g_raw_at = place[0]
    g_raw = sb("g_raw", [P, 2, KD, GP])
    acc = sb("acc", [P, 2, GP])
    hid = place[0]
    hid_hi = sb("hid_hi", [P, 12 * S], F32R)
    hid_lo = sb("hid_lo", [P, 12 * S], F32R)
    tmp = place[0]
    gate_t = sb("gate_t", [P, 2, S])
    prod_t = sb("prod_t", [P, 2, S])
    squares = sb("squares", [P, 8, S], at=tmp)
    unit_t = sb("unit_t", [P, 2, S])
    full_t = sb("full_t", [P, 2, S])
    rstd = sb("rstd", [P, S])
    modc = sb("modc", [P, MOD_COLS])
    colv = sb("colv", [P, row_tiles * P])
    c_col = sb("c_col", [P, 3 * KD])
    ident = sb("ident", [P, P])
    mean_m = sb("mean_m", [P, P])
    ones = sb("ones", [P, 1])
    eps = sb("eps", [P, 2])
    spare = place[0]
    row_in = sb("row_in", [P, row_tiles, P], at=hid)
    x_rows = sb("x_rows", [P, 4, D], at=hid + 4096)
    c_rows = sb("c_rows", [P, 2, D], at=g_raw_at + 8192)
    x_out = sb("x_out", [P, 4, D], at=hid)
    mq = sb("mq", [P, 4, S], at=hid)
    mk = sb("mk", [P, S], at=hid + 8192)
    mv = sb("mv", [P, 4, P], at=hid + 10240)
    lx = sb("lx", [P, 2, S], at=hid + 12288)
    lg = sb("lg", [P, 2, S], at=hid + 16384)
    sbt = sb("sbt", [P, 2, S], at=hid + 20480)
    sct = sb("sct", [P, 2, S], at=hid + 24576)
    sxt = sb("sxt", [P, 2, S], at=hid + 28672)
    alibi = sb("alibi", [P, NQ, 2 * P], at=hid + 32768)
    att = sb("att", [P, 2, 4, 2 * P], at=hid + 40960)
    att_t = sb("att_t", [P, 2, 8, P], at=spare)
    accs = (acc, sb("acc_1", [P, 2, GP], at=spare + 4096))
    diags = sb("diags", [P, 2, 4, P], at=tmp + 8192)
    cx = sb("cx", [P, 2, S], at=tmp)
    ga = sb("ga", [P, 2, S], at=tmp + 4096)
    gx = sb("gx", [P, 2, S], at=tmp + 8192)
    lt = sb("lt", [P, 2, S], at=tmp + 12288)
    gate_w = sb("gate_w", [P, 2, 2, P], at=spare + 8192)
    small = sb("small", [P, 256], at=spare + 10240)
    sinks = small[:, 0:NQ]
    lsp = small[:, 16:16 + 4 * 2]
    sm = lambda k, n=4: small[:, 32 + 4 * k:32 + 4 * k + n]

    low_hi = sb("low_hi", [P, 5, T], F32R, at=hid + 16384)
    low_lo = sb("low_lo", [P, 5, T], F32R, at=hid + 16384 + 15360)
    ch_hi = sb("ch_hi", [P, KD * C], F32R, at=hid)
    ch_lo = sb("ch_lo", [P, KD * C], F32R, at=hid + 8192)
    c0_hi = sb("c0_hi", [P, KD * C], F32R, at=g_raw_at)
    c0_lo = sb("c0_lo", [P, KD * C], F32R, at=g_raw_at + 8192)
    low = sb("low", [P, 5, T], at=hid)
    low_pe = sb("low_pe", [P, T], at=tmp)
    low_squares = (sb("low_squares_q", [P, 3, T], at=spare), sb("low_squares_kv", [P, 2, T], at=hid + 16384 + 15360 + 9216))
    low_rstd = (sb("low_rstd_q", [P, T], at=spare + 9216), sb("low_rstd_kv", [P, T], at=tmp + 14336))
    q_flat = sb("q_flat", [P, PER, S], at=h_at)
    q_turn = sb("q_turn", [P, PER, S], at=h_at + 8192)
    q_ctx = sb("q_ctx", [P, PER, C], at=h_at + 16384)
    keys = sb("keys", [P, PER, T], at=h_at + 20480)
    vals = sb("vals", [P, 6, PER * HD], at=g_raw_at)
    diag = sb("diag", [P, 2, P], at=g_raw_at + 9216)
    prob_t = sb("prob_t", [P, 2, T], at=spare)
    prob = sb("prob", [P, 2, T], at=spare + 6144)
    o_lat = sb("o_lat", [P, KD, S], at=hid)
    o_ctx = sb("o_ctx", [P, KD, C], at=tmp)
    oc_hi = sb("oc_hi", [P, KD * C], F32R, at=hid + 16384)
    oc_lo = sb("oc_lo", [P, KD * C], F32R, at=hid + 16384 + 8192)
    turns = sb("turns", [P, 2, S], at=tmp + 8192)
    turned = sb("turned", [P, S], at=tmp + 12288)
    turn_m = sb("turn_m", [P, DQ], at=spare + 12288)
    stat = sb("stat", [P, 96], at=spare + 12288 + 384)
    nq = sb("nq", [P, 2, S], at=g_raw_at)
    nk = sb("nk", [P, 2, T], at=g_raw_at + 4096)
    nv = sb("nv", [P, 6, PER * HD], at=spare)
    nvb = sb("nvb", [P, 4, 2, PER * HD], at=tmp + 4096)
    on_lat = sb("on_lat", [P, KD, S], at=hid + 16384)
    prob_n = sb("prob_n", [P, 2, S], at=hid + 32768)
    bias_m = sb("bias_m", [P, 4, ROWS, KC_], at=hid + 36864)
    prob_nt = sb("prob_nt", [P, 2, S], at=hid + 40960)
    diag_n = sb("diag_n", [P, 2, P], at=hid + 45056)
    bias_w = sb("bias_w", [P, 2, ROWS, WIDE], at=tmp)
    na_mask = sb("na_mask", [P, 3, KC_], at=tmp + 3072)
    table = sb("table", [8 * 15, 2, 64], at=spare)
    wide = nc.dram_tensor("bias_rows", [QC, NH * 15 * WIDE], F32, kind="Internal").ap()

    ps_all = nc.alloc_psum_tensor("ps_all", [P, 8, S], F32)
    ps_g, ps_u, ps_d = ps_all[:, 0:2, :], ps_all[:, 2:4, :], ps_all[:, 4:6, :]
    ps_mod, ps_s = ps_all[:, 6, :], ps_all[:, 7, :]

    names = sorted(set(totals.at) | {"raw_in0", "raw_in1", "w_split_hi", "w_split_lo", "panel_used",
                                     "gemv_in0", "gemv_in1", "gemv_done", "gemv_reduced", "rows_in", "const_in", "x_rows_in", "c_rows_in",
                                     "consts", "act_chain", "dve_chain", "pool_chain", "stored", "table_in", "table_zero", "table_scaled", "wide_in"})
    sem = {n: nc.alloc_semaphore(n) for n in names}

    def src(st):
        return (hc, C) if st["ctx"] else (x, S)

    def dst_of(st):
        return {"ch": (ch_hi, ch_lo), "c0": (c0_hi, c0_lo), "h": (h_hi, h_lo)}[st["dst"]]

    def half_of(gemvs, i):
        return gemvs[i * len(gemvs) // 2:(i + 1) * len(gemvs) // 2]

    def w_view(t, slot, shape):
        nk, n = shape
        return t[:, slot, 0:nk * n].rearrange("p (k n) -> p k n", n=n)

    def ahead(st, i, j, last):
        per = len(st["shapes"])
        if j + 2 < per:
            return st, i, j + 2
        if not last:
            return st, i + 1, j + 2 - per
        f = st["following"]
        return (f, 0, j + 2 - per) if f is not None else None

    def number(st, i, j):
        return st["p0"] + i * len(st["shapes"]) + j

    def raw_need(st, i, j):
        per = 16 * sum(st["n_dma"][j % 2::2])
        upto = 16 * sum(st["n_dma"][j % 2:j + 1:2])
        return st["raw0"][j % 2] + i * per + upto

    block_cm = nc.Block()
    block = block_cm.__enter__()

    @block.sync
    def _(sp):
        def load_panel(st, i, j):
            parts = st["dma"](i, j)
            if not (st["p0"] == 0 and isinstance(i, int) and i == 0 and j < 2):
                sp.wait_ge(sem["w_split_lo"], number(st, i, j) - 1)
            for where, ap in parts:
                dst = w_view(raw, j % 2, st["shapes"][j])
                if where and where[0] == "cols":
                    dst = dst[:, :, where[1]:where[1] + where[2]]
                elif where and where[0] == "k":
                    dst = dst[where[3]:where[4], where[1]:where[2], :]
                sp.dma_start(dst, ap).then_inc(sem[f"raw_in{j % 2}"], 16)

        def gemv_ap(g, i=0):
            if g < G_ADA:
                l, w = g // MOD_PANELS, a["w_mod"]
                off = (g % MOD_PANELS) * GP
            else:
                l, w = (g - G_ADA) // ADA_PANELS, a["ada_w_2"]
                off = ((g - G_ADA) % ADA_PANELS) * GP
            return weight_panels(w[l])[:, :, ds(off + i * GP, GP)]

        for t in range(row_tiles):
            for name, ap in rows:
                lo, hi = max(col[name], t * P), min(col[name] + ap.shape[0], (t + 1) * P)
                if lo < hi:
                    sp.dma_start(row_in[lo - t * P:hi - t * P, t, :], ap[lo - col[name]:hi - col[name], :]).then_inc(sem["rows_in"], 16)
        sp.dma_start(ident[:, :], a["k_ident"]).then_inc(sem["const_in"], 16)

        def load_tokens(name, dst, sem_name):
            sp.dma_start(dst[:, :, :], a[name][0].rearrange("(t p) n -> p t n", p=P)).then_inc(sem[sem_name], 16)

        def load_biases():
            sp.wait_ge(sem["table_zero"], 1)
            for t in range(2):
                sp.dma_start(table[:, t, 16:47], a["na_rpb_2"][0].rearrange("h m n -> (h m) n")[t * 120:(t + 1) * 120, :]).then_inc(sem["table_in"], 16)

        def spread_biases():
            sp.wait_ge(sem["table_scaled"], 1)
            for t in range(2):
                for q in range(QC):
                    sp.dma_start(wide[q, t * 120 * WIDE:(t + 1) * 120 * WIDE].rearrange("(m n) -> m n", n=WIDE), table[:, t, 15 - q:15 - q + WIDE]).then_inc(sem["wide_in"], 16)

        early = None
        for st in PLAN:
            b = st["base"]
            if st["kind"] == "prologue":
                for n, g in enumerate(st["gemvs"]):
                    if g >= 1:
                        sp.wait_ge(sem["gemv_done"], max(g - 1, 0) if n else g)
                    sp.dma_start(g_raw[:, n % 2, :, :], gemv_ap(g)).then_inc(sem[f"gemv_in{n % 2}"], 16)
                    if g == 0:
                        load_tokens("x", x_rows, "x_rows_in")
                    if g in (3, 5):
                        load_panel(streams[0], 0, g // 4)
            elif st["kind"] == "mixer":
                l = st["l"]
                for n in range(2):
                    load_panel(st, 0, n)
                sp.wait_ge(sem["down1"], b["down1"])
                sp.dma_start(alibi[:, :, :], a["k_alibi"]).then_inc(sem["misc_in"], 16)
                sp.dma_start(sinks, a["attn_sinks"][l:l + 1, :].broadcast_to([P, NQ])).then_inc(sem["misc_in"], 16)
                for m, name in enumerate(("lru_gate_a_w", "lru_gate_x_w")):
                    for h in range(4):
                        q = HD * (h % 2)
                        sp.wait_ge(sem["consts"], 5)
                        if l:
                            sp.wait_ge(sem["gates_i"], b["gates_i"])
                        sp.dma_start(gate_w[q:q + HD, m, h // 2, q:q + HD], a[name][l, h]).then_inc(sem["misc_in"], 16)
                for n in range(2, max(8, len(st["gemvs"]) + 2)):
                    if n < 8:
                        load_panel(st, 0, n)
                    if 2 <= n < len(st["gemvs"]) + 2:
                        g = st["gemvs"][n - 2]
                        sp.wait_ge(sem["gemv_done"], g)
                        sp.dma_start(g_raw[:, 0, :, :], gemv_ap(g)).then_inc(sem["gemv_in0"], 16)
            elif st["kind"] == "mla_in":
                for j in range(4):
                    load_panel(st, 0, j)
                sp.wait_ge(sem["h_ready"], b["h_ready"])
                sp.dma_start(turns[64:96, 0, :], a["k_rope"][0]).then_inc(sem["rope_in"], 16)
                sp.dma_start(turns[64:96, 1, :], a["k_rope"][1]).then_inc(sem["rope_in"], 16)
                sp.dma_start(turn_m[0:DQ, :], a["k_turn"]).then_inc(sem["rope_in"], 16)
            elif st["kind"] == "na":
                for j in range(4):
                    load_panel(st, 0, j)
                sp.wait_ge(sem["h_ready"], b["h_ready"])
                sp.wait_ge(sem["wide_in"], 16 * 2 * QC)
                sp.dma_start(na_mask[:, :, :], a["k_na_mask"]).then_inc(sem["na_mask"], 16)

                def biases(i, h, first):
                    of_row = lambda row: wide[:, ds((h * 15 + 7 - row) * WIDE + i * (PER * 15 * WIDE), ROWS * WIDE)]
                    source = of_row(0)
                    if h >= 2 or not first:
                        sp.wait_ge(sem["bias_made"], b["bias_made"] + (i * PER + h - 1) * 4)
                    for row in range(ROWS):
                        dst = bias_w[row * QC:(row + 1) * QC, h % 2, :, :].rearrange("q m n -> q (m n)")
                        sp.dma_start(dst, source if row == 0 else of_row(row)).then_inc(sem[f"bias_in{h % 2}"], 16)

                def one(i, first, last):
                    for j in () if first else (2, 3):
                        load_panel(st, i, j)
                    for h in (0, 1):
                        biases(i, h, first)
                    for j in range(2):
                        load_panel(st["following"] if last else st, 0 if last else i + 1, j)
                    sp.wait_ge(sem["n_out"], b["n_out"] + i + 1)
                    for j in range(4):
                        for row in range(ROWS):
                            p0, q0 = (row % 4) * KC_, (row % 2) * GRID + BAND[j]
                            sp.dma_start(nvb[p0:p0 + KC_, j, row // 4, :], nv[q0:q0 + KC_, 2 + row // 2, :]).then_inc(sem["band_in"], 16)
                    for h in (2, 3):
                        biases(i, h, first)
                one(0, True, False)
                with sp.Fori(1, st["iters"] - 1) as i:
                    one(i, False, False)
                one(st["iters"] - 1, False, True)
                early = st["following"]
            elif st["shapes"] and st["kind"] in ("gu", "dn", "proj", "mla"):
                def one(i, g, loaded=False):
                    for j in range(0 if loaded else len(st["shapes"])):
                        load_panel(st, i, j)
                    gemvs = half_of(st["gemvs"], i) if st["kind"] == "proj" else ()
                    for n, gg in enumerate(gemvs):
                        if n == 0:
                            sp.wait_ge(sem["h_ready"], b["h_ready"])
                        slot = (gg - st["gemvs"][0] + 1) % 2
                        sp.wait_ge(sem["gemv_done"], gg - 1)
                        sp.dma_start(g_raw[:, slot, :, :], gemv_ap(gg)).then_inc(sem[f"gemv_in{slot}"], 16)
                    if g is not None:
                        sp.wait_ge(sem["gemv_done"], g + i)
                        sp.dma_start(g_raw[:, 0, :, :], gemv_ap(g, i)).then_inc(sem["gemv_in0"], 16)
                if st["kind"] == "proj":
                    one(0, None, st is early)
                    one(1, None)
                    continue
                start = 0
                if st["p0"] == 0:
                    one(0, st.get("gemv"), True)
                    start = 1
                with sp.Fori(start, st["iters"]) as i:
                    one(i, st.get("gemv"))
                if st["p0"] == 0:
                    load_biases()
                    sp.wait_ge(sem["gemv_done"], PROLOGUE)
                    load_tokens("ctx_2", c_rows, "c_rows_in")
                elif st is streams[1]:
                    spread_biases()
        b = PLAN[-1]["base"]
        for t in range(4):
            sp.wait_ge(sem["o_out"], b["o_out"] + t + 1)
            sp.dma_start(out[0].rearrange("(t p) n -> p t n", p=P)[:, t, :], x_out[:, t, :]).then_inc(sem["stored"], 16)
        sp.wait_ge(sem["stored"], 64)
        sp.wait_ge(sem["wide_in"], 16 * 2 * QC)

    @block.gpsimd
    def _(pool):
        pool.memset(mean_m[:, :], 1.0 / D).then_inc(sem["consts"], 1)
        pool.memset(ones[:, :], 1.0).then_inc(sem["consts"], 1)
        pool.memset(eps[:, 0:1], EPS_RMS).then_inc(sem["consts"], 1)
        pool.memset(eps[:, 1:2], EPS_LN).then_inc(sem["consts"], 1)
        pool.memset(gate_w[:, :, :, :], 0.0).then_inc(sem["consts"], 1)
        pool.memset(table[:, :, :], 0.0).then_inc(sem["table_zero"], 1)

        def split_lo(target):
            if target is None:
                return
            st, i, j = target
            pool.wait_ge(sem["w_split_hi"], number(st, i, j) + 1)
            v = lambda t: w_view(t, j % 2, st["shapes"][j])
            nc.gpsimd.tensor_tensor(v(w_lo), v(raw), v(w_hi).bitcast(F32), ALU.subtract).then_inc(sem["w_split_lo"], 1)

        def h_low(b, n, k, N, full, to):
            hi, lo = to
            pool.wait_ge(sem["h_hi"], b["h_hi"] + n + 1)
            nc.gpsimd.tensor_tensor(lo[:, k * N:(k + 1) * N], full, hi[:, k * N:(k + 1) * N].bitcast(F32),
                                    ALU.subtract).then_inc(sem["h_ready"], 1)

        split_lo((streams[0], 0, 0))
        split_lo((streams[0], 0, 1))
        for st in PLAN:
            b = st["base"]
            if st["kind"] == "norm" and "h_ready" in st["totals"]:
                for k in range(KD):
                    h_low(b, k, k, st["N"], full_t[:, k % 2, 0:st["N"]], dst_of(st))
            elif st["kind"] == "mixer":
                for j in range(6):
                    split_lo(ahead(st, 0, j, True))
                order = [(4, lt[:, 0, :]), (5, lt[:, 1, :]), (6, sxt[:, 0, :]), (7, sxt[:, 1, :])] + [(i, mq[:, i, :]) for i in range(4)]
                for j in (6, 7):
                    split_lo(ahead(st, 0, j, True))
                for n, (k, full) in enumerate(order):
                    h_low(b, n, k, S, full, (h_hi, h_lo))
            elif st["kind"] == "gather":
                for k in range(KD):
                    h_low(b, k, k, S, (o_lat if st["ctx"] else on_lat)[:, k, :], (h_hi, h_lo))
                if st["ctx"]:
                    for k in range(KD):
                        h_low(b, KD + k, k, C, o_ctx[:, k, :], (oc_hi, oc_lo))
            elif st["kind"] == "mla_in":
                for j in range(4):
                    split_lo(ahead(st, 0, j, True))
                for k in range(5):
                    pool.wait_ge(sem["low_hi"], b["low_hi"] + k + 1)
                    nc.gpsimd.tensor_tensor(low_lo[:, k, :], low[:, k, :], low_hi[:, k, :].bitcast(F32), ALU.subtract).then_inc(sem["low_lo"], 1)
            elif st["kind"] == "na":
                pool.wait_ge(sem["na_mask"], 16)

                def one(i, last):
                    for j in range(4):
                        split_lo(ahead(st, i, j, last))
                        h = j
                        pool.wait_ge(sem[f"bias_in{h % 2}"], b[f"bias_in{h % 2}"] + (i * (PER // 2) + h // 2 + 1) * (16 * ROWS))
                        for u in range(4):
                            kind_j = (0, 1, 1, 2)[u]
                            x0 = BAND[u] - u * QC + QC
                            if not (isinstance(i, int) and i * PER + h < 1):
                                pool.wait_ge(sem["s_biased"], b["s_biased"] + i * (4 * PER) + h * 4 + u - 3)
                            nc.gpsimd.tensor_tensor(bias_m[:, u, :, :], bias_w[:, h % 2, :, x0:x0 + KC_],
                                                    na_mask[:, kind_j, :].rearrange("p (o n) -> p o n", o=1).broadcast_to([P, ROWS, KC_]),
                                                    ALU.add).then_inc(sem["bias_made"], 1)
                one(0, False)
                with pool.Fori(1, st["iters"] - 1) as i:
                    one(i, False)
                one(st["iters"] - 1, True)
            elif st["kind"] in ("gu", "dn", "proj", "mla"):
                def one(i, last):
                    for j in range(len(st["shapes"])):
                        split_lo(ahead(st, i, j, last))
                Chain(pool, sem["pool_chain"]).loop(st["iters"], 0, one)
                if st["p0"] == 0:
                    pool.wait_ge(sem["table_in"], 32)
                    nc.gpsimd.tensor_scalar(table[:, :, :], table[:, :, :], HD ** 0.5, None, ALU.mult).then_inc(sem["table_scaled"], 1)

    def mixer_act(st, b, act, split_hi):
        l = st["l"]
        dest = [lx[:, :, :], lg[:, :, :], sct[:, :, :], sxt[:, :, :], sbt[:, :, :], None, mq[:, 0:2, :], mq[:, 2:4, :]]

        def evac(j):
            act.wait_ge(sem["panel_used"], st["p0"] + j + 1)
            pair = (ps_g, ps_u)[j % 2]
            if j == 5:
                nc.scalar.activation(mk[:, :], pair[:, 0, :], ACT.Copy)
                nc.scalar.activation(mv[:, :, :].rearrange("p a b -> p (a b)"), pair[:, 1, :], ACT.Copy).then_inc(sem["in_evac"], 1)
            else:
                nc.scalar.activation(dest[j], pair[:, :, :], ACT.Copy).then_inc(sem["in_evac"], 1)
            split_hi(ahead(st, 0, j, True))

        act.wait_ge(sem["lam_in"], b["lam_in"] + 1)
        nc.scalar.activation(sm(14, 2), sm(17, 2), ACT.Exp).then_inc(sem["lam_exp"], 1)
        evac(0)
        evac(1)
        evac(2)
        bc = lambda name, c: colv[:, col[name] + l * 2 + c:col[name] + l * 2 + c + 1]
        for c in range(2):
            act.wait_ge(sem["gates_mm"], b["gates_mm"] + 1)
            nc.scalar.activation(ga[:, c, :], ps_d[:, c, :], ACT.Sigmoid, bias=bc("gate_a_b", c)).then_inc(sem["gates_r"], 1)
        evac(3)
        evac(4)
        for c in range(2):
            act.wait_ge(sem["gates_mm"], b["gates_mm"] + 2)
            nc.scalar.activation(gx[:, c, :], ps_d[:, c, :], ACT.Sigmoid, bias=bc("gate_x_b", c)).then_inc(sem["gates_i"], 1)
        act.wait_ge(sem["lru_q"], b["lru_q"] + 1)
        act.wait_ge(sem["gates_r"], b["gates_r"] + 2)
        for c in range(2):
            ins = nc.scalar.activation(lt[:, c, :], ga[:, c, :], ACT.Tanh, scale=lsp[:, c:c + 1])
        ins.then_inc(sem["lru_t"], 1)
        act.wait_ge(sem["lru_t"], b["lru_t"] + 1)
        evac(5)
        for c in range(2):
            ins = nc.scalar.activation(ga[:, c, :], ga[:, c, :], ACT.Exp, scale=lsp[:, 4 + c:5 + c])
        ins.then_inc(sem["act_chain"], 1)
        evac(6)
        evac(7)
        act.wait_ge(sem["lru_m"], b["lru_m"] + 1)
        nc.scalar.activation(lt[:, :, :], lt[:, :, :], ACT.Sqrt, scale=2.0)
        nc.scalar.activation(lg[:, :, :], lg[:, :, :], ACT.Gelu_apprx_tanh).then_inc(sem["gelu"], 1)

        def high(n, k, full):
            nc.scalar.activation(h_hi[:, k * S:(k + 1) * S], full, ACT.Copy).then_inc(sem["h_hi"], 1)

        def exps(h):
            q = h % 2
            act.wait_ge(sem["at_max"], b["at_max"] + h + 1)
            nm, es, su = (sm(q * 6 + t) for t in (1, 2, 3))
            nc.scalar.activation(es, nm, ACT.Exp, bias=sinks_col(h))
            for n in range(4):
                ins = nc.scalar.activation(att[:, q, n, :], att[:, q, n, :], ACT.Exp, bias=nm[:, n:n + 1], accum_out=su[:, n:n + 1])
            ins.then_inc(sem["at_exp"], 1)

        exps(0)
        act.wait_ge(sem["y_lru"], b["y_lru"] + 1)
        high(0, 4, lt[:, 0, :])
        high(1, 5, lt[:, 1, :])
        act.wait_ge(sem["y_sc"], b["y_sc"] + 1)
        high(2, 6, sxt[:, 0, :])
        high(3, 7, sxt[:, 1, :])
        for h in range(1, NQ):
            exps(h)
            pt_copy(act, b, h - 1)
        pt_copy(act, b, NQ - 1)

    def sinks_col(h):
        head = h // 2 + 4 * (h % 2)
        return sinks[:, head:head + 1]

    def pt_copy(act, b, h):
        act.wait_ge(sem["at_t0"], b["at_t0"] + h + 1)
        if h >= 2:
            act.wait_ge(sem["at_o"], b["at_o"] + h - 1)
        nc.scalar.activation(att_t[:, h % 2, 0:4, :], ps_d[:, 0, :].rearrange("p (j q) -> p j q", q=P), ACT.Copy).then_inc(sem["at_pt0"], 1)
        if h % 2 == 1:
            i = h // 2
            act.wait_ge(sem["at_o"], b["at_o"] + 2 * i + 2)
            nc.scalar.activation(mq[:, i, :], ps_s[:, :], ACT.Copy).then_inc(sem["y_at"], 1)
            act.wait_ge(sem["y_at"], b["y_at"] + i + 1)
            nc.scalar.activation(h_hi[:, i * S:(i + 1) * S], mq[:, i, :], ACT.Copy).then_inc(sem["h_hi"], 1)

    def mla_in_act(st, b, act, split_hi):
        def evac(k, bank, cbank, c):
            nc.scalar.activation(low[:, k, C:T], bank, ACT.Copy)
            return nc.scalar.activation(low[:, k, 0:C], cbank[:, c * C:(c + 1) * C], ACT.Copy)

        places = [[(0, ps_g[:, 0, :], 0), (1, ps_g[:, 1, :], 1)], [(2, ps_u[:, 0, :], 0), (3, ps_u[:, 1, :], 1)], [(4, ps_g[:, 0, :], 0)]]

        def square(k0, k1):
            act.wait_ge(sem["low_out"], b["low_out"] + (k1 + 1) // 2)
            for k in range(k0, k1):
                n, at = k // 3, k % 3
                nc.scalar.activation(low_squares[n][:, at, :], low[:, k, :], ACT.Square).then_inc(sem["low_sq"], 1)

        def deviation(n):
            act.wait_ge(sem["low_sum"], b["low_sum"] + n + 1)
            pair = ((ps_g[:, 1, :], ps_s[:, 0:C]), (ps_u[:, 1, :], ps_mod[:, 0:C]))[n]
            for o, i_ in zip((low_rstd[n][:, C:T], low_rstd[n][:, 0:C]), pair):
                ins = nc.scalar.activation(o, i_, ACT.Sqrt, scale=float(D) / (LQ, LKV)[n], bias=eps[:, 0:1])
            ins.then_inc(sem["low_dev"], 1)

        for j in range(3):
            act.wait_ge(sem["panel_used"], st["p0"] + j + 1)
            for k, bank, c in places[j]:
                ins = evac(k, bank, ps_d[:, j % 2, :], c)
            ins.then_inc(sem["low_out"], 1)
            split_hi(ahead(st, 0, j, True))
            square(2 * j, min(2 * j + 2, 5))
        deviation(0)
        act.wait_ge(sem["panel_used"], st["p0"] + 4)
        act.wait_ge(sem["rope_in"], 48)
        nc.scalar.activation(low_pe[64:96, C:T], ps_u[64:96, 0, :], ACT.Copy)
        nc.scalar.activation(low_pe[64:96, 0:C], ps_d[64:96, 1, 0:C], ACT.Copy).then_inc(sem["low_out"], 1)
        split_hi(ahead(st, 0, 3, True))
        deviation(1)
        for k in range(5):
            act.wait_ge(sem["low_full"], b["low_full"] + k + 1)
            nc.scalar.activation(low_hi[:, k, :], low[:, k, :], ACT.Copy).then_inc(sem["low_hi"], 1)
        act.wait_ge(sem["low_out"], b["low_out"] + 4)
        for h in range(PER):
            ins = nc.scalar.activation(keys[64:96, h, 0:C], low_pe[64:96, 0:C], ACT.Copy)
        ins.then_inc(sem["act_chain"], 1)

    MLA_UNITS = [(h, ctx, q) for h in range(PER) for ctx, n in ((0, 4), (1, 2)) for q in range(n)]
    MLA_LAT = [sum(1 for u in MLA_UNITS[:n] if not u[1]) for n in range(len(MLA_UNITS))]

    def mla_act(st, b, act, split_hi, i, last):
        base_of = lambda name, per: b[name] + i * per
        U = len(MLA_UNITS)
        act.wait_ge(sem["panel_used"], st["p0"] + i * 2 + 1)
        for h in range(PER):
            nc.scalar.activation(q_ctx[0:DQ, h, :], ps_d[0:DQ, h // 2, (h % 2) * C:(h % 2 + 1) * C], ACT.Copy)
        for h in range(PER):
            ins = nc.scalar.activation(q_flat[0:DQ, h, :], ps_all[0:DQ, h, :], ACT.Copy)
        ins.then_inc(sem["head_out"], 1)
        split_hi(ahead(st, i, 0, last))
        for n, heads in ((0, (2, 3)), (2, (0, 1))):
            act.wait_ge(sem["head_mm"], base_of("head_mm", 4) + n + 1)
            for h in heads:
                ins = nc.scalar.activation(keys[0:NOPE, h, C:T], ps_all[0:NOPE, 4 + h, :], ACT.Copy)
            ins.then_inc(sem["head_out"], 1)
        act.wait_ge(sem["head_mm"], base_of("head_mm", 4) + 4)
        for h in range(PER):
            nc.scalar.activation(keys[0:NOPE, h, 0:C], ps_all[0:NOPE, 6 + h // 2, (h % 2) * C:(h % 2 + 1) * C], ACT.Copy)
        for t in (0, 2, 4):
            if t == 4:
                act.wait_ge(sem["panel_used"], st["p0"] + i * 2 + 2)
            ins = nc.scalar.activation(vals[:, t:t + 2, :], ps_all[:, (2, 3, 4)[t // 2], :].rearrange("p (t n) -> p t n", t=2), ACT.Copy)
        ins.then_inc(sem["head_out"], 1)
        split_hi(ahead(st, i, 1, last))

        def exps(n):
            h, ctx, q = MLA_UNITS[n]
            act.wait_ge(sem["s_max"], base_of("s_max", U) + n + 1)
            if n >= 2:
                act.wait_ge(sem["turned0"], base_of("turned0", U) + n - 1)
                if not MLA_UNITS[n - 2][1]:
                    act.wait_ge(sem["turned1"], base_of("turned1", 4 * PER) + MLA_LAT[n - 2] + 1)
            pair = ps_all[:, 2 * (n % 2):2 * (n % 2) + 2, :].rearrange("p b n -> p (b n)")
            W = C if ctx else T
            nc.scalar.activation(prob[:, n % 2, 0:W], pair[:, C:C + W], ACT.Exp, scale=DQ ** -0.5,
                                 bias=stat[:, 4 * (n % 2) + 1:4 * (n % 2) + 2], accum_out=stat[:, 4 * (n % 2) + 2:4 * (n % 2) + 3]).then_inc(sem["s_exp"], 1)

        def copy(n):
            h, ctx, q = MLA_UNITS[n]
            act.wait_ge(sem["turned0"], base_of("turned0", U) + n + 1)
            if n >= 2:
                act.wait_ge(sem["s_weighted"], base_of("s_weighted", U) + n - 1)
            W = (2 if ctx else 3) * P
            nc.scalar.activation(prob_t[:, n % 2, 0:W], ps_all[:, 4, 0:W], ACT.Copy).then_inc(sem["copied0"], 1)

        def keep(n):
            h, ctx, q = MLA_UNITS[n]
            act.wait_ge(sem["s_weighted"], base_of("s_weighted", U) + n + 1)
            N, to = (C, o_ctx) if ctx else (S, o_lat)
            nc.scalar.activation(to.rearrange("p k n -> p (k n)")[:, ds(i * (2 * N) + (h // 2) * N, N)], ps_all[:, 6 + ctx, 0:N], ACT.Copy).then_inc(sem["s_kept"], 1)

        exps(0)
        for n in range(U):
            if n + 1 < U:
                exps(n + 1)
            copy(n)
            if n >= 2 and MLA_UNITS[n - 2][0] % 2 and MLA_UNITS[n - 2][1:] in ((0, 3), (1, 1)):
                keep(n - 2)
        keep(U - 1)

    NA_UNITS = [(h, j) for h in range(PER) for j in range(4)]

    def na_act(st, b, act, split_hi, i, last):
        base_of = lambda name, per: b[name] + i * per
        U = len(NA_UNITS)
        act.wait_ge(sem["panel_used"], st["p0"] + i * 4 + 1)
        for c in range(2):
            nc.scalar.activation(nq[:, c, :].rearrange("p (j r q) -> p r j q", j=GRID // QC, q=QC),
                                 ps_g[:, c, :].rearrange("p (r j q) -> p r j q", j=GRID // QC, q=QC), ACT.Copy)
        split_hi(ahead(st, i, 0, last))
        split_hi(ahead(st, i, 1, last))
        act.wait_ge(sem["panel_used"], st["p0"] + i * 4 + 3)
        for t in (0, 2, 4):
            ins = nc.scalar.activation(nv[:, t:t + 2, :], ps_all[:, 5 + t // 2, :].rearrange("p (t n) -> p t n", t=2), ACT.Copy)
        ins.then_inc(sem["n_out"], 1)
        split_hi(ahead(st, i, 2, last))
        for c in range(2):
            if c:
                act.wait_ge(sem["panel_used"], st["p0"] + i * 4 + 4)
            else:
                act.wait_ge(sem["key_mm"], base_of("key_mm", 1) + 1)
            nc.scalar.activation(nk[:, c, 0:C], ps_all[:, 4, c * C:(c + 1) * C], ACT.Copy)
            nc.scalar.activation(nk[:, c, C:T], ps_u[:, c, :], ACT.Copy).then_inc(sem["keys_out"], 1)
        split_hi(ahead(st, i, 3, last))

        def exps(n):
            act.wait_ge(sem["s_max"], base_of("s_max", U) + n + 1)
            if n >= 2:
                act.wait_ge(sem["turned1"], base_of("turned1", U) + n - 1)
            nc.scalar.activation(prob_n[:, n % 2, :], ps_all[:, n % 4, :], ACT.Exp, scale=HD ** -0.5,
                                 bias=stat[:, 4 * (n % 4) + 1:4 * (n % 4) + 2], accum_out=stat[:, 4 * (n % 4) + 2:4 * (n % 4) + 3]).then_inc(sem["s_exp"], 1)

        def copy(n):
            act.wait_ge(sem["turned0"], base_of("turned0", U) + n + 1)
            if n >= 2:
                act.wait_ge(sem["s_weighted"], base_of("s_weighted", U) + n - 1)
            nc.scalar.activation(prob_nt[:, n % 2, 0:C], ps_all[:, 4, 0:C], ACT.Copy).then_inc(sem["copied0"], 1)

        def keep(n):
            h, j = NA_UNITS[n]
            act.wait_ge(sem["s_weighted"], base_of("s_weighted", U) + n + 1)
            to = on_lat.rearrange("p k n -> p (k n)")[:, ds(i * (2 * S) + (h // 2) * S, S)]
            nc.scalar.activation(to.rearrange("p (r j q) -> p r j q", j=GRID // QC, q=QC),
                                 ps_all[:, 6 + h // 2, :].rearrange("p (j r q) -> p r j q", j=GRID // QC, q=QC), ACT.Copy).then_inc(sem["s_kept"], 1)

        exps(0)
        for n in range(U):
            if n + 1 < U:
                exps(n + 1)
            copy(n)
            if n >= 2 and NA_UNITS[n - 2] == (1, 3):
                keep(n - 2)
        keep(U - 1)

    @block.scalar
    def _(act):
        ch = Chain(act, sem["act_chain"])

        def split_hi(target):
            if target is None:
                return
            st, i, j = target
            act.wait_ge(sem[f"raw_in{j % 2}"], raw_need(st, i, j))
            if not (st["p0"] == 0 and isinstance(i, int) and i == 0 and j < 2):
                act.wait_ge(sem["panel_used"], number(st, i, j) - 1)
            nc.scalar.activation(w_view(w_hi, j % 2, st["shapes"][j]), w_view(raw, j % 2, st["shapes"][j]),
                                 ACT.Copy).then_inc(sem["w_split_hi"], 1)

        for st in PLAN:
            b = st["base"]
            if st["kind"] == "load":
                for t in range(row_tiles):
                    act.wait_ge(sem["row_tile"], t + 1)
                    n = min(P, n_rows - t * P)
                    nc.scalar.activation(colv[:, t * P:t * P + n], ps_d[:, t % 2, 0:n], ACT.Copy).then_inc(sem["row_col"], 1)
                act.wait_ge(sem["row_col"], row_tiles)
                nc.scalar.activation(c_col[:, :], colv[:, 0:3 * KD], ACT.Silu).then_inc(sem["c_act"], 1)
                for k in range(KD):
                    act.wait_ge(sem["x_tr"], k + 1)
                    nc.scalar.activation(x[:, k * S:(k + 1) * S], ps_g[:, k % 2, :], ACT.Copy).then_inc(sem["x_in"], 1)
                act.wait_ge(sem["x_in"], KD)
                for k in range(KD):
                    nc.scalar.activation(squares[:, k, :], x[:, k * S:(k + 1) * S], ACT.Square).then_inc(sem["squared"], 1)
                split_hi((streams[0], 0, 0))
                split_hi((streams[0], 0, 1))
            elif st["kind"] == "context":
                for k in range(KD):
                    act.wait_ge(sem["hc_tr"], k + 1)
                    nc.scalar.activation(hc[:, k * C:(k + 1) * C], ps_u[:, k % 2, 0:C], ACT.Copy).then_inc(sem["hc_in"], 1)
            elif st["kind"] == "norm":
                buf, N = src(st)
                if st["mode"] != "mod_h":
                    if "squared" in st["totals"]:
                        for n in ("x_in", "down0", "down1", "proj0", "proj1", "x_new"):
                            if b[n] and st["mode"] != "ln_x":
                                act.wait_ge(sem[n], b[n])
                        if b["h_ready"]:
                            act.wait_ge(sem["h_ready"], b["h_ready"])
                        for k in range(KD):
                            if st["mode"] == "ln_x":
                                act.wait_ge(sem["centred"], b["centred"] + k + 1)
                            nc.scalar.activation(squares[:, k, 0:N], buf[:, k * N:(k + 1) * N], ACT.Square).then_inc(sem["squared"], 1)
                        act.wait_ge(sem["square_summed"], b["square_summed"] + 1)
                    else:
                        act.wait_ge(sem["square_summed"], b["square_summed"])
                    e = eps[:, 1:2] if st["mode"] == "ln_x" else eps[:, 0:1]
                    act.wait_ge(sem["consts"], 5)
                    nc.scalar.activation(rstd[:, 0:N], ps_s[:, 0:N], ACT.Sqrt, bias=e).then_inc(sem["deviation"], 1)
                if "h_hi" in st["totals"]:
                    for k in range(KD):
                        act.wait_ge(sem["h_full"], b["h_full"] + k + 1)
                        nc.scalar.activation(dst_of(st)[0][:, k * N:(k + 1) * N], full_t[:, k % 2, 0:N], ACT.Copy).then_inc(sem["h_hi"], 1)
            elif st["kind"] == "gu":
                N = st["N"]
                p0, pr, hl = st["p0"], b["product"], b["hid_lo"]

                def one(i, last):
                    split_hi(ahead(st, i, 0, last))
                    act.wait_ge(sem["panel_used"], p0 + i * 2 + 1)
                    act.wait_ge(sem["product"], pr + i)
                    if st["conv"] is None:
                        nc.scalar.activation(gate_t[:, :, 0:N], ps_g[:, :, 0:N], ACT.Silu).then_inc(sem["g_read"], 1)
                        split_hi(ahead(st, i, 1, last))
                    else:
                        wc, bc = st["conv"]
                        for c in range(2):
                            cc = st["k0"] + i * 2 + c
                            ins = nc.scalar.activation(gate_t[:, c, 0:N], ps_g[:, c, 0:N], ACT.Identity,
                                                       scale=colv[:, ds(wc + 2 * FC + st["k0"] + FC + c + i * 2, 1)], bias=colv[:, ds(bc + FC + st["k0"] + c + i * 2, 1)])
                        ins.then_inc(sem["g_affine"], 1)
                        act.wait_ge(sem["g_conv"], b["g_conv"] + i + 1)
                        nc.scalar.activation(gate_t[:, :, 0:N], gate_t[:, :, 0:N], ACT.Silu).then_inc(sem["g_read"], 1)
                        split_hi(ahead(st, i, 1, last))
                        act.wait_ge(sem["panel_used"], p0 + i * 2 + 2)
                        act.wait_ge(sem["hid_lo"], hl + i)
                        for c in range(2):
                            ins = nc.scalar.activation(prod_t[:, c, 0:N], ps_u[:, c, 0:N], ACT.Identity,
                                                       scale=colv[:, ds(wc + 2 * FC + st["k0"] + c + i * 2, 1)], bias=colv[:, ds(bc + st["k0"] + c + i * 2, 1)])
                        ins.then_inc(sem["u_affine"], 1)
                    act.wait_ge(sem["product"], pr + i + 1)
                    nc.scalar.activation(hid_hi[:, ds(i * (2 * N), 2 * N)].rearrange("p (c n) -> p c n", c=2), prod_t[:, :, 0:N],
                                         ACT.Copy).then_inc(sem["hid_hi"], 1)
                ch.loop(st["iters"], 0, one)
            elif st["kind"] in ("dn", "proj"):
                N, name, per = st["N"], {"dn": "down", "proj": "proj"}[st["kind"]], KD // 2 // st["iters"]
                v = src(st)[0]

                def one(i, last):
                    for j in range(len(st["shapes"])):
                        split_hi(ahead(st, i, j, last))
                        if st["sums"] == "square":
                            if b["h_ready"]:
                                act.wait_ge(sem["h_ready"], b["h_ready"])
                            act.wait_ge(sem[f"{name}{j}"], b[f"{name}{j}"] + i + 1)
                            for c in range(per):
                                w = ds(i * (2 * per * N) + (j * per + c) * N, N)
                                nc.scalar.activation(squares.rearrange("p k n -> p (k n)")[:, w], v[:, w], ACT.Square).then_inc(sem["squared"], 1)
                ch.loop(st["iters"], 0, one)
            elif st["kind"] == "mixer":
                mixer_act(st, b, act, split_hi)
            elif st["kind"] == "mla_in":
                mla_in_act(st, b, act, split_hi)
            elif st["kind"] == "mla":
                ch.loop(st["iters"], 0, lambda i, last: mla_act(st, b, act, split_hi, i, last))
            elif st["kind"] == "na":
                ch.loop(st["iters"], 0, lambda i, last: na_act(st, b, act, split_hi, i, last))
            elif st["kind"] == "gather":
                act.wait_ge(sem["s_kept"], b["s_kept"])
                for k in range(KD):
                    nc.scalar.activation(h_hi[:, k * S:(k + 1) * S], (o_lat if st["ctx"] else on_lat)[:, k, :], ACT.Copy).then_inc(sem["h_hi"], 1)
                if st["ctx"]:
                    for k in range(KD):
                        nc.scalar.activation(oc_hi[:, k * C:(k + 1) * C], o_ctx[:, k, :], ACT.Copy).then_inc(sem["h_hi"], 1)
            elif st["kind"] == "store":
                for t in range(4):
                    act.wait_ge(sem["o_tr"], b["o_tr"] + t + 1)
                    nc.scalar.activation(x_out[:, t, :].rearrange("p (c n) -> p c n", c=2), ps_all[:, 2 * t:2 * t + 2, :], ACT.Copy).then_inc(sem["o_out"], 1)

    def mixer_pe(st, b, pe, reduce_gemv, triple):
        for j in range(8):
            pair = (ps_g, ps_u)[j % 2]
            pe.wait_ge(sem["w_split_lo"], st["p0"] + j + 1)
            if j >= 2:
                pe.wait_ge(sem["in_evac"], b["in_evac"] + j - 1)
            whi, wlo = (w_view(t, j % 2, st["shapes"][j]) for t in (w_hi, w_lo))
            for k in range(KD):
                if j == 0:
                    pe.wait_ge(sem["h_ready"], b["h_ready"] - KD + k + 1)
                hh, hl = (t[:, k * S:(k + 1) * S] for t in (h_hi, h_lo))
                for c in range(2):
                    cc = slice(c * P, (c + 1) * P)
                    if j == 5 and c == 1:
                        continue
                    ins = triple(pair[:, c, :], whi[:, k, cc], wlo[:, k, cc], hh, hl, k == 0, k == KD - 1)
            if j == 5:
                for t in range(4):
                    tt = slice(t * P, (t + 1) * P)
                    for k in range(KD):
                        hh, hl = (u[:, k * S:(k + 1) * S][:, tt] for u in (h_hi, h_lo))
                        ins = triple(pair[:, 1, tt], hh, hl, whi[:, k, P:2 * P], wlo[:, k, P:2 * P], k == 0, k == KD - 1)
            ins.then_inc(sem["panel_used"], 1)
            if 2 <= j <= 6 and j - 2 < len(st["gemvs"]):
                reduce_gemv(st["gemvs"][j - 2])
            if j in (2, 4):
                m = j // 2 - 1
                pe.wait_ge(sem["lconv"], b["lconv"] + 2)
                if m == 0:
                    pe.wait_ge(sem["misc_in"], 16 * 10 * (st["l"] + 1))
                else:
                    pe.wait_ge(sem["gates_r"], b["gates_r"] + 2)
                for c in range(2):
                    ins = nc.tensor.matmul(ps_d[:, c, :], gate_w[:, m, c, :], cx[:, c, :], start=True, stop=True)
                ins.then_inc(sem["gates_mm"], 1)
        pe.wait_ge(sem["in_evac"], b["in_evac"] + 8)
        pe.wait_ge(sem["gates_i"], b["gates_i"] + 2)

        def scores(h):
            i, g = h // 2, h % 2
            pr = slice(g * HD, (g + 1) * HD)
            pair = (ps_g, ps_u)[g]
            if h >= 2:
                pe.wait_ge(sem["at_s_read"], b["at_s_read"] + h - 1)
            for n in range(4):
                q = mq[pr, i, n * P:(n + 1) * P]
                o = pair[:, n // 2, (n % 2) * 2 * P:(n % 2 + 1) * 2 * P]
                if n == 0:
                    ins = nc.tensor.matmul(o[:, P:2 * P], q, mk[pr, 0:P], start=True, stop=True)
                else:
                    ins = nc.tensor.matmul(o, q, mk[pr, (n - 1) * P:(n + 1) * P], start=True, stop=True)
            ins.then_inc(sem["at_s"], 1)

        def weigh(h):
            i, g = h // 2, h % 2
            pe.wait_ge(sem["at_p"], b["at_p"] + h + 1)
            for n in range(4):
                if h >= 1 and n % 2 == 0:
                    pe.wait_ge(sem[f"at_pt{n // 2}"], b[f"at_pt{n // 2}"] + h)
                for j in range(2):
                    if n == 0 and j == 0:
                        continue
                    t = 2 * n + j
                    ins = nc.tensor.matmul(ps_d[:, t // 4, (t % 4) * P:(t % 4 + 1) * P], att[:, g, n, j * P:(j + 1) * P], diags[:, g, n, :], start=True, stop=True)
                if n % 2:
                    ins.then_inc(sem[f"at_t{n // 2}"], 1)

        def values(h):
            i, g = h // 2, h % 2
            for n in range(2):
                pe.wait_ge(sem[f"at_pt{n}"], b[f"at_pt{n}"] + h + 1)
            if h >= 2 and g == 0:
                pe.wait_ge(sem["y_at"], b["y_at"] + i)
            for n in range(4):
                o = ps_s[g * HD:(g + 1) * HD, n * P:(n + 1) * P]
                for j in range(1 if n == 0 else 0, 2):
                    ins = nc.tensor.matmul(o, mv[:, n - 1 + j, g * HD:(g + 1) * HD], att_t[:, g, 2 * n + j, :],
                                           start=(j == 0 or n == 0), stop=(j == 1))
            ins.then_inc(sem["at_o"], 1)

        scores(0)
        for h in range(NQ):
            if h + 1 < NQ:
                scores(h + 1)
            if h >= 1:
                values(h - 1)
            weigh(h)
            if h == 2:
                for n in range(5, len(st["gemvs"])):
                    reduce_gemv(st["gemvs"][n])
        values(NQ - 1)

    def mla_in_pe(st, b, pe, triple):
        def sums(n):
            for k in ((0, 1, 2), (3, 4))[n]:
                pe.wait_ge(sem["low_sq"], b["low_sq"] + k + 1)
                first, last = k == 3 * n, k == 2 + 2 * n
                nc.tensor.matmul((ps_g, ps_u)[n][:, 1, :], mean_m[:, :], low_squares[n][:, k - 3 * n, C:T], start=first, stop=last)
                ins = nc.tensor.matmul((ps_s, ps_mod)[n][:, 0:C], mean_m[:, :], low_squares[n][:, k - 3 * n, 0:C], start=first, stop=last)
            ins.then_inc(sem["low_sum"], 1)

        plans = [[(ps_g[:, 0, :], 0, P, 0), (ps_g[:, 1, :], P, 2 * P, 1)], [(ps_u[:, 0, :], 0, P, 0), (ps_u[:, 1, :], P, 2 * P, 1)],
                 [(ps_g[:, 0, :], 0, P, 0)], [(ps_u[:, 0, :], 0, DQ, 0)]]
        for j in range(4):
            pe.wait_ge(sem["w_split_lo"], st["p0"] + j + 1)
            if j >= 2:
                pe.wait_ge(sem["low_out"], b["low_out"] + j - 1)
            whi, wlo = (w_view(t, j % 2, st["shapes"][j]) for t in (w_hi, w_lo))
            for bank, c0, c1, c in plans[j]:
                for k in range(KD):
                    if j == 0 and c == 0:
                        pe.wait_ge(sem["h_ready"], b["h_ready"] - KD + k + 1)
                    m = [t[:, k * S:(k + 1) * S] for t in (h_hi, h_lo)]
                    triple(bank[0:c1 - c0, :], whi[:, k, c0:c1], wlo[:, k, c0:c1], *m, k == 0, k == KD - 1)
                for k in range(KD):
                    m = [t[:, k * C:(k + 1) * C] for t in (c0_hi, c0_lo)]
                    ins = triple(ps_d[0:c1 - c0, j % 2, c * C:(c + 1) * C], whi[:, k, c0:c1], wlo[:, k, c0:c1], *m, k == 0, k == KD - 1)
            ins.then_inc(sem["panel_used"], 1)
            if j == 2:
                sums(0)
        pe.wait_ge(sem["low_out"], b["low_out"] + 4)
        pe.wait_ge(sem["low_dev"], b["low_dev"] + 1)
        nc.tensor.matmul(ps_s[64:96, :], turn_m[NOPE:DQ, NOPE:DQ], low_pe[64:96, C:T], start=True, stop=True).then_inc(sem["pe_rot"], 1)
        sums(1)

    def mla_pe(st, b, pe, triple, i):
        base_of = lambda name, per: b[name] + i * per
        U = len(MLA_UNITS)
        p0 = st["p0"]
        lows = lambda k, s: [t[:, k, s] for t in (low_hi, low_lo)]
        lat, ctx_s = slice(C, T), slice(0, C)
        pe.wait_ge(sem["low_lo"], b["low_lo"] - 2)
        pe.wait_ge(sem["low_dev"], b["low_dev"])
        pe.wait_ge(sem["w_split_lo"], p0 + i * 2 + 1)
        whi, wlo = (w_view(t, 0, st["shapes"][0]) for t in (w_hi, w_lo))
        for h in range(PER):
            cc = slice(h * DQ, (h + 1) * DQ)
            for k in range(3):
                triple(ps_all[0:DQ, h, :], whi[:, k, cc], wlo[:, k, cc], *lows(k, lat), k == 0, k == 2)
            for k in range(3):
                ins = triple(ps_d[0:DQ, h // 2, (h % 2) * C:(h % 2 + 1) * C], whi[:, k, cc], wlo[:, k, cc], *lows(k, ctx_s), k == 0, k == 2)
        ins.then_inc(sem["panel_used"], 1)
        pe.wait_ge(sem["w_split_lo"], p0 + i * 2 + 2)
        pe.wait_ge(sem["low_lo"], b["low_lo"])
        pe.wait_ge(sem["pe_key"], b["pe_key"])
        pe.wait_ge(sem["s_kept"], base_of("s_kept", PER))
        whi, wlo = (w_view(t, 1, st["shapes"][1]) for t in (w_hi, w_lo))

        def keys_of(h):
            cc = slice(h * P, (h + 1) * P)
            for k in range(2):
                ins = triple(ps_all[:, 4 + h, :], whi[:, k, cc], wlo[:, k, cc], *lows(3 + k, lat), k == 0, k == 1)
            return ins

        keys_of(2)
        keys_of(3).then_inc(sem["head_mm"], 1)
        pe.wait_ge(sem["head_out"], base_of("head_out", 4) + 1)
        for h in range(PER):
            ins = nc.tensor.matmul(ps_all[0:DQ, h, :], turn_m[0:DQ, :], q_flat[0:DQ, h, :], start=True, stop=True)
        ins.then_inc(sem["head_mm"], 1)
        keys_of(0)
        keys_of(1).then_inc(sem["head_mm"], 1)
        pe.wait_ge(sem["head_out"], base_of("head_out", 4) + 2)
        for h in range(PER):
            cc = slice(h * P, (h + 1) * P)
            for k in range(2):
                triple(ps_all[:, 6 + h // 2, (h % 2) * C:(h % 2 + 1) * C], whi[:, k, cc], wlo[:, k, cc], *lows(3 + k, ctx_s), k == 0, k == 1)
        pe.wait_ge(sem["q_rot"], base_of("q_rot", 1) + 1)

        def tile_of_values(t):
            tt = slice(t * P, (t + 1) * P)
            o = ps_all[:, 2 + t // 2, (t % 2) * C:(t % 2 + 1) * C].rearrange("p (h n) -> p h n", n=HD)
            for k in range(2):
                vh, vl = (w[:, k, :].rearrange("p (h n) -> p h n", n=P)[:, :, NOPE:P] for w in (whi, wlo))
                ins = triple(o, *lows(3 + k, tt), vh, vl, k == 0, k == 1)
            return ins

        for t in range(4):
            ins = tile_of_values(t)
        ins.then_inc(sem["head_mm"], 1)
        pe.wait_ge(sem["head_out"], base_of("head_out", 4) + 3)
        for t in (4, 5):
            ins = tile_of_values(t)
        ins.then_inc(sem["panel_used"], 1)
        pe.wait_ge(sem["head_out"], base_of("head_out", 4) + 4)

        def scores(n):
            h, ctx, q = MLA_UNITS[n]
            if n >= 2:
                pe.wait_ge(sem["s_exp"], base_of("s_exp", U) + n - 1)
            qq = slice(q * P, (q + 1) * P)
            o = ps_all[:, 2 * (n % 2), C:2 * C]
            if ctx:
                ins = nc.tensor.matmul(o, q_ctx[0:DQ, h, qq], keys[0:DQ, h, 0:C], start=True, stop=True)
            else:
                nc.tensor.matmul(o, q_flat[0:DQ, h, qq], keys[0:DQ, h, 0:C], start=True, stop=True)
                ins = nc.tensor.matmul(ps_all[:, 2 * (n % 2) + 1, :], q_turn[0:DQ, h, qq], keys[0:DQ, h, C:T], start=True, stop=True)
            ins.then_inc(sem["s_made"], 1)

        def turn(n):
            h, ctx, q = MLA_UNITS[n]
            pe.wait_ge(sem["s_shared"], base_of("s_shared", U) + n + 1)
            pe.wait_ge(sem["copied0"], base_of("copied0", U) + n)
            for t in range(2 if ctx else 3):
                ins = nc.tensor.matmul(ps_all[:, 4, t * P:(t + 1) * P], prob[:, n % 2, t * P:(t + 1) * P], diag[:, n % 2, :], start=True, stop=True)
            ins.then_inc(sem["turned0"], 1)
            if not ctx:
                pe.wait_ge(sem["copied1"], base_of("copied1", 4 * PER) + MLA_LAT[n])
                for t in range(3, 6):
                    ins = nc.tensor.matmul(ps_all[:, 5, (t - 3) * P:(t - 2) * P], prob[:, n % 2, t * P:(t + 1) * P], diag[:, n % 2, :], start=True, stop=True)
                ins.then_inc(sem["turned1"], 1)

        def weigh(n):
            h, ctx, q = MLA_UNITS[n]
            pe.wait_ge(sem["copied0"], base_of("copied0", U) + n + 1)
            if not ctx:
                pe.wait_ge(sem["copied1"], base_of("copied1", 4 * PER) + MLA_LAT[n] + 1)
            if q == 0 and h == 2:
                pe.wait_ge(sem["s_kept"], base_of("s_kept", PER) + ctx + 1)
            for t in range(2 if ctx else 6):
                v = vals[:, t, h * HD:(h + 1) * HD]
                ins = nc.tensor.matmul(ps_all[(h % 2) * HD:(h % 2 + 1) * HD, 6 + ctx, q * P:(q + 1) * P], v, prob_t[:, n % 2, t * P:(t + 1) * P], start=(t == 0), stop=(t == (1 if ctx else 5)))
            ins.then_inc(sem["s_weighted"], 1)

        scores(0)
        for n in range(U):
            if n + 1 < U:
                scores(n + 1)
            if n:
                weigh(n - 1)
            turn(n)
        weigh(U - 1)

    def na_pe(st, b, pe, triple, i):
        base_of = lambda name, per: b[name] + i * per
        U = len(NA_UNITS)
        p0 = st["p0"]
        for j in range(4):
            pe.wait_ge(sem["w_split_lo"], p0 + i * 4 + j + 1)
            if j < 2:
                pe.wait_ge(sem["h_ready"], b["h_ready"] - (0 if j else KD))
            whi, wlo = (w_view(t, j % 2, st["shapes"][j]) for t in (w_hi, w_lo))
            if j == 1:
                pe.wait_ge(sem["s_kept"], base_of("s_kept", PER // 2))
            if j in (0, 3):
                if j == 3:
                    for c in range(2):
                        for k in range(KD):
                            m = [t[:, k * C:(k + 1) * C] for t in (ch_hi, ch_lo)]
                            triple(ps_all[:, 4, c * C:(c + 1) * C], whi[:, k, c * P:(c + 1) * P], wlo[:, k, c * P:(c + 1) * P], *m, k == 0, k == KD - 1)
                for c in range(2):
                    cc = slice(c * P, (c + 1) * P)
                    for k in range(KD):
                        m = [t[:, k * S:(k + 1) * S] for t in (h_hi, h_lo)]
                        ins = triple(ps_all[:, (0, 2)[j // 3] + c, :], whi[:, k, cc], wlo[:, k, cc], *m, k == 0, k == KD - 1)
                    if j == 3 and c == 0:
                        ins.then_inc(sem["key_mm"], 1)
            else:
                for t in range(6):
                    bank = ps_all[:, 5 + t // 2, (t % 2) * 2 * P:(t % 2 + 1) * 2 * P]
                    for kk in range(KD // 2):
                        k = (j - 1) * (KD // 2) + kk
                        if t < 2:
                            m = [u[:, k * C + t * P:k * C + (t + 1) * P] for u in (ch_hi, ch_lo)]
                        else:
                            m = [u[:, k * S + (t - 2) * P:k * S + (t - 1) * P] for u in (h_hi, h_lo)]
                        ins = triple(bank, *m, whi[:, kk, :], wlo[:, kk, :], k == 0 and t % 2 == 0, k == KD - 1 and t % 2 == 1)
            ins.then_inc(sem["panel_used"], 1)

        def scores(n):
            h, j = NA_UNITS[n]
            r, c = slice((h % 2) * HD, (h % 2 + 1) * HD), h // 2
            if n >= 4:
                pe.wait_ge(sem["s_exp"], base_of("s_exp", U) + n - 3)
            if n % 8 == 0:
                pe.wait_ge(sem["keys_out"], base_of("keys_out", 2) + n // 8 + 1)
            q = nq[r, c, j * P:(j + 1) * P]
            kk = nk[r, c, C:T].rearrange("p (r n) -> p r n", n=GRID)[:, :, BAND[j]:BAND[j] + KC_]
            nc.tensor.matmul(ps_all[:, n % 4, 0:C], q, nk[r, c, 0:C], start=True, stop=True)
            nc.tensor.matmul(ps_all[:, n % 4, C:2 * C].rearrange("p (r n) -> p r n", n=KC_), q, kk, start=True, stop=True).then_inc(sem["s_made"], 1)

        def turn(n):
            pe.wait_ge(sem["s_shared"], base_of("s_shared", U) + n + 1)
            for half in range(2):
                pe.wait_ge(sem[f"copied{half}"], base_of(f"copied{half}", U) + n)
                for t in range(2):
                    w = slice((2 * half + t) * P, (2 * half + t + 1) * P)
                    ins = nc.tensor.matmul(ps_all[:, 4 + half, t * P:(t + 1) * P], prob_n[:, n % 2, w], diag_n[:, n % 2, :], start=True, stop=True)
                ins.then_inc(sem[f"turned{half}"], 1)

        def weigh(n):
            h, j = NA_UNITS[n]
            for half in range(2):
                pe.wait_ge(sem[f"copied{half}"], base_of(f"copied{half}", U) + n + 1)
            if n == 0:
                pe.wait_ge(sem["band_in"], base_of("band_in", 16 * 4 * ROWS) + 16 * 4 * ROWS)
            cc = slice(h * HD, (h + 1) * HD)
            for t in range(4):
                v = nv[:, t, cc] if t < 2 else nvb[:, j, t - 2, cc]
                ins = nc.tensor.matmul(ps_all[(h % 2) * HD:(h % 2 + 1) * HD, 6 + h // 2, j * P:(j + 1) * P], v, prob_nt[:, n % 2, t * P:(t + 1) * P], start=(t == 0), stop=(t == 3))
            ins.then_inc(sem["s_weighted"], 1)

        scores(0)
        scores(1)
        pe.wait_ge(sem["keys_out"], base_of("keys_out", 2) + 2)
        for n in range(U):
            if n + 2 < U:
                scores(n + 2)
            if n:
                weigh(n - 1)
            turn(n)
        weigh(U - 1)

    @block.tensor
    def _(pe):
        def reduce_gemv(g, i=0, slot=0):
            pe.wait_ge(sem["gemv_done"], g + i + 1)
            for h in range(2):
                part = lambda t: accs[slot][:, t, h * P:(h + 1) * P]
                if g < G_ADA:
                    ins = nc.tensor.matmul(ps_mod[:, ds(2 * g + h + i * 2, 1)], part(0), ones[:, :], start=True, stop=True)
                else:
                    nc.tensor.matmul(ps_mod[:, ds(2 * g + h + i * 2, 1)], part(0), ones[:, :], start=True, stop=True)
                    ins = nc.tensor.matmul(ps_mod[:, ds(CTX_COL + 2 * (g - G_ADA) + h + i * 2, 1)], part(1), ones[:, :], start=True, stop=True)
            ins.then_inc(sem["gemv_reduced"], 1)

        def sums_of(st, b, i, name, last=False):
            N, per = st["N"], KD // 2 // st["iters"]
            if isinstance(i, int) and i == 0:
                if b["deviation"]:
                    pe.wait_ge(sem["deviation"], b["deviation"])
            for j in range(2):
                if st["sums"] == "mean":
                    pe.wait_ge(sem[f"{name}{j}"], b[f"{name}{j}"] + i + 1)
                for c in range(per):
                    k = j * per + c
                    if st["sums"] == "square":
                        pe.wait_ge(sem["squared"], b["squared"] + i * (2 * per) + k + 1)
                    buf = squares.rearrange("p k n -> p (k n)") if st["sums"] == "square" else src(st)[0]
                    ins = nc.tensor.matmul(ps_s[:, 0:N], mean_m[:, :], buf[:, ds(i * (2 * per * N) + k * N, N)],
                                           start=(isinstance(i, int) and i == 0 and k == 0), stop=(last and k == 2 * per - 1))
            if last:
                ins.then_inc(sem["square_summed" if st["sums"] == "square" else "mean_summed"], 1)

        def triple(o, whi, wlo, mhi, mlo, first, last):
            nc.tensor.matmul(o, whi, mhi, start=first, stop=False)
            nc.tensor.matmul(o, whi, mlo, start=False, stop=False)
            return nc.tensor.matmul(o, wlo, mhi, start=False, stop=last)

        pe.wait_ge(sem["consts"], 5)
        for st in PLAN:
            b = st["base"]
            kind = st["kind"]
            if kind == "load":
                pe.wait_ge(sem["const_in"], 16)
                n_in = sum(1 for t in range(row_tiles) for name, ap in rows
                           if max(col[name], t * P) < min(col[name] + ap.shape[0], (t + 1) * P))
                pe.wait_ge(sem["rows_in"], 16 * n_in)
                for t in range(row_tiles):
                    n = min(P, n_rows - t * P)
                    if t >= 2:
                        pe.wait_ge(sem["row_col"], t - 1)
                    nc.tensor.transpose(ps_d[:, t % 2, 0:n], row_in[0:n, t, :], ident[0:n, 0:n]).then_inc(sem["row_tile"], 1)
            elif kind == "prologue":
                for n, g in enumerate(st["gemvs"]):
                    reduce_gemv(g, slot=n % 2)
                    for k in range(2 * n - 2, 2 * n) if 1 <= n <= 4 else ():
                        if k == 0:
                            pe.wait_ge(sem["x_rows_in"], 16)
                        if k >= 2:
                            pe.wait_ge(sem["x_in"], k - 1)
                        for t in range(4):
                            ins = nc.tensor.transpose(ps_g[:, k % 2, t * P:(t + 1) * P], x_rows[:, t, k * P:(k + 1) * P], ident[:, :])
                        ins.then_inc(sem["x_tr"], 1)
                    for k in range(3 * n - 15, min(3 * n - 12, KD)) if n >= 5 else ():
                        pe.wait_ge(sem["squared"], k + 1)
                        ins = nc.tensor.matmul(ps_s[:, :], mean_m[:, :], squares[:, k, :], start=(k == 0), stop=(k == KD - 1))
                        if k == KD - 1:
                            ins.then_inc(sem["square_summed"], 1)
            elif kind == "context":
                pe.wait_ge(sem["c_rows_in"], 16)
                pe.wait_ge(sem["product"], b["product"])
                for k in range(KD):
                    if k >= 2:
                        pe.wait_ge(sem["hc_in"], k - 1)
                    for t in range(2):
                        ins = nc.tensor.transpose(ps_u[:, k % 2, t * P:(t + 1) * P], c_rows[:, t, k * P:(k + 1) * P], ident[:, :])
                    ins.then_inc(sem["hc_tr"], 1)
            elif kind == "norm" and st["mode"] != "mod_h":
                buf, N = src(st)
                if "mean_summed" in st["totals"]:
                    for n in ("down0", "down1", "proj0", "proj1", "deviation"):
                        if b[n]:
                            pe.wait_ge(sem[n], b[n])
                    for k in range(KD):
                        ins = nc.tensor.matmul(ps_s[:, 0:N], mean_m[:, :], buf[:, k * N:(k + 1) * N], start=(k == 0), stop=(k == KD - 1))
                    ins.then_inc(sem["mean_summed"], 1)
                if st["mode"] == "ln_x":
                    pe.wait_ge(sem["centred"], b["centred"] + KD)
                if "squared" in st["totals"]:
                    for k in range(KD):
                        pe.wait_ge(sem["squared"], b["squared"] + k + 1)
                        ins = nc.tensor.matmul(ps_s[:, 0:N], mean_m[:, :], squares[:, k, 0:N], start=(k == 0), stop=(k == KD - 1))
                    ins.then_inc(sem["square_summed"], 1)
            elif kind == "gu":
                N, p0 = st["N"], st["p0"]

                def one(i, last):
                    for j, bank in enumerate((ps_g, ps_u)):
                        pe.wait_ge(sem["w_split_lo"], p0 + i * 2 + j + 1)
                        if st is streams[2] and j == 1:
                            pe.wait_ge(sem["hc_in"], KD)
                        read = ("g_read", "product")[j]
                        pe.wait_ge(sem[read], b[read] + i)
                        whi, wlo = (w_view(t, j, st["shapes"][j]) for t in (w_hi, w_lo))
                        for k in range(KD):
                            if st["wait_h"] and j == 0:
                                pe.wait_ge(sem["h_ready"], b["h_ready"] - KD + k + 1)
                            m = [t[:, k * N:(k + 1) * N] for t in ((c0_hi, c0_lo) if st["ctx"] else (h_hi, h_lo))]
                            for c in range(2):
                                cc = slice(c * P, (c + 1) * P)
                                ins = triple(bank[:, c, 0:N], whi[:, k, cc], wlo[:, k, cc], *m, k == 0, k == KD - 1)
                        ins.then_inc(sem["panel_used"], 1)
                    if st["gemv"] is not None:
                        reduce_gemv(st["gemv"], i)
                Chain(pe, None).loop(st["iters"], 0, one)
            elif kind == "dn":
                N, p0, nk = st["N"], st["p0"], st["nk"]

                def one(i, last):
                    for j in range(2):
                        pe.wait_ge(sem["w_split_lo"], p0 + i * 2 + j + 1)
                        pe.wait_ge(sem[f"down{j}"], b[f"down{j}"] + i)
                        whi, wlo = (w_view(t, j, st["shapes"][j]) for t in (w_hi, w_lo))
                        for k in range(nk):
                            if j == 0 and k % 2 == 0:
                                pe.wait_ge(sem["hid_lo"], b["hid_lo"] - (nk - k) // 2 + 1)
                            m = [t[:, k * N:(k + 1) * N] for t in (hid_hi, hid_lo)]
                            ins = triple(ps_d[:, j, 0:N], whi[:, k, :], wlo[:, k, :], *m, k == 0, k == nk - 1)
                        ins.then_inc(sem["panel_used"], 1)
                    if st["gemv"] is not None:
                        reduce_gemv(st["gemv"], i)
                if st["sums"] is None:
                    Chain(pe, None).loop(st["iters"], 0, one)
                else:
                    one(0, False)
                    one(1, False)
                    sums_of(st, b, 0, "down")
                    with pe.Fori(2, st["iters"]) as i:
                        one(i, False)
                        sums_of(st, b, i - 1, "down")
                    sums_of(st, b, st["iters"] - 1, "down", True)
            elif kind == "proj":
                p0 = st["p0"]

                def one(i, gemvs):
                    for j, bank in enumerate((ps_g, ps_u)):
                        pe.wait_ge(sem["w_split_lo"], p0 + i * 2 + j + 1)
                        pe.wait_ge(sem[f"proj{j}"], b[f"proj{j}"] + i)
                        whi, wlo = (w_view(t, j, st["shapes"][j]) for t in (w_hi, w_lo))
                        for n, k in enumerate(st["order"]):
                            if i == 0 and j == 0:
                                made = KD if st["ctx_gate"] is None else 2 * KD
                                pe.wait_ge(sem["h_ready"], b["h_ready"] - made + n + 1)
                            m = [t[:, k * S:(k + 1) * S] for t in (h_hi, h_lo)]
                            for c in range(2):
                                cc = slice(c * P, (c + 1) * P)
                                ins = triple(bank[:, c, :], whi[:, k, cc], wlo[:, k, cc], *m, n == 0, n == KD - 1)
                            if j == 1 and n == 3 and len(gemvs) == 3:
                                reduce_gemv(gemvs[1])
                        if st["ctx_gate"] is not None:
                            pe.wait_ge(sem["h_ready"], b["h_ready"])
                            for c in range(2):
                                cc = slice(c * P, (c + 1) * P)
                                for k in range(KD):
                                    m = [t[:, k * C:(k + 1) * C] for t in (oc_hi, oc_lo)]
                                    ins = triple(ps_d[:, j, c * C:(c + 1) * C], whi[:, k, cc], wlo[:, k, cc], *m, k == 0, k == KD - 1)
                        ins.then_inc(sem["panel_used"], 1)
                        if len(gemvs) > j:
                            reduce_gemv(gemvs[-1 if j else 0])
                for i in range(2):
                    one(i, half_of(st["gemvs"], i))
                    if i:
                        sums_of(st, b, 0, "proj")
                sums_of(st, b, 1, "proj", True)
            elif kind == "mixer":
                mixer_pe(st, b, pe, reduce_gemv, triple)
            elif kind == "mla_in":
                mla_in_pe(st, b, pe, triple)
            elif kind == "mla":
                Chain(pe, None).loop(st["iters"], 0, lambda i, last: mla_pe(st, b, pe, triple, i))
            elif kind == "na":
                Chain(pe, None).loop(st["iters"], 0, lambda i, last: na_pe(st, b, pe, triple, i))
            elif kind == "store":
                for n in ("down0", "down1", "x_new", "x_in", "proj0", "proj1", "h_ready", "s_kept", "low_lo"):
                    if b[n] and not (n == "x_new" and n in PLAN[-2]["totals"]):
                        pe.wait_ge(sem[n], b[n])
                for k in range(KD):
                    if "x_new" in PLAN[-2]["totals"]:
                        pe.wait_ge(sem["x_new"], b["x_new"] - KD + k + 1)
                    for t in range(4):
                        tok = hc[:, k * C + (t % 2) * P:k * C + (t % 2 + 1) * P] if st["probe"] else x[:, k * S + t * P:k * S + (t + 1) * P]
                        ins = nc.tensor.transpose(ps_all[:, 2 * t + k // 4, (k % 4) * P:(k % 4 + 1) * P], tok, ident[:, :])
                        if k == KD - 1:
                            ins.then_inc(sem["o_tr"], 1)

    def mixer_dve(st, b, dve, ch, mix_gemv):
        l = st["l"]
        V = nc.vector
        cw = lambda name, t, c, taps: colv[:, col[name] + (l * taps + t) * 2 + c:col[name] + (l * taps + t) * 2 + c + 1]
        cb = lambda name, c: colv[:, col[name] + l * 2 + c:col[name] + l * 2 + c + 1]
        lam = colv[:, col["lam"] + 2 * l:col["lam"] + 2 * l + 2]
        y, z, z2, s = sm(14, 2), sm(15, 2), sm(16, 2), sm(17, 2)
        mix_gemv(0)
        ch.link(V.tensor_scalar(z, lam, -1.0, None, ALU.mult))
        ch.link(V.tensor_tensor(z2, z, lam, ALU.min))
        V.tensor_scalar(s, z2, 1.0, None, ALU.mult).then_inc(sem["lam_in"], 1)
        dve.wait_ge(sem["lam_exp"], b["lam_exp"] + 1)
        ch.link(V.tensor_scalar(z, y, 2.0, None, ALU.add))
        ch.link(V.reciprocal(z, z))
        ch.link(V.tensor_tensor(z, z, y, ALU.mult))
        ch.link(V.tensor_tensor(z2, z, z, ALU.mult))
        ch.link(V.tensor_scalar(s, z2, 1.0 / 17, 1.0 / 15, ALU.mult, ALU.add))
        for d in (13, 11, 9, 7, 5, 3, 1):
            ch.link(V.tensor_tensor(s, s, z2, ALU.mult))
            ch.link(V.tensor_scalar(s, s, 1.0 / d, None, ALU.add))
        ch.link(V.tensor_tensor(s, s, z, ALU.mult))
        ch.link(V.tensor_scalar(z, lam, -1.0, 0.0, ALU.mult, ALU.max))
        ch.link(V.scalar_tensor_tensor(s, s, 2.0, z, ALU.mult, ALU.add))
        ch.link(V.tensor_scalar(lsp[:, 0:2], s, 8.0, None, ALU.mult))
        V.tensor_scalar(lsp[:, 4:6], s, -8.0, None, ALU.mult).then_inc(sem["lru_q"], 1)
        dve.wait_ge(sem["in_evac"], b["in_evac"] + 1)
        for c in range(2):
            ch.link(V.tensor_scalar(cx[:, c, :], lx[:, c, :], cw("lconv_w", 3, c, 4), cb("lconv_b", c), ALU.mult, ALU.add))
            for t in (1, 2, 3):
                o = cx[:, c, t:]
                ins = V.scalar_tensor_tensor(o, lx[:, c, 0:S - t], cw("lconv_w", 3 - t, c, 4), o, ALU.mult, ALU.add)
                if t < 3:
                    ch.link(ins)
            ins.then_inc(sem["lconv"], 1)
        mix_gemv(1)
        mix_gemv(2)
        dve.wait_ge(sem["in_evac"], b["in_evac"] + 4)
        ch.link(V.tensor_tensor(sct[:, :, :], sct[:, :, :], sxt[:, :, :], ALU.mult))
        for c in range(2):
            ch.link(V.tensor_scalar(sxt[:, c, :], sct[:, c, :], cw("sconv_w", 2, c, 3), None, ALU.mult))
            for t in (1, 2):
                o = sxt[:, c, t:]
                ch.link(V.scalar_tensor_tensor(o, sct[:, c, 0:S - t], cw("sconv_w", 2 - t, c, 3), o, ALU.mult, ALU.add))
        dve.wait_ge(sem["in_evac"], b["in_evac"] + 5)
        V.tensor_tensor(sxt[:, :, :], sxt[:, :, :], sbt[:, :, :], ALU.mult).then_inc(sem["y_sc"], 1)
        mix_gemv(3)
        dve.wait_ge(sem["lru_t"], b["lru_t"] + 1)
        ch.link(V.tensor_scalar(lx[:, :, :], lt[:, :, :], 1.0, None, ALU.add))
        ch.link(V.reciprocal(lx[:, :, :], lx[:, :, :]))
        V.tensor_tensor(lt[:, :, :], lt[:, :, :], lx[:, :, :], ALU.mult).then_inc(sem["lru_m"], 1)
        mix_gemv(4)
        dve.wait_ge(sem["gates_i"], b["gates_i"] + 2)
        ch.link(V.tensor_tensor(gx[:, :, :], gx[:, :, :], cx[:, :, :], ALU.mult))
        for q in range(2):
            ch.link(V.memset(att[:, q, 0, 0:P], NEG))
        dve.wait_ge(sem["misc_in"], 160 * (l + 1))

        def soften(h):
            q, head = h % 2, h // 2 + 4 * (h % 2)
            pair = (ps_g, ps_u)[q]
            mx, nm, es, su = (sm(q * 6 + t) for t in range(4))
            dve.wait_ge(sem["at_s"], b["at_s"] + h + 1)
            if h >= 2:
                dve.wait_ge(sem["at_t1"], b["at_t1"] + h - 1)
                V.memset(att[:, q, 0, 0:P], NEG)
            ch.step(V.scalar_tensor_tensor(att[:, q, 0, P:2 * P], pair[:, 0, P:2 * P], HD ** -0.5, alibi[:, head, P:2 * P], ALU.mult, ALU.add))
            ch.step(V.scalar_tensor_tensor(att[:, q, 1, :], pair[:, 0, 2 * P:4 * P], HD ** -0.5, alibi[:, head, :], ALU.mult, ALU.add))
            for n in (2, 3):
                last = V.scalar_tensor_tensor(att[:, q, n, :], pair[:, 1, (n - 2) * 2 * P:(n - 1) * 2 * P], HD ** -0.5, alibi[:, head, :], ALU.mult, ALU.add)
                if n == 2:
                    ch.step(last)
            last.then_inc(sem["at_s_read"], 1)
            dve.wait_ge(sem["at_s_read"], b["at_s_read"] + h + 1)
            ch.link(V.tensor_reduce(mx, att[:, q, :, :], AX_X, ALU.max))
            ch.link(V.tensor_scalar(mx, mx, sinks_col(h), None, ALU.max))
            V.tensor_scalar(nm, mx, -1.0, None, ALU.mult).then_inc(sem["at_max"], 1)

        def share(h):
            q = h % 2
            mx, nm, es, su = (sm(q * 6 + t) for t in range(4))
            dve.wait_ge(sem["at_exp"], b["at_exp"] + h + 1)
            ch.link(V.tensor_tensor(su, su, es, ALU.add))
            ch.link(V.reciprocal(su, su))
            for n in range(4):
                ins = V.tensor_scalar(diags[:, q, n, :], ident[:, :], su[:, n:n + 1], None, ALU.mult)
            ins.then_inc(sem["at_p"], 1)

        def copy(h):
            dve.wait_ge(sem["at_t1"], b["at_t1"] + h + 1)
            if h >= 2:
                dve.wait_ge(sem["at_o"], b["at_o"] + h - 1)
            V.tensor_copy(att_t[:, h % 2, 4:8, :], ps_d[:, 1, :].rearrange("p (j q) -> p j q", q=P)).then_inc(sem["at_pt1"], 1)

        soften(0)
        dve.wait_ge(sem["gelu"], b["gelu"] + 1)
        ch.link(V.memset(lt[:, :, 0:1], 1.0))
        ch.link(V.tensor_tensor(gx[:, :, :], gx[:, :, :], lt[:, :, :], ALU.mult))
        for c in range(2):
            ch.link(V.tensor_tensor_scan(lx[:, c, :], ga[:, c, :], gx[:, c, :], 0.0, ALU.mult, ALU.add))
        V.tensor_tensor(lt[:, :, :], lx[:, :, :], lg[:, :, :], ALU.mult).then_inc(sem["y_lru"], 1)
        for h in range(NQ):
            if h:
                copy(h - 1)
            share(h)
            if h + 1 < NQ:
                soften(h + 1)
            if h == 0:
                for n in range(5, len(st["gemvs"])):
                    mix_gemv(n)
        copy(NQ - 1)

    def conv_taps(st, b, i, dve, ch):
        N, p0 = st["N"], st["p0"]
        wc, bc = st["conv"]
        V = nc.vector
        for half, (ready, t_, ps, off) in enumerate((("g_affine", gate_t, ps_g, FC), ("u_affine", prod_t, ps_u, 0))):
            dve.wait_ge(sem[ready], b[ready] + i + 1)
            w = lambda tap, c: colv[:, ds(wc + tap * 2 * FC + off + st["k0"] + c + i * 2, 1)]
            tok = []
            for c in range(2):
                o = t_[:, c, 1:N]
                tok.append(ch.step(V.scalar_tensor_tensor(o, ps[:, c, 0:N - 1], w(0, c), o, ALU.mult, ALU.add)))
            for c in range(2):
                o = t_[:, c, 0:N - 1]
                ch.wait(tok[c])
                ins = V.scalar_tensor_tensor(o, ps[:, c, 1:N], w(2, c), o, ALU.mult, ALU.add)
                if half == 0 and c == 1:
                    ins.then_inc(sem["g_conv"], 1)
                else:
                    last = ch.step(ins)
                    if half == 0:
                        ch.wait(last)
        ch.wait(last)

    def rope(dve, ch, o, x_, swapped):
        V = nc.vector
        ch.step(V.tensor_tensor(o, x_, turns[64:96, 0, :], ALU.mult))
        ch.link(V.tensor_tensor(turned[64:96, :], swapped, turns[64:96, 1, :], ALU.mult))
        return V.tensor_tensor(o, o, turned[64:96, :], ALU.add)

    def mla_in_dve(st, b, dve, ch):
        V = nc.vector
        for n, (k0, k1, g) in enumerate(((0, 3, col["q_norm"]), (3, 5, col["kv_norm"]))):
            if n:
                dve.wait_ge(sem["rope_in"], 48)
                dve.wait_ge(sem["pe_rot"], b["pe_rot"] + 1)
                ch.link(rope(dve, ch, keys[64:96, 0, C:T], low_pe[64:96, C:T], ps_s[64:96, :]))
                for h in range(1, PER):
                    ins = V.tensor_copy(keys[64:96, h, C:T], keys[64:96, 0, C:T])
                ins.then_inc(sem["pe_key"], 1)
            dve.wait_ge(sem["low_dev"], b["low_dev"] + n + 1)
            r = low_rstd[n][:, :]
            ch.link(V.reciprocal(r, r))
            for k in range(k0, k1):
                ch.link(V.tensor_tensor(low[:, k, :], low[:, k, :], r, ALU.mult))
                V.tensor_scalar(low[:, k, :], low[:, k, :], colv[:, g + k - k0:g + k - k0 + 1], None, ALU.mult).then_inc(sem["low_full"], 1)
    def share(dve, ch, s_, ready, o):
        dve.wait_ge(sem["s_exp"], ready)
        ch.link(nc.vector.reciprocal(s_(3), s_(2)))
        nc.vector.tensor_scalar(o, ident[:, :], s_(3), None, ALU.mult).then_inc(sem["s_shared"], 1)

    MLA_LINKS = 2 * PER + (PER - 1) + 2 * PER * 6

    def mla_dve(st, b, dve, ch, i):
        V = nc.vector
        base_of = lambda name, per: b[name] + i * per
        U = len(MLA_UNITS)
        dve.wait_ge(sem["head_out"], base_of("head_out", 4) + 1)
        V.tensor_copy(q_turn[0:NOPE, :, :], q_flat[0:NOPE, :, :])
        dve.wait_ge(sem["head_mm"], base_of("head_mm", 4) + 2)
        for h in range(PER):
            ins = rope(dve, ch, q_turn[64:96, h, :], q_flat[64:96, h, :], ps_all[64:96, h, :])
            if h < PER - 1:
                ch.link(ins)
            else:
                ins.then_inc(sem["q_rot"], 1)

        def most(n):
            h, ctx, q = MLA_UNITS[n]
            dve.wait_ge(sem["s_made"], base_of("s_made", U) + n + 1)
            pair = ps_all[:, 2 * (n % 2):2 * (n % 2) + 2, :].rearrange("p b n -> p (b n)")
            s_ = lambda t: stat[:, 4 * (n % 2) + t:4 * (n % 2) + t + 1]
            if n >= 2:
                dve.wait_ge(sem["s_shared"], base_of("s_shared", U) + n - 1)
            ch.link(V.tensor_reduce(s_(0), pair[:, C:C + (C if ctx else T)], AX_X, ALU.max))
            V.tensor_scalar(s_(1), s_(0), -(DQ ** -0.5), None, ALU.mult).then_inc(sem["s_max"], 1)

        def copy(n):
            h, ctx, q = MLA_UNITS[n]
            if ctx:
                return
            dve.wait_ge(sem["turned1"], base_of("turned1", 4 * PER) + MLA_LAT[n] + 1)
            if n >= 2:
                dve.wait_ge(sem["s_weighted"], base_of("s_weighted", U) + n - 1)
            V.tensor_copy(prob_t[:, n % 2, 3 * P:T], ps_all[:, 5, 0:3 * P]).then_inc(sem["copied1"], 1)

        most(0)
        for n in range(U):
            if n:
                copy(n - 1)
            share(dve, ch, lambda t: stat[:, 4 * (n % 2) + t:4 * (n % 2) + t + 1], base_of("s_exp", U) + n + 1, diag[:, n % 2, :])
            if n + 1 < U:
                most(n + 1)
        copy(U - 1)

    NA_LINKS = 2 * 16

    def na_dve(st, b, dve, ch, i):
        V = nc.vector
        base_of = lambda name, per: b[name] + i * per
        U = len(NA_UNITS)

        def most(n):
            h, j = NA_UNITS[n]
            dve.wait_ge(sem["s_made"], base_of("s_made", U) + n + 1)
            dve.wait_ge(sem["bias_made"], base_of("bias_made", U) + n + 1)
            s_ = lambda t: stat[:, 4 * (n % 4) + t:4 * (n % 4) + t + 1]
            band = ps_all[:, n % 4, C:2 * C].rearrange("p (r n) -> p r n", n=KC_)
            V.tensor_tensor(band, band, bias_m[:, j, :, :], ALU.add).then_inc(sem["s_biased"], 1)
            dve.wait_ge(sem["s_biased"], base_of("s_biased", U) + n + 1)
            ch.link(V.tensor_reduce(s_(0), ps_all[:, n % 4, :], AX_X, ALU.max))
            V.tensor_scalar(s_(1), s_(0), -(HD ** -0.5), None, ALU.mult).then_inc(sem["s_max"], 1)

        def copy(n):
            dve.wait_ge(sem["turned1"], base_of("turned1", U) + n + 1)
            if n >= 2:
                dve.wait_ge(sem["s_weighted"], base_of("s_weighted", U) + n - 1)
            V.tensor_copy(prob_nt[:, n % 2, C:2 * C], ps_all[:, 5, 0:C]).then_inc(sem["copied1"], 1)

        most(0)
        for n in range(U):
            if n:
                copy(n - 1)
            share(dve, ch, lambda t: stat[:, 4 * (n % 4) + t:4 * (n % 4) + t + 1], base_of("s_exp", U) + n + 1, diag_n[:, n % 2, :])
            if n + 1 < U:
                most(n + 1)
        copy(U - 1)

    @block.vector
    def _(dve):
        ch = Chain(dve, sem["dve_chain"])
        def gemv(g, slot=0, i=0, count=None, ahead=0):
            dve.wait_ge(sem[f"gemv_in{slot}"], count)
            if not (isinstance(i, int) and g + i - ahead <= 0):
                dve.wait_ge(sem["gemv_reduced"], g + i - ahead)
            two = g >= G_ADA
            seen = []
            total = 16 if two else 8
            place = ahead and slot
            for t in range(total):
                k = t // 2 if two else t
                cc = (KD * (1 + t % 2) if two else 0) + k
                s, o, w = c_col[:, cc:cc + 1], accs[place][:, t % 2, :], g_raw[:, slot, k, :]
                if t >= 2:
                    ch.wait(seen[t - 1] if two and t == total - 1 else seen[t - 2])
                    ins = nc.vector.scalar_tensor_tensor(o, w, s, o, ALU.mult, ALU.add)
                else:
                    ins = nc.vector.tensor_scalar(o, w, s, None, ALU.mult)
                if not (two and t == total - 1):
                    seen.append(ch.step(ins))
            if not two:
                ch.wait(seen[-1])
                ins = nc.vector.tensor_tensor(accs[place][:, 0, :], accs[place][:, 0, :], accs[place][:, 1, :], ALU.add)
            ins.then_inc(sem["gemv_done"], 1)

        n_gemv = [0, 0]
        for st in PLAN:
            b = st["base"]
            kind = st["kind"]
            if kind == "load":
                dve.wait_ge(sem["c_act"], 1)
                dve.wait_ge(sem["consts"], 5)
            elif kind == "prologue":
                for n, g in enumerate(st["gemvs"]):
                    n_gemv[n % 2] += 16
                    gemv(g, n % 2, 0, n_gemv[n % 2], ahead=1)
            elif kind == "mods":
                dve.wait_ge(sem["gemv_reduced"], st["need"])
                for lo, hi, bias in st["spans"]:
                    ch.link(nc.vector.tensor_tensor(modc[:, lo:hi], ps_mod[:, lo:hi], colv[:, col["b_mod"] + bias:col["b_mod"] + bias + hi - lo], ALU.add))
                for c0, g0 in st["plus"]:
                    v = modc[:, c0:c0 + KD]
                    if g0 is None:
                        ch.link(nc.vector.tensor_scalar(v, v, 1.0, None, ALU.add))
                    else:
                        ch.link(nc.vector.scalar_tensor_tensor(v, v, 1.0, colv[:, g0:g0 + KD], ALU.add, ALU.mult))
                for c0 in st["half"]:
                    v = modc[:, c0:c0 + KD]
                    ch.link(nc.vector.tensor_scalar(v, v, 0.5, None, ALU.mult))
            elif kind == "norm":
                buf, N = src(st)
                mode = st["mode"]
                cols_of = modc if mode in ("rms_h", "mod_h") else colv
                A = lambda k: cols_of[:, st["A"] + k:st["A"] + k + 1]
                B = lambda k: cols_of[:, st["B"] + k:st["B"] + k + 1]
                if mode == "ln_x":
                    dve.wait_ge(sem["mean_summed"], b["mean_summed"] + (0 if st["fused"] else 1))
                    for k in range(KD):
                        v = buf[:, k * N:(k + 1) * N]
                        nc.vector.tensor_tensor(v, v, ps_s[:, 0:N], ALU.subtract).then_inc(sem["centred"], 1)
                if mode != "mod_h":
                    dve.wait_ge(sem["deviation"], b["deviation"] + 1)
                    ch.link(nc.vector.reciprocal(rstd[:, 0:N], rstd[:, 0:N]))
                for k in range(KD):
                    v = buf[:, k * N:(k + 1) * N]
                    unit = v
                    if mode != "mod_h":
                        unit = unit_t[:, k % 2, 0:N]
                        ch.link(nc.vector.tensor_tensor(unit, v, rstd[:, 0:N], ALU.mult))
                    if mode in ("rms_x", "ln_x"):
                        ins = nc.vector.tensor_scalar(v, unit, A(k), None if mode == "rms_x" else B(k), ALU.mult, *(() if mode == "rms_x" else (ALU.add,)))
                        ins.then_inc(sem["x_new"], 1)
                    if "h_full" in st["totals"]:
                        if b["h_ready"] + k >= 2:
                            dve.wait_ge(sem["h_ready"], b["h_ready"] + k - 1)
                        scale, shift, given = A(k), None if st["B"] is None else B(k), unit
                        if st["then"]:
                            dve.wait_ge(sem["x_new"], b["x_new"] + k + 1)
                            scale, shift = (modc[:, c0 + k:c0 + k + 1] for c0 in st["then"])
                            given = v
                        nc.vector.tensor_scalar(full_t[:, k % 2, 0:N], given, scale, shift, ALU.mult, ALU.add).then_inc(sem["h_full"], 1)
                if "x_new" in st["totals"]:
                    dve.wait_ge(sem["x_new"], b["x_new"] + KD)
            elif kind == "gu":
                N, p0, hh = st["N"], st["p0"], b["hid_hi"]
                per_g = 0 if st["gemv"] is None else (15 if st["gemv"] >= G_ADA else 8)
                start0 = n_gemv[0]

                def one(i, last):
                    if per_g:
                        gemv(st["gemv"], 0, i, start0 + 16 + i * 16)
                    if st["conv"] is not None:
                        conv_taps(st, b, i, dve, ch)
                    dve.wait_ge(sem["g_read"], b["g_read"] + i + 1)
                    dve.wait_ge(sem["panel_used"], p0 + i * 2 + 2)
                    dve.wait_ge(sem["hid_hi"], hh + i)
                    other = ps_u[:, :, 0:N] if st["conv"] is None else prod_t[:, :, 0:N]
                    nc.vector.tensor_tensor(prod_t[:, :, 0:N], gate_t[:, :, 0:N], other, ALU.mult).then_inc(sem["product"], 1)
                    dve.wait_ge(sem["hid_hi"], hh + i + 1)
                    w = ds(i * (2 * N), 2 * N)
                    nc.vector.tensor_tensor(hid_lo[:, w].rearrange("p (c n) -> p c n", c=2), prod_t[:, :, 0:N],
                                            hid_hi[:, w].rearrange("p (c n) -> p c n", c=2).bitcast(F32), ALU.subtract).then_inc(sem["hid_lo"], 1)
                ch.loop(st["iters"], per_g + (7 if st["conv"] is not None else 0), one)
                if per_g:
                    n_gemv[0] += 16 * st["iters"]
            elif kind == "dn":
                N, p0 = st["N"], st["p0"]
                buf, _ = src(st)
                per_g = 0 if st["gemv"] is None else (15 if st["gemv"] >= G_ADA else 8)
                start0 = n_gemv[0]

                def one(i, last):
                    if per_g:
                        gemv(st["gemv"], 0, i, start0 + 16 + i * 16)
                    for j in range(2):
                        dve.wait_ge(sem["panel_used"], p0 + i * 2 + j + 1)
                        v = buf[:, ds(i * (2 * N) + j * N, N)]
                        nc.vector.scalar_tensor_tensor(v, ps_d[:, j, 0:N], modc[:, ds(st["gate"] + j + i * 2, 1)], v, ALU.mult, ALU.add).then_inc(sem[f"down{j}"], 1)
                ch.loop(st["iters"], per_g, one)
                if per_g:
                    n_gemv[0] += 16 * st["iters"]
                for j in range(2):
                    dve.wait_ge(sem[f"down{j}"], b[f"down{j}"] + st["iters"])
            elif kind == "proj":
                p0 = st["p0"]

                def one(i, last):
                    gemvs = half_of(st["gemvs"], i)
                    for j, bank in enumerate((ps_g, ps_u)):
                        for g in (gemvs[:2], gemvs[2:])[j]:
                            slot = (g - st["gemvs"][0] + 1) % 2
                            n_gemv[slot] += 16
                            gemv(g, slot, 0, n_gemv[slot])
                        dve.wait_ge(sem["panel_used"], p0 + i * 2 + j + 1)
                        for c in range(2):
                            v = x[:, ds(i * (4 * S) + (2 * j + c) * S, S)]
                            ins = nc.vector.scalar_tensor_tensor(v, bank[:, c, :], modc[:, ds(st["gate"] + 2 * j + c + i * 4, 1)], v, ALU.mult, ALU.add)
                        for c in range(2 if st["ctx_gate"] is not None else 0):
                            v = hc[:, ds(i * (4 * C) + (2 * j + c) * C, C)]
                            ins = nc.vector.scalar_tensor_tensor(v, ps_d[:, j, c * C:(c + 1) * C], modc[:, ds(st["ctx_gate"] + 2 * j + c + i * 4, 1)], v, ALU.mult, ALU.add)
                        ins.then_inc(sem[f"proj{j}"], 1)
                one(0, False)
                one(1, True)
                for j in range(2):
                    dve.wait_ge(sem[f"proj{j}"], b[f"proj{j}"] + st["iters"])
            elif kind == "alpha":
                dve.wait_ge(sem["h_full"], b["h_full"])
                v = hc if st["ctx"] else x
                n = KD * (C if st["ctx"] else S)
                ch.link(nc.vector.tensor_scalar(v[:, 0:n], v[:, 0:n], ALPHA, None, ALU.mult))
            elif kind == "mla_in":
                mla_in_dve(st, b, dve, ch)
            elif kind == "mla":
                ch.loop(st["iters"], MLA_LINKS, lambda i, last: mla_dve(st, b, dve, ch, i))
            elif kind == "na":
                ch.loop(st["iters"], NA_LINKS, lambda i, last: na_dve(st, b, dve, ch, i))
            elif kind == "mixer":
                def mix_gemv(n):
                    if n < len(st["gemvs"]):
                        n_gemv[0] += 16
                        gemv(st["gemvs"][n], 0, 0, n_gemv[0])
                mixer_dve(st, b, dve, ch, mix_gemv)

    block_cm.__exit__(None, None, None)


def constants():
    q, k = np.arange(P)[:, None], np.arange(2 * P)[None, :]
    dist = (q + P - k).astype(np.float32)
    slopes = (2.0 ** (-8.0 * np.arange(1, NQ + 1) / NQ)).astype(np.float32)
    valid = (dist >= 0) & (dist < P)
    alibi = np.where(valid[:, None, :], -slopes[None, :, None] * dist[:, None, :], np.float32(NEG)).astype(np.float32)
    t = np.arange(S)
    inv = (10000.0 ** (-np.arange(ROPE // 4, dtype=np.float32) / (ROPE // 4))).astype(np.float32)
    ang = np.concatenate([(t // GRID).astype(np.float32)[:, None] * inv, (t % GRID).astype(np.float32)[:, None] * inv], -1)
    rope = np.stack([np.cos(ang).T, np.sin(ang).T]).astype(np.float32)
    rope = np.ascontiguousarray(np.concatenate([rope, rope], 1))
    half = ROPE // 2
    turn = np.zeros((DQ, DQ), np.float32)
    for i in range(NOPE, NOPE + half):
        turn[i + half, i], turn[i, i + half] = -1.0, 1.0
    mask = np.zeros((P, 3, KC_), np.float32)
    for n, j in enumerate((0, 1, 3)):
        qc = j * QC + np.arange(QC)
        start = np.clip(qc - NA_COLS // 2, 0, GRID - NA_COLS)
        kc = BAND[j] + np.arange(KC_)
        ok = (kc[None, :] >= start[:, None]) & (kc[None, :] < start[:, None] + NA_COLS)
        mask[:, n, :] = np.tile(np.where(ok, 0.0, NEG), (ROWS, 1))
    return {"k_ident": np.eye(P, dtype=np.float32), "k_alibi": alibi, "k_rope": rope, "k_turn": turn, "k_na_mask": mask}


INS = ["x", "c", "w_mod", "b_mod", "g_norm", "w_ffn1_gu", "w_ffn1_down", "w_ffn2_gu", "w_ffn2_down", "w_in", "w_out",
       "attn_sinks", "lru_conv_w", "lru_conv_b", "lru_gate_a_w", "lru_gate_a_b", "lru_gate_x_w", "lru_gate_x_b",
       "lru_lambda", "sc_conv_w", "g_final", "c_2", "ctx_2", "c_ctx_2", "ada_w_2", "ada_b_2", "ln1_g_2", "ln1_b_2",
       "ln2_g_2", "ln2_b_2", "ffn_w_in_2", "ffn_conv_w_2", "ffn_conv_b_2", "ffn_w_out_2", "mla_w_in_2",
       "mla_q_norm_2", "mla_kv_norm_2", "mla_w_qb_2", "mla_w_kvb_2", "mla_w_o_2", "na_w_qkv_2", "na_rpb_2", "na_w_o_2"]


def kernel(**inputs):
    import numpy as _np
    import concourse.bacc as _bacc
    from concourse import mybir as _mybir
    from concourse.bass_utils import run_bass_kernel_spmd as _run

    nc = _bacc.Bacc("TRN2", target_bir_lowering=False, num_devices=1)
    arrays, aps = {}, {}
    given = {name: _np.ascontiguousarray(inputs[name]) for name in INS}
    for name, a in {**given, **constants()}.items():
        arrays[f"in_{name}_dram"] = a
        aps[name] = nc.dram_tensor(f"in_{name}_dram", a.shape, _mybir.dt.from_np(a.dtype), kind="ExternalInput").ap()
    out = nc.dram_tensor("out_0_dram", (1, S, D), _mybir.dt.float32, kind="ExternalOutput").ap()
    build(nc, aps, out)
    r = _run(nc, [arrays], core_ids=[0])
    return r.results[0]["out_0_dram"]
```
